# Optimizing a Trainium2 kernel written in Bass

```python
import math
import jax, jax.numpy as jnp
from jax import lax
import numpy as np

D_MODEL = 1024
BATCH = 1
SEQ = 1024
DEPTH = 1
DEC_BATCH = 1
DEC_SEQ = 4096
PAST_LEN = 128

GRID_W = 64
D_MIX = D_MODEL
NA_HEAD_DIM = 64
NA_HEADS = (D_MIX // 2) // NA_HEAD_DIM
NA_WIDTH = NA_HEADS * NA_HEAD_DIM
NA_WIN_H = 8
NA_WIN_W = 16
NA_QBLK = 16
NA_KBLK = 32
RET_HEAD_DIM = 128
RET_HEADS = (D_MIX // 2) // RET_HEAD_DIM
RET_WIDTH = RET_HEADS * RET_HEAD_DIM
RET_CHUNK = 128
ROPE_BASE = 10000.0
NORM_EPS = 1e-6
IN_WIDTH = 4 * NA_WIDTH + 4 * RET_WIDTH

kernel_name = 'hybrid_na_retention_encoder'

def rms_norm(x, gain):
    xf = x.astype(jnp.float32)
    y = xf * lax.rsqrt(jnp.mean(xf * xf, axis=-1, keepdims=True) + NORM_EPS)
    return (y * gain.astype(jnp.float32)).astype(x.dtype)

def rotary(x):
    T, d = x.shape[2], x.shape[3]
    half = d // 2
    inv = ROPE_BASE ** (-jnp.arange(half, dtype=jnp.float32) / half)
    ang = jnp.arange(T, dtype=jnp.float32)[:, None] * inv[None, :]
    cos, sin = jnp.cos(ang), jnp.sin(ang)
    x1 = x[..., :half].astype(jnp.float32)
    x2 = x[..., half:].astype(jnp.float32)
    return jnp.concatenate([x1 * cos - x2 * sin, x1 * sin + x2 * cos], axis=-1).astype(x.dtype)

def _na_column_blocks():
    q_col = np.arange(GRID_W)
    win_start = np.clip(q_col - NA_WIN_W // 2, 0, GRID_W - NA_WIN_W)
    n_blk = GRID_W // NA_QBLK
    blk = np.arange(n_blk)
    k_start = np.clip(blk * NA_QBLK - NA_WIN_W // 2, 0, GRID_W - NA_KBLK)
    k_idx = k_start[:, None] + np.arange(NA_KBLK)
    q_idx = blk[:, None] * NA_QBLK + np.arange(NA_QBLK)
    ws = win_start[q_idx][:, :, None]
    kk = k_idx[:, None, :]
    valid = (kk >= ws) & (kk < ws + NA_WIN_W)
    dc = np.clip(kk - q_idx[:, :, None] + NA_WIN_W - 1, 0, 2 * NA_WIN_W - 2)
    return k_idx, valid, dc

def neighborhood_attention(q, k, v, rpb):
    B, H, T, d = q.shape
    rows = T // GRID_W
    kh = min(NA_WIN_H, rows)
    k_idx, valid, dc = _na_column_blocks()
    n_blk = k_idx.shape[0]
    kg = k.reshape(B, H, rows, GRID_W, d)
    vg = v.reshape(B, H, rows, GRID_W, d)
    qg = jnp.moveaxis(q.reshape(B, H, rows, GRID_W, d), 2, 0)
    bias_c = rpb.astype(jnp.float32)[:, :, dc]
    bias_c = jnp.where(valid, bias_c, -jnp.inf)

    def row_step(args):
        r, q_r = args
        start = jnp.clip(r - kh // 2, 0, rows - kh)
        k_rows = lax.dynamic_slice_in_dim(kg, start, kh, axis=2)
        v_rows = lax.dynamic_slice_in_dim(vg, start, kh, axis=2)
        k_blk = k_rows[:, :, :, k_idx]
        v_blk = v_rows[:, :, :, k_idx]
        q_b = q_r.reshape(B, H, n_blk, NA_QBLK, d)
        s = jnp.einsum('bhnqd,bhrnkd->bhnqrk', q_b, k_blk).astype(jnp.float32)
        dr = start + jnp.arange(kh) - r + (NA_WIN_H - 1)
        bias = jnp.transpose(bias_c[:, dr], (0, 2, 3, 1, 4))
        s = s + bias[None]
        p = jax.nn.softmax(s.reshape(B, H, n_blk, NA_QBLK, kh * NA_KBLK), axis=-1).reshape(s.shape)
        o = jnp.einsum('bhnqrk,bhrnkd->bhnqd', p.astype(v.dtype), v_blk)
        return o.reshape(B, H, GRID_W, d)

    out = lax.map(row_step, (jnp.arange(rows), qg))
    return jnp.moveaxis(out, 0, 2).reshape(B, H, T, d)

def retention_chunkwise(q, k, v, log_gamma, strict):
    B, H, T, dk = q.shape
    dv = v.shape[-1]
    C = RET_CHUNK
    N = T // C
    q = q.reshape(B, H, N, C, dk)
    k = k.reshape(B, H, N, C, dk)
    v = v.reshape(B, H, N, C, dv)
    pos = jnp.arange(C, dtype=jnp.float32)
    diff = pos[:, None] - pos[None, :]
    lower = (diff > 0) if strict else (diff >= 0)
    dmat = jnp.where(lower, jnp.exp(log_gamma[:, None, None] * jnp.maximum(diff, 0.0)), 0.0)
    s = jnp.einsum('bhnid,bhnjd->bhnij', q, k) * dmat[None, :, None]
    o_intra = jnp.einsum('bhnij,bhnjd->bhnid', s, v)
    k_dec = k * jnp.exp(log_gamma[:, None] * (C - 1 - pos)[None, :])[None, :, None, :, None]
    kv = jnp.einsum('bhnjd,bhnje->nbhde', k_dec, v).astype(jnp.float32)
    chunk_decay = jnp.exp(log_gamma * C)[None, :, None, None]

    def step(S, kv_n):
        return chunk_decay * S + kv_n, S

    _, S_prev = lax.scan(step, jnp.zeros((B, H, dk, dv), jnp.float32), kv)
    q_dec = q * jnp.exp(log_gamma[:, None] * (pos + 1.0)[None, :])[None, :, None, :, None]
    o_cross = jnp.einsum('bhnid,nbhde->bhnie', q_dec, S_prev)
    return (o_intra + o_cross).reshape(B, H, T, dv)

def encoder_layer(x, c, norm_gain, w_ada, b_ada, w_in, na_q_gain, na_k_gain, na_rpb,
                  ret_decay_f, ret_decay_b, ret_out_gain, w_out):
    B, T, _ = x.shape
    mod = jax.nn.silu(c) @ w_ada + b_ada
    shift, scale, gate = jnp.split(mod, 3, axis=-1)
    h = rms_norm(x, norm_gain) * (1 + scale[:, None]) + shift[:, None]
    proj = h @ w_in
    sizes = [NA_WIDTH] * 4 + [RET_WIDTH] * 4
    qa, ka, va, ga, qr, kr, vr, gr = jnp.split(proj, list(np.cumsum(sizes)[:-1]), axis=-1)

    def to_heads(t, n):
        return t.reshape(B, T, n, -1).transpose(0, 2, 1, 3)

    qa = rms_norm(to_heads(qa, NA_HEADS), na_q_gain) * (NA_HEAD_DIM ** -0.5)
    ka = rms_norm(to_heads(ka, NA_HEADS), na_k_gain)
    na = neighborhood_attention(qa, ka, to_heads(va, NA_HEADS), na_rpb)
    na = na.transpose(0, 2, 1, 3).reshape(B, T, NA_WIDTH) * jax.nn.silu(ga)

    qr = rotary(to_heads(qr, RET_HEADS))
    kr = rotary(to_heads(kr, RET_HEADS)) * (RET_HEAD_DIM ** -0.5)
    vr = to_heads(vr, RET_HEADS)
    lg_f = -jnp.exp(ret_decay_f.astype(jnp.float32))
    lg_b = -jnp.exp(ret_decay_b.astype(jnp.float32))
    flip = lambda t: t[:, :, ::-1]
    fwd = retention_chunkwise(qr, kr, vr, lg_f, strict=False)
    bwd = flip(retention_chunkwise(flip(qr), flip(kr), flip(vr), lg_b, strict=True))
    ret = (fwd + bwd).transpose(0, 2, 1, 3)
    ret = rms_norm(ret, ret_out_gain).reshape(B, T, RET_WIDTH).astype(x.dtype) * jax.nn.silu(gr)

    mix = jnp.concatenate([na, ret], axis=-1) @ w_out
    return x + gate[:, None] * mix

def setup_inputs(seed: int = 0) -> dict:
    key = jax.random.key(seed)
    ks = jax.random.split(key, 16)
    f32 = jnp.float32
    base = jnp.log(-jnp.log1p(-(2.0 ** (-5.0 - jnp.arange(RET_HEADS, dtype=f32)))))
    return {
        'x_prompt': jax.random.normal(ks[0], (BATCH, SEQ, D_MODEL), f32),
        'x_sample': jax.random.normal(ks[1], (DEC_BATCH, DEC_SEQ, D_MODEL), f32),
        'c_prompt': jax.random.normal(ks[2], (BATCH, D_MODEL), f32),
        'c_sample': jax.random.normal(ks[3], (DEC_BATCH, D_MODEL), f32),
        'norm_gain': 1.0 + 0.02 * jax.random.normal(ks[4], (DEPTH, D_MODEL), f32),
        'w_ada': 0.5 * D_MODEL ** -0.5 * jax.random.normal(ks[5], (DEPTH, D_MODEL, 3 * D_MODEL), f32),
        'b_ada': 0.02 * jax.random.normal(ks[6], (DEPTH, 3 * D_MODEL), f32),
        'w_in': D_MODEL ** -0.5 * jax.random.normal(ks[7], (DEPTH, D_MODEL, IN_WIDTH), f32),
        'na_q_gain': 1.0 + 0.02 * jax.random.normal(ks[8], (DEPTH, NA_HEAD_DIM), f32),
        'na_k_gain': 1.0 + 0.02 * jax.random.normal(ks[9], (DEPTH, NA_HEAD_DIM), f32),
        'na_rpb': 0.02 * jax.random.normal(ks[10], (DEPTH, NA_HEADS, 2 * NA_WIN_H - 1, 2 * NA_WIN_W - 1), f32),
        'ret_decay_f': base[None] + 0.01 * jax.random.normal(ks[11], (DEPTH, RET_HEADS), f32),
        'ret_decay_b': base[None] + 0.01 * jax.random.normal(ks[12], (DEPTH, RET_HEADS), f32),
        'ret_out_gain': 1.0 + 0.02 * jax.random.normal(ks[13], (DEPTH, RET_HEADS, RET_HEAD_DIM), f32),
        'w_out': D_MIX ** -0.5 * jax.random.normal(ks[14], (DEPTH, D_MIX, D_MODEL), f32),
    }

def reference(x_prompt, x_sample, c_prompt, c_sample, norm_gain, w_ada, b_ada, w_in,
              na_q_gain, na_k_gain, na_rpb, ret_decay_f, ret_decay_b, ret_out_gain, w_out):
    y_prompt = x_prompt
    y_sample = x_sample
    for l in range(DEPTH):
        y_prompt = encoder_layer(y_prompt, c_prompt, norm_gain[l], w_ada[l], b_ada[l], w_in[l],
                                 na_q_gain[l], na_k_gain[l], na_rpb[l], ret_decay_f[l],
                                 ret_decay_b[l], ret_out_gain[l], w_out[l])
        y_sample = encoder_layer(y_sample, c_sample, norm_gain[l], w_ada[l], b_ada[l], w_in[l],
                                 na_q_gain[l], na_k_gain[l], na_rpb[l], ret_decay_f[l],
                                 ret_decay_b[l], ret_out_gain[l], w_out[l])
    return (y_prompt, y_sample)


_drawn_inputs = setup_inputs


def setup_inputs(seed=0):
    import zlib

    import numpy as np

    out = dict(_drawn_inputs(seed))
    spreads = {}
    factors = {'norm_gain': 8.0,
     'b_ada': 3.763,
     'na_q_gain': 8.0,
     'na_k_gain': 8.0,
     'na_rpb': 8.0,
     'ret_out_gain': 8.0}
    for name, (base, spread) in spreads.items():
        noise = np.random.default_rng([zlib.crc32(name.encode()), seed]).standard_normal(out[name].shape)
        drawn = base * np.exp(spread * noise) if base else spread * noise
        out[name] = __import__('jax').numpy.asarray(drawn.astype(out[name].dtype))
    for name, factor in factors.items():
        out[name] = (out[name] * factor).astype(out[name].dtype)
    return out
```

```python
from contextlib import ExitStack

import concourse.bass as bass
import numpy as np
from concourse import mybir

F32 = mybir.dt.float32
F32R = mybir.dt.float32r
BF16 = mybir.dt.bfloat16
ALU = mybir.AluOpType
ACT = mybir.ActivationFunctionType
AX = mybir.AxisListType

P = 128
D = 1024
KB = D // P
T_SAMPLE, T_PROMPT = 4096, 1024
T = T_SAMPLE + T_PROMPT
TILES = T // P
PAIRS = TILES // 2
HALF = D // 2
NH, NHD = 8, 64
RH, RHD = 4, 128
C = 128
EPS = 1e-6
W = 64
QR, QC = 8, 16
KR, KC = 15, 32
KEYS = KR * KC
WIN_H, WIN_W = 8, 16
NDR, NDC = 2 * WIN_H - 1, 2 * WIN_W - 1
MASKED = 1.0e30
COLS = W // QC
K0 = [0, 8, 24, 32]
KIND = [0, 1, 1, 2]
TABLE = 3 * NH * KEYS
S_ROWS, P_ROWS = T_SAMPLE // W, T_PROMPT // W
STRIPS = (
    [(0, 0), (S_ROWS, S_ROWS)]
    + [(QR * b, QR * b - 4) for b in range(1, S_ROWS // QR - 1)]
    + [(S_ROWS - QR, S_ROWS - KR), (S_ROWS + P_ROWS - QR, S_ROWS + P_ROWS - KR)]
)
BODIES = len(STRIPS) // 2


def at_least(eng, sem, count):
    if isinstance(count, int) and count <= 0:
        return
    eng.wait_ge(sem, count)


def apart(passed):

    def wait_apart(eng, sem, count):
        at_least(eng, sem, count)
        if not isinstance(count, int):
            eng.sem_inc(passed, 1)

    return wait_apart


def over_pairs(eng, body):
    body(0, False)
    with eng.Fori(1, PAIRS - 1) as i:
        body(i, False)
    body(PAIRS - 1, True)


def modulation_stage(nc, cT, w_ada, b_ada, norm_gain, rpb, ident, modx, exps, gate_rows,
                     bias_rows):
    with ExitStack() as ctx:
        sb = lambda n, s, d=F32: ctx.enter_context(nc.sbuf_tensor(n, s, d))
        sem = lambda n: ctx.enter_context(nc.semaphore(n))
        ada = sb("ada", [P, KB, 3 * D])
        cond = sb("cond", [P, KB, 2])
        silu_c = sb("silu_c", [P, KB, 2])
        b_rows = sb("b_rows", [2, 3 * D])
        mod = sb("mod", [2, 3 * D])
        gain = sb("gain", [P, KB])
        mod_cols = sb("mod_cols", [P, 16, 2])
        one_seq = sb("one_seq", [P, 2, 16])
        rpb_rows = sb("rpb_rows", [NH * NDR, NDC])
        spread = sb("spread", [NH * NDR, 3, QC, KC])
        banks = [ctx.enter_context(nc.psum_tensor(f"mod_bank{j}", [P, 512], F32)) for j in range(6)]
        cols_bank = ctx.enter_context(nc.psum_tensor("cols_bank", [P, 16, 2], F32))
        wait_apart = apart(sem("m_passed"))
        small_in, ada_in = sem("small_in"), [sem(f"ada_in{k}") for k in range(KB)]
        ident_made, silu_made, mod_summed = sem("ident_made"), sem("silu_made"), sem("mod_summed")
        mod_made, cols_turned, modx_made = sem("mod_made"), sem("cols_turned"), sem("modx_made")
        spread_made, mod_stored = sem("spread_made"), sem("mod_stored")
        block = ctx.enter_context(nc.Block())

        @block.sync
        def _(sp):
            sp.dma_start(cond[:], cT).then_inc(small_in, 16)
            sp.dma_start(b_rows[0:1, :], b_ada).then_inc(small_in, 16)
            sp.dma_start(b_rows[1:2, :], b_ada).then_inc(small_in, 16)
            sp.dma_start(gain[:], norm_gain).then_inc(small_in, 16)
            sp.dma_start(rpb_rows[:], rpb).then_inc(small_in, 16)
            for k in range(KB):
                sp.dma_start(ada[:, k, :], w_ada[k * P:(k + 1) * P, :]).then_inc(ada_in[k], 16)
            wait_apart(sp, spread_made, 6)
            for k in range(3):
                sp.dma_start(bias_rows[:, k].rearrange("c hd x -> hd c x"), spread[:, k]).then_inc(mod_stored, 16)
            wait_apart(sp, mod_made, 6)
            sp.dma_start(gate_rows, mod[:, 2 * D:3 * D]).then_inc(mod_stored, 16)
            wait_apart(sp, mod_stored, 64)

        @block.gpsimd
        def _(pool):
            nc.gpsimd.memset(ident[:], 0.0).then_inc(ident_made, 1)
            wait_apart(pool, ident_made, 1)
            nc.gpsimd.affine_select(out=ident[:], in_=ident[:], compare_op=ALU.not_equal, fill=1.0, base=0,
                                    pattern=[[-1, P]], channel_multiplier=1).then_inc(ident_made, 1)
            nc.gpsimd.memset(exps[:], -0.5).then_inc(ident_made, 1)

        @block.scalar
        def _(act):
            act.wait_ge(small_in, 80)
            nc.scalar.activation(silu_c[:], cond[:], ACT.Silu).then_inc(silu_made, 1)

        @block.vector
        def _(dve):
            nc.vector.memset(spread[:], MASKED).then_inc(spread_made, 1)
            dve.wait_ge(small_in, 80)
            dve.wait_ge(spread_made, 1)
            mid = NDC // 2

            def put(kind, c0, c1, key0, key_step, dc0, dc_step):
                flat = spread[:].rearrange("q k c x -> q (k c x)")
                src = rpb_rows[:]
                for c in range(c0, c1):
                    k_at = (kind * QC + c) * KC + key0 + key_step * (c - c0)
                    d_at = dc0 + dc_step * (c - c0)
                    last = nc.vector.tensor_scalar(flat[:, k_at:k_at + WIN_W], src[:, d_at:d_at + WIN_W], -1.0,
                                                   None, ALU.mult)
                last.then_inc(spread_made, 1)

            put(0, 0, 8, 0, 0, mid, -1)
            put(0, 8, QC, 0, 1, mid - 8, 0)
            put(1, 0, QC, 0, 1, mid - 8, 0)
            put(2, 0, 9, 8, 1, mid - 8, 0)
            put(2, 9, QC, 16, 0, mid - 9, -1)
            dve.wait_ge(mod_summed, 1)
            for n in range(6):
                nc.vector.tensor_tensor(mod[:, 512 * n:512 * (n + 1)], banks[n][0:2, :],
                                        b_rows[:, 512 * n:512 * (n + 1)], ALU.add).then_inc(mod_made, 1)
            dve.wait_ge(cols_turned, 1)
            nc.vector.tensor_copy(mod_cols[:], cols_bank[:]).then_inc(modx_made, 1)
            dve.wait_ge(modx_made, 1)
            for s in range(2):
                nc.vector.scalar_tensor_tensor(out=one_seq[:, s, 0:8], in0=mod_cols[:, 8:16, s], scalar=1.0,
                                               in1=gain[:], op0=ALU.add, op1=ALU.mult)
                nc.vector.tensor_copy(one_seq[:, s, 8:16], mod_cols[:, 0:8, s]).then_inc(modx_made, 1)
            dve.wait_ge(modx_made, 3)
            t_s = T_SAMPLE // P
            nc.vector.tensor_copy(modx[:, 0:t_s, :], one_seq[:, 0:1, :].to_broadcast([P, t_s, 16]))
            nc.vector.tensor_copy(modx[:, t_s:TILES, :],
                                  one_seq[:, 1:2, :].to_broadcast([P, TILES - t_s, 16])).then_inc(modx_made, 1)

        @block.tensor
        def _(pe):
            pe.wait_ge(silu_made, 1)
            for k in range(KB):
                pe.wait_ge(ada_in[k], 16)
                for n in range(6):
                    last = nc.tensor.matmul(banks[n][0:2, :], silu_c[:, k, :], ada[:, k, 512 * n:512 * (n + 1)],
                                            start=(k == 0), stop=(k == KB - 1))
            last.then_inc(mod_summed, 1)
            pe.wait_ge(ident_made, 2)
            pe.wait_ge(mod_made, 6)
            for j in range(16):
                last = nc.tensor.transpose(cols_bank[:, j, :], mod[:, j * P:(j + 1) * P], ident[0:2, 0:2])
            last.then_inc(cols_turned, 1)


class Front:

    def __init__(self, nc, ctx, tag, x_tiles, w, modx, ident, half_eps, reverse):
        sb = lambda n, s, d=F32: ctx.enter_context(nc.sbuf_tensor(f"{tag}_{n}", s, d))
        sem = lambda n: ctx.enter_context(nc.semaphore(f"{tag}_{n}"))
        self.nc, self.x_tiles, self.w, self.modx, self.ident = nc, x_tiles, w, modx, ident
        self.half, self.reverse = half_eps, reverse
        self.w_hi, self.w_lo = sb("w_hi", [P, KB, 4 * HALF], F32R), sb("w_lo", [P, KB, 4 * HALF], F32R)
        self.x = sb("x", [P, 2, D])
        self.h_full = sb("h_full", [P, D])
        self.h_hi, self.h_lo = sb("h_hi", [P, 2, KB, P], F32R), sb("h_lo", [P, 2, KB, P], F32R)
        self.junk = sb("junk", [P, D], BF16)
        self.work = sb("work", [P, 4096])
        self.x_stat = sb("x_stat", [P, 4])
        self.mod_now = sb("mod_now", [P, 2, 16])
        self.turn_banks = [ctx.enter_context(nc.psum_tensor(f"{tag}_turn{j}", [P, 4, P], F32)) for j in range(2)]
        self.wait_apart = apart(sem("passed"))
        self.x_in = [sem("x_in0"), sem("x_in1")]
        self.w_in = [sem("w_in0"), sem("w_in1")]
        self.w_hi_made, self.w_lo_made = sem("w_hi_made"), sem("w_lo_made")
        self.x_squared, self.x_mean, self.x_rstd = sem("x_squared"), sem("x_mean"), sem("x_rstd")
        self.x_normed, self.x_turned, self.mod_placed = sem("x_normed"), sem("x_turned"), sem("mod_placed")
        self.h_modulated, self.h_hi_made, self.h_split = sem("h_modulated"), sem("h_hi_made"), sem("h_split")
        self.projected = sem("projected")

    def tile(self, s):
        return TILES - 1 - s if self.reverse else s

    def load_x(self, sp, s, par):
        self.wait_apart(sp, self.x_normed, s - 1)
        sp.dma_start(self.x[:, par, :], self.x_tiles[self.tile(s)]).then_inc(self.x_in[par], 16)

    def load_w(self, sp):
        for k in range(KB):
            if k >= 2:
                self.wait_apart(sp, self.w_lo_made, k - 1)
            sp.dma_start(self.work[:, 2048 * (k % 2):2048 * (k % 2 + 1)],
                         self.w[k * P:(k + 1) * P, :]).then_inc(self.w_in[k % 2], 16)

    def split_w_hi(self, act, k):
        act.wait_ge(self.w_in[k % 2], 16 * (k // 2 + 1))
        self.nc.scalar.activation(self.w_hi[:, k, :], self.work[:, 2048 * (k % 2):2048 * (k % 2 + 1)],
                                  ACT.Copy).then_inc(self.w_hi_made, 1)

    def split_w_lo(self, dve, k):
        dve.wait_ge(self.w_hi_made, k + 1)
        self.nc.vector.tensor_tensor(self.w_lo[:, k, :], self.work[:, 2048 * (k % 2):2048 * (k % 2 + 1)],
                                     self.w_hi[:, k, :].bitcast(F32), ALU.subtract).then_inc(self.w_lo_made, 1)

    def square_x(self, act, s, par, i):
        act.wait_ge(self.x_in[par], 16 * (i + 1))
        at_least(act, self.x_mean, s)
        self.nc.scalar.activation(self.junk[:], self.x[:, par, :], ACT.Square,
                                  accum_out=self.x_stat[:, 0:1]).then_inc(self.x_squared, 1)

    def mean_x(self, dve, s):
        dve.wait_ge(self.x_squared, s + 1)
        self.nc.vector.tensor_scalar(self.x_stat[:, 1:2], self.x_stat[:, 0:1], 1.0 / D, EPS, ALU.mult,
                                     ALU.add).then_inc(self.x_mean, 1)

    def rstd_x(self, pool, s):
        self.wait_apart(pool, self.x_mean, s + 1)
        self.nc.gpsimd.tensor_tensor(self.x_stat[:, 2:3], self.x_stat[:, 1:2], self.half[:, 0:1],
                                     ALU.pow).then_inc(self.x_rstd, 1)

    def norm_x(self, dve, s, par):
        dve.wait_ge(self.x_rstd, s + 1)
        at_least(dve, self.x_turned, s)
        at_least(dve, self.h_split, s)
        self.nc.vector.tensor_scalar(self.h_full[:], self.x[:, par, :], self.x_stat[:, 2:3], None,
                                     ALU.mult).then_inc(self.x_normed, 1)

    def place_mod(self, pool, s, par):
        self.wait_apart(pool, self.h_modulated, s - 1)
        self.nc.gpsimd.tensor_copy(self.mod_now[:, par, :], self.modx[:, bass.ds(self.tile(s), 1), :]
                                   .rearrange("p a b -> p (a b)")).then_inc(self.mod_placed, 1)

    def turn_x(self, pe, s):
        pe.wait_ge(self.x_normed, s + 1)
        at_least(pe, self.h_modulated, s)
        for k in range(KB):
            last = self.nc.tensor.transpose(self.turn_banks[k // 4][:, k % 4, :],
                                            self.h_full[:, k * P:(k + 1) * P], self.ident[:])
        last.then_inc(self.x_turned, 1)

    def modulate(self, act, s, par):
        act.wait_ge(self.x_turned, s + 1)
        act.wait_ge(self.mod_placed, s + 1)
        for k in range(KB):
            last = self.nc.scalar.activation(self.h_full[:, k * P:(k + 1) * P], self.turn_banks[k // 4][:, k % 4, :],
                                             ACT.Identity, scale=self.mod_now[:, par, k:k + 1],
                                             bias=self.mod_now[:, par, KB + k:KB + k + 1])
        last.then_inc(self.h_modulated, 1)

    def split_h(self, dve, s, par):
        dve.wait_ge(self.h_modulated, s + 1)
        at_least(dve, self.projected, 4 * (s - 1))
        hi = self.h_hi[:, par].rearrange("p k t -> p (k t)")
        lo = self.h_lo[:, par].rearrange("p k t -> p (k t)")
        self.nc.vector.tensor_copy(hi, self.h_full[:]).then_inc(self.h_hi_made, 1)
        dve.wait_ge(self.h_hi_made, s + 1)
        self.nc.vector.tensor_tensor(lo, self.h_full[:], hi.bitcast(F32), ALU.subtract).then_inc(self.h_split, 1)

    def project(self, pe, s, par, n, bank):
        if n == 0:
            pe.wait_ge(self.h_split, s + 1)
        cols = slice(n * HALF, (n + 1) * HALF)
        for k in range(KB):
            if isinstance(s, int) and s == 0 and n == 0:
                pe.wait_ge(self.w_lo_made, k + 1)
            for j, (h, w) in enumerate([(self.h_hi, self.w_hi), (self.h_hi, self.w_lo), (self.h_lo, self.w_hi)]):
                last = self.nc.tensor.matmul(bank, h[:, par, k, :], w[:, k, cols], start=(k == 0 and j == 0),
                                             stop=(k == KB - 1 and j == 2))
        last.then_inc(self.projected, 1)


def attention_in_stage(nc, x_tiles, w, gains, modx, ident, exps, qT_d, kT_d, vg_d):
    with ExitStack() as ctx:
        f = Front(nc, ctx, "a", x_tiles, w, modx, ident, exps, False)
        sb = lambda n, s, d=F32: ctx.enter_context(nc.sbuf_tensor(n, s, d))
        sem = lambda n: ctx.enter_context(nc.semaphore(n))
        gain = sb("qk_gain", [P, 2])
        normed = f.work[:, 0:1024].rearrange("p (a n) -> p a n", a=2)
        squares = f.work[:, 1024:2048].rearrange("p (a n) -> p a n", a=2)
        vg = f.work[:, 2048:4096].rearrange("p (a n) -> p a n", a=2)
        turned = sb("qkT", [P, 2, 4, 2 * P])
        stat = sb("qk_stat", [P, 3, 2, NH])
        banks = [ctx.enter_context(nc.psum_tensor(f"a_proj{j}", [P, 512], F32)) for j in range(4)]
        qk_banks = [ctx.enter_context(nc.psum_tensor(f"a_qkT{j}", [P, 4, P], F32)) for j in range(2)]
        wait_apart = f.wait_apart
        gain_in, gain_made = sem("gain_in"), sem("gain_made")
        squared, summed, meaned, rstd_made = sem("qk_squared"), sem("qk_summed"), sem("qk_meaned"), sem("qk_rstd")
        qk_normed, qk_turned, qk_out = sem("qk_normed"), sem("qk_turned"), sem("qk_out")
        vg_made = sem("vg_made")
        vg_stored, qk_stored = [sem("vg_stored0"), sem("vg_stored1")], sem("qk_stored")
        block = ctx.enter_context(nc.Block())

        @block.sync
        def _(sp):
            for par in range(2):
                f.load_x(sp, par, par)
            sp.dma_start(gain[:], gains).then_inc(gain_in, 16)
            f.load_w(sp)

            def store_vg(t, par):
                wait_apart(sp, vg_made, 2 * t + 2)
                sp.dma_start(vg_d[t], vg[:, par, :]).then_inc(vg_stored[par], 16)

            def store_qk(i):
                wait_apart(sp, qk_out, 4 * i + 4)
                for a, dst in enumerate((qT_d, kT_d)):
                    sp.dma_start(dst[:, :, bass.ds(i * 2 * P, 2 * P)], turned[:, a]).then_inc(qk_stored, 16)

            def body(i, last):
                for par in range(2):
                    t = 2 * i + par
                    if not last:
                        f.load_x(sp, t + 2, par)
                    store_vg(t, par)
                store_qk(i)

            over_pairs(sp, body)
            wait_apart(sp, vg_stored[0], 16 * PAIRS)
            wait_apart(sp, vg_stored[1], 16 * PAIRS)
            wait_apart(sp, qk_stored, 32 * PAIRS)

        @block.gpsimd
        def _(pool):
            f.rstd_x(pool, 0)
            f.place_mod(pool, 0, 0)
            f.rstd_x(pool, 1)

            def body(i, last):
                for par in range(2):
                    t = 2 * i + par
                    for a in range(2):
                        wait_apart(pool, meaned, 2 * t + a + 1)
                        nc.gpsimd.tensor_tensor(stat[:, 2, a, :], stat[:, 1, a, :], exps[:, 0:NH],
                                                ALU.pow).then_inc(rstd_made, 1)
                    if not (last and par == 1):
                        f.place_mod(pool, t + 1, 1 - par)
                    if not last:
                        f.rstd_x(pool, t + 2)

            over_pairs(pool, body)

        @block.scalar
        def _(act):
            f.square_x(act, 0, 0, 0)
            f.modulate(act, 0, 0)
            f.square_x(act, 1, 1, 0)
            for k in range(KB):
                f.split_w_hi(act, k)

            def body(i, last):
                for par in range(2):
                    t = 2 * i + par
                    for a in range(2):
                        act.wait_ge(f.projected, 4 * t + a + 1)
                        at_least(act, summed, 2 * t + a - 1)
                        nc.scalar.activation(squares[:, a, :], banks[a][:], ACT.Square).then_inc(squared, 1)
                    if not (last and par == 1):
                        f.modulate(act, t + 1, 1 - par)
                    act.wait_ge(f.projected, 4 * t + 3)
                    at_least(act, vg_stored[par], 16 * i)
                    nc.scalar.activation(vg[:, par, 0:HALF], banks[2][:], ACT.Copy).then_inc(vg_made, 1)
                    if not last:
                        f.square_x(act, t + 2, par, i + 1)
                    act.wait_ge(f.projected, 4 * t + 4)
                    nc.scalar.activation(vg[:, par, HALF:D], banks[3][:], ACT.Silu).then_inc(vg_made, 1)

            over_pairs(act, body)

        @block.vector
        def _(dve):
            f.mean_x(dve, 0)
            f.norm_x(dve, 0, 0)
            f.split_h(dve, 0, 0)
            f.mean_x(dve, 1)
            f.norm_x(dve, 1, 1)
            for k in range(KB):
                f.split_w_lo(dve, k)
            dve.wait_ge(gain_in, 16)
            nc.vector.tensor_scalar(gain[:, 0:1], gain[:, 0:1], -(NHD ** -0.5), None, ALU.mult).then_inc(gain_made, 1)
            dve.wait_ge(gain_made, 1)

            def norm_heads(t, a):
                n = 2 * t + a
                dve.wait_ge(squared, n + 1)
                nc.vector.tensor_reduce(stat[:, 0, a, :], squares[:, a, :].rearrange("p (h d) -> p h d", h=NH),
                                        AX.X, ALU.add).then_inc(summed, 1)
                dve.wait_ge(summed, n + 1)
                nc.vector.tensor_scalar(stat[:, 1, a, :], stat[:, 0, a, :], 1.0 / NHD, EPS, ALU.mult,
                                        ALU.add).then_inc(meaned, 1)
                dve.wait_ge(rstd_made, n + 1)
                at_least(dve, qk_turned, n - 1)
                nc.vector.tensor_tensor(normed[:, a, :].rearrange("p (h d) -> p h d", h=NH),
                                        banks[a][:].rearrange("p (h d) -> p h d", h=NH),
                                        stat[:, 2, a, :].unsqueeze(2).to_broadcast([P, NH, NHD]),
                                        ALU.mult).then_inc(qk_normed, 1)

            def heads_out(i, t, par, a):
                dve.wait_ge(qk_turned, 2 * t + a + 1)
                if par == 0:
                    at_least(dve, qk_stored, 32 * i)
                nc.vector.tensor_scalar(turned[:, a, :, par * P:(par + 1) * P], qk_banks[a][:], gain[:, a:a + 1],
                                        None, ALU.mult).then_inc(qk_out, 1)

            def body(i, last):
                for par in range(2):
                    t = 2 * i + par
                    norm_heads(t, 0)
                    norm_heads(t, 1)
                    if not (last and par == 1):
                        f.split_h(dve, t + 1, 1 - par)
                    if not last:
                        f.mean_x(dve, t + 2)
                        f.norm_x(dve, t + 2, par)
                    heads_out(i, t, par, 0)
                    heads_out(i, t, par, 1)

            over_pairs(dve, body)

        @block.tensor
        def _(pe):
            f.turn_x(pe, 0)

            def turn_heads(t, a):
                pe.wait_ge(qk_normed, 2 * t + a + 1)
                at_least(pe, qk_out, 2 * t + a - 1)
                for j in range(4):
                    last = nc.tensor.transpose(qk_banks[a][:, j, :], normed[:, a, j * P:(j + 1) * P], ident[:])
                last.then_inc(qk_turned, 1)

            def body(i, last):
                for par in range(2):
                    t = 2 * i + par
                    for n in range(4):
                        if n < 2:
                            at_least(pe, qk_normed, 2 * t + n - 1)
                        else:
                            at_least(pe, vg_made, 2 * t + n - 3)
                        f.project(pe, t, par, n, banks[n][:])
                        if n == 1 and not (last and par == 1):
                            f.turn_x(pe, t + 1)
                        if n == 2:
                            turn_heads(t, 0)
                    turn_heads(t, 1)

            over_pairs(pe, body)


def retention_in_stage(nc, x_tiles, w, decays, rope, modx, ident, exps, part_d, qf_d, kv_d, gate_d):
    with ExitStack() as ctx:
        f = Front(nc, ctx, "r", x_tiles, w, modx, ident, exps, True)
        sb = lambda n, s, d=F32: ctx.enter_context(nc.sbuf_tensor(n, s, d))
        sem = lambda n: ctx.enter_context(nc.semaphore(n))
        raw = f.work[:, 0:1024].rearrange("p (a n) -> p a n", a=2)
        rot = f.work[:, 1024:2048].rearrange("p (a n) -> p a n", a=2)
        v = f.work[:, 2048:2560]
        gate = f.work[:, 2560:3072]
        turned = f.work[:, 3072:4096].rearrange("p (a n) -> p a n", a=2)
        cs = sb("cos_sin", [P, 2, 2, 64])
        product = sb("rot_product", [P, 2, 256])
        q_dec = sb("q_dec", [P, 2, HALF])
        k_dec = sb("k_dec", [P, 2, HALF])
        weighted = sb("weighted", [P, HALF])
        state = sb("state_b", [P, 2, HALF])
        kv_out = sb("kv_out", [P, HALF])
        part = sb("part", [P, HALF])
        within = sb("within", [P, RH, C])
        q_scale = sb("q_scale", [P, 2, RH, C])
        lg = sb("lg", [P, 2 * RH])
        k_scale = sb("k_scale", [P, 2 * RH])
        chunk_decay = sb("chunk_decay", [P, 2 * RH])
        pos = sb("pos", [P, 2])
        proj = [ctx.enter_context(nc.psum_tensor(f"r_proj{j}", [P, 512], F32)) for j in range(2)]
        qk_banks = [ctx.enter_context(nc.psum_tensor(f"r_qkT{j}", [P, 4, P], F32)) for j in range(2)]
        so_bank = ctx.enter_context(nc.psum_tensor("r_so", [P, 512], F32))
        kv_bank = ctx.enter_context(nc.psum_tensor("r_kv", [P, 512], F32))
        wait_apart = f.wait_apart
        decay_in, lg_made, pos_made = sem("decay_in"), sem("lg_made"), sem("pos_made")
        const_made, expo_made = sem("const_made"), sem("expo_made")
        cs_in = [sem("cs_in0"), sem("cs_in1")]
        raw_made, multiplied, rotated = sem("raw_made"), sem("multiplied"), sem("rotated")
        v_made, gate_made = sem("v_made"), sem("gate_made")
        qk_turned, turned_out, q_decayed, k_decayed = sem("rqk_turned"), sem("turned_out"), sem("q_decayed"), sem("k_decayed")
        scored, kv_b_done, kv_f_done, part_done = sem("scored"), sem("kv_b_done"), sem("kv_f_done"), sem("part_done")
        weighted_made, state_decayed, state_made = sem("weighted_made"), sem("state_decayed"), sem("state_made")
        kv_out_made, part_made = sem("kv_out_made"), sem("part_made")
        kv_stored, part_stored, qf_stored, gate_stored = sem("kv_stored"), sem("part_stored"), sem("qf_stored"), sem("gate_stored")
        block = ctx.enter_context(nc.Block())

        def heads(ap):
            return ap.rearrange("p (h n) -> p h n", h=RH)

        @block.sync
        def _(sp):
            sp.dma_start(lg[:], decays.partition_broadcast(P)).then_inc(decay_in, 16)

            def load_cs(s, par):
                wait_apart(sp, rotated, 4 * (s - 1))
                sp.dma_start(cs[:, par], rope[f.tile(s)]).then_inc(cs_in[par], 16)

            for par in range(2):
                f.load_x(sp, par, par)
                load_cs(par, par)
            f.load_w(sp)

            def store_late(s):
                wait_apart(sp, kv_out_made, s + 1)
                sp.dma_start(kv_d[f.tile(s)], kv_out[:]).then_inc(kv_stored, 16)
                wait_apart(sp, part_made, s + 1)
                sp.dma_start(part_d[f.tile(s)], part[:]).then_inc(part_stored, 16)

            def body(i, last):
                for par in range(2):
                    s = 2 * i + par
                    if not last:
                        f.load_x(sp, s + 2, par)
                    if not (isinstance(i, int) and s == 0):
                        store_late(s - 1)
                    wait_apart(sp, q_decayed, 2 * s + 1)
                    sp.dma_start(qf_d[f.tile(s)], q_dec[:, 0]).then_inc(qf_stored, 16)
                    wait_apart(sp, gate_made, s + 1)
                    sp.dma_start(gate_d[f.tile(s)], gate).then_inc(gate_stored, 16)
                    if not last:
                        load_cs(s + 2, par)

            over_pairs(sp, body)
            store_late(TILES - 1)
            for q in (kv_stored, part_stored, qf_stored, gate_stored):
                wait_apart(sp, q, 16 * TILES)

        @block.gpsimd
        def _(pool):
            nc.gpsimd.iota(within[:], pattern=[[0, RH], [1, C]], base=0, channel_multiplier=-1,
                           allow_small_or_imprecise_dtypes=True).then_inc(pos_made, 1)
            nc.gpsimd.iota(q_scale[:, 0], pattern=[[0, RH], [1, C]], base=1, channel_multiplier=0,
                           allow_small_or_imprecise_dtypes=True).then_inc(pos_made, 1)
            nc.gpsimd.iota(q_scale[:, 1], pattern=[[0, RH], [-1, C]], base=C, channel_multiplier=0,
                           allow_small_or_imprecise_dtypes=True).then_inc(pos_made, 1)
            nc.gpsimd.iota(pos[:, 0:1], pattern=[[0, 1]], base=C - 1, channel_multiplier=-1,
                           allow_small_or_imprecise_dtypes=True).then_inc(pos_made, 1)
            nc.gpsimd.iota(pos[:, 1:2], pattern=[[0, 1]], base=0, channel_multiplier=1,
                           allow_small_or_imprecise_dtypes=True).then_inc(pos_made, 1)
            f.rstd_x(pool, 0)
            f.place_mod(pool, 0, 0)
            f.rstd_x(pool, 1)

            def body(i, last):
                for par in range(2):
                    s = 2 * i + par
                    if not (last and par == 1):
                        f.place_mod(pool, s + 1, 1 - par)
                    if not last:
                        f.rstd_x(pool, s + 2)

            over_pairs(pool, body)

        @block.scalar
        def _(act):
            act.wait_ge(decay_in, 16)
            nc.scalar.activation(lg[:], lg[:], ACT.Exp).then_inc(lg_made, 1)
            act.wait_ge(expo_made, 12)
            nc.scalar.activation(within[:], within[:], ACT.Exp).then_inc(const_made, 1)
            nc.scalar.activation(q_scale[:], q_scale[:], ACT.Exp).then_inc(const_made, 1)
            nc.scalar.activation(k_scale[:], k_scale[:], ACT.Exp).then_inc(const_made, 1)
            nc.scalar.activation(chunk_decay[:], lg[:], ACT.Exp, scale=float(C)).then_inc(const_made, 1)
            f.square_x(act, 0, 0, 0)
            f.modulate(act, 0, 0)
            f.square_x(act, 1, 1, 0)
            for k in range(KB):
                f.split_w_hi(act, k)

            def late(s):
                act.wait_ge(kv_f_done, s + 1)
                at_least(act, kv_stored, 16 * s)
                nc.scalar.activation(kv_out[:], kv_bank[:], ACT.Copy).then_inc(kv_out_made, 1)
                act.wait_ge(part_done, s + 1)
                at_least(act, part_stored, 16 * s)
                nc.scalar.activation(part[:], so_bank[:], ACT.Copy).then_inc(part_made, 1)

            def body(i, last):
                for par in range(2):
                    s = 2 * i + par
                    for a in range(2):
                        act.wait_ge(f.projected, 4 * s + a + 1)
                        at_least(act, rotated, 4 * s + 2 * a - 2)
                        nc.scalar.activation(raw[:, a], proj[a][:], ACT.Copy,
                                             scale=(1.0 if a == 0 else RHD ** -0.5)).then_inc(raw_made, 1)
                    if not (last and par == 1):
                        f.modulate(act, s + 1, 1 - par)
                    if not (isinstance(i, int) and s == 0):
                        late(s - 1)
                    act.wait_ge(f.projected, 4 * s + 3)
                    nc.scalar.activation(v, proj[0][:], ACT.Copy).then_inc(v_made, 1)
                    act.wait_ge(qk_turned, 2 * s + 1)
                    at_least(act, q_decayed, 2 * s)
                    nc.scalar.activation(turned[:, 0], qk_banks[0][:].rearrange("p h n -> p (h n)"),
                                         ACT.Copy).then_inc(turned_out, 1)
                    if not last:
                        f.square_x(act, s + 2, par, i + 1)
                    act.wait_ge(f.projected, 4 * s + 4)
                    at_least(act, gate_stored, 16 * s)
                    nc.scalar.activation(gate, proj[1][:], ACT.Silu).then_inc(gate_made, 1)
                    act.wait_ge(qk_turned, 2 * s + 2)
                    nc.scalar.activation(turned[:, 1], qk_banks[1][:].rearrange("p h n -> p (h n)"),
                                         ACT.Copy).then_inc(turned_out, 1)

            over_pairs(act, body)
            late(TILES - 1)

        @block.vector
        def _(dve):
            dve.wait_ge(lg_made, 1)
            nc.vector.tensor_scalar(lg[:], lg[:], -1.0, None, ALU.mult).then_inc(expo_made, 1)
            dve.wait_ge(pos_made, 5)
            dve.wait_ge(expo_made, 1)
            for h in range(RH):
                nc.vector.tensor_scalar(weighted[:, h * C:(h + 1) * C], within[:, h, :], 0.0, lg[:, h:h + 1],
                                        ALU.max, ALU.mult)
                last = nc.vector.tensor_scalar(part[:, h * C:(h + 1) * C], within[:, h, :], 0.0,
                                               lg[:, RH + h:RH + h + 1], ALU.min, ALU.mult)
            last.then_inc(expo_made, 1)
            dve.wait_ge(expo_made, 2)
            nc.vector.tensor_tensor(within[:].rearrange("p h n -> p (h n)"), weighted[:], part[:],
                                    ALU.subtract).then_inc(expo_made, 1)
            for a in range(2):
                for h in range(RH):
                    nc.vector.tensor_scalar(q_scale[:, a, h, :], q_scale[:, a, h, :], lg[:, a * RH + h:a * RH + h + 1],
                                            None, ALU.mult).then_inc(expo_made, 1)
                last = nc.vector.tensor_scalar(k_scale[:, a * RH:(a + 1) * RH], lg[:, a * RH:(a + 1) * RH],
                                               pos[:, a:a + 1], None, ALU.mult)
            last.then_inc(expo_made, 1)
            nc.vector.memset(state[:, 1], 0.0).then_inc(state_made, 1)

            f.mean_x(dve, 0)
            f.norm_x(dve, 0, 0)
            f.split_h(dve, 0, 0)
            f.mean_x(dve, 1)
            f.norm_x(dve, 1, 1)
            for k in range(KB):
                f.split_w_lo(dve, k)
            dve.wait_ge(const_made, 4)

            def late(s, par):
                dve.wait_ge(scored, s + 1)
                at_least(dve, part_done, s)
                nc.vector.tensor_tensor(weighted[:], so_bank[:], within[:].rearrange("p h n -> p (h n)"),
                                        ALU.mult).then_inc(weighted_made, 1)
                dve.wait_ge(state_made, s + 1)
                at_least(dve, part_done, s)
                if isinstance(s, int) and s == T_PROMPT // P - 1:
                    nc.vector.memset(state[:, par, 0:HALF // 2], 0.0).then_inc(state_decayed, 1)
                    dve.wait_ge(state_decayed, s + 1)
                    dve.wait_ge(kv_b_done, s + 1)
                    nc.vector.memset(state[:, par, HALF // 2:], 0.0).then_inc(state_made, 1)
                    return
                for h in range(RH):
                    last = nc.vector.tensor_scalar(state[:, par, h * RHD:(h + 1) * RHD],
                                                   state[:, 1 - par, h * RHD:(h + 1) * RHD],
                                                   chunk_decay[:, RH + h:RH + h + 1], None, ALU.mult)
                last.then_inc(state_decayed, 1)
                dve.wait_ge(state_decayed, s + 1)
                dve.wait_ge(kv_b_done, s + 1)
                nc.vector.tensor_tensor(state[:, par], state[:, par], kv_bank[:], ALU.add).then_inc(state_made, 1)

            def rotate(s, par, a, i):
                n = 2 * s + a
                dve.wait_ge(raw_made, n + 1)
                dve.wait_ge(cs_in[par], 16 * (i + 1))
                at_least(dve, qk_turned, n - 1)
                src = raw[:, a].rearrange("p (h x n) -> p x h n", h=RH, x=2)
                dst = rot[:, a].rearrange("p (h x n) -> p x h n", h=RH, x=2)
                prod = [product[:, j].rearrange("p (h n) -> p h n", h=RH) for j in range(2)]
                trig = [cs[:, par, j:j + 1, :].to_broadcast([P, RH, 64]) for j in range(2)]
                for x, (first, second, op) in enumerate([(0, 1, ALU.subtract), (1, 0, ALU.add)]):
                    at_least(dve, rotated, 2 * n + x)
                    nc.vector.tensor_tensor(prod[0], src[:, 0], trig[first], ALU.mult)
                    nc.vector.tensor_tensor(prod[1], src[:, 1], trig[second], ALU.mult).then_inc(multiplied, 1)
                    dve.wait_ge(multiplied, 2 * n + x + 1)
                    nc.vector.tensor_tensor(dst[:, x], prod[0], prod[1], op).then_inc(rotated, 1)

            def body(i, last):
                for par in range(2):
                    s = 2 * i + par
                    if not (isinstance(i, int) and s == 0):
                        late(s - 1, 1 - par)
                    rotate(s, par, 0, i)
                    rotate(s, par, 1, i)
                    if not (last and par == 1):
                        f.split_h(dve, s + 1, 1 - par)
                    dve.wait_ge(rotated, 4 * s + 4)
                    for a, done in enumerate((kv_f_done, kv_b_done)):
                        at_least(dve, done, s)
                        k = nc.vector.tensor_tensor(heads(k_dec[:, a]), heads(rot[:, 1]),
                                                    k_scale[:, a * RH:(a + 1) * RH].unsqueeze(2)
                                                    .to_broadcast([P, RH, RHD]), ALU.mult)
                    k.then_inc(k_decayed, 1)
                    if not last:
                        f.mean_x(dve, s + 2)
                        f.norm_x(dve, s + 2, par)
                    dve.wait_ge(turned_out, 2 * s + 1)
                    at_least(dve, qf_stored, 16 * s)
                    at_least(dve, part_done, s)
                    for a in range(2):
                        nc.vector.tensor_tensor(q_dec[:, a], turned[:, 0], q_scale[:, a].rearrange("p h n -> p (h n)"),
                                                ALU.mult).then_inc(q_decayed, 1)

            seam = T_PROMPT // P
            body(0, False)
            with dve.Fori(1, seam // 2) as i:
                body(i, False)
            body(seam // 2, False)
            with dve.Fori(seam // 2 + 1, PAIRS - 1) as i:
                body(i, False)
            body(PAIRS - 1, True)
            late(TILES - 1, 1)

        @block.tensor
        def _(pe):
            f.turn_x(pe, 0)
            pe.wait_ge(const_made, 4)

            def turn_heads(s, a):
                pe.wait_ge(rotated, 4 * s + 2 * a + 2)
                at_least(pe, turned_out, 2 * s + a - 1)
                for h in range(RH):
                    last = nc.tensor.transpose(qk_banks[a][:, h, :], rot[:, a, h * RHD:(h + 1) * RHD], ident[:])
                last.then_inc(qk_turned, 1)

            def scores(s):
                pe.wait_ge(turned_out, 2 * s + 2)
                at_least(pe, part_made, s)
                for h in range(RH):
                    cols = slice(h * C, (h + 1) * C)
                    last = nc.tensor.matmul(so_bank[:, cols], turned[:, 1, cols], turned[:, 0, cols],
                                            start=True, stop=True)
                last.then_inc(scored, 1)

            def key_values(s, a, done):
                pe.wait_ge(k_decayed, s + 1)
                if a == 1:
                    pe.wait_ge(v_made, s + 1)
                    at_least(pe, kv_out_made, s)
                else:
                    pe.wait_ge(state_made, s + 2)
                for h in range(RH):
                    cols = slice(h * RHD, (h + 1) * RHD)
                    last = nc.tensor.matmul(kv_bank[:, cols], k_dec[:, a, cols], v[:, cols], start=True, stop=True)
                last.then_inc(done, 1)

            def outputs(s, par):
                pe.wait_ge(weighted_made, s + 1)
                pe.wait_ge(q_decayed, 2 * s + 2)
                pe.wait_ge(state_made, s + 1)
                for h in range(RH):
                    cols = slice(h * C, (h + 1) * C)
                    nc.tensor.matmul(so_bank[:, cols], weighted[:, cols], v[:, cols], start=True, stop=False)
                    last = nc.tensor.matmul(so_bank[:, cols], q_dec[:, 1, cols], state[:, 1 - par, cols],
                                            start=False, stop=True)
                last.then_inc(part_done, 1)

            def body(i, last):
                for par in range(2):
                    s = 2 * i + par
                    late = not (isinstance(i, int) and s == 0)
                    at_least(pe, v_made, s)
                    f.project(pe, s, par, 0, proj[0][:])
                    if late:
                        scores(s - 1)
                        key_values(s - 1, 1, kv_b_done)
                    at_least(pe, gate_made, s)
                    f.project(pe, s, par, 1, proj[1][:])
                    if not (last and par == 1):
                        f.turn_x(pe, s + 1)
                    if late:
                        key_values(s - 1, 0, kv_f_done)
                        outputs(s - 1, 1 - par)
                    pe.wait_ge(raw_made, 2 * s + 1)
                    f.project(pe, s, par, 2, proj[0][:])
                    turn_heads(s, 0)
                    pe.wait_ge(raw_made, 2 * s + 2)
                    f.project(pe, s, par, 3, proj[1][:])
                    turn_heads(s, 1)

            over_pairs(pe, body)
            s = TILES - 1
            scores(s)
            key_values(s, 1, kv_b_done)
            key_values(s, 0, kv_f_done)
            outputs(s, 1)


def attention_stage(nc, qT_d, kT_d, vg_d, bias_rows, ident, na_d):
    with ExitStack() as ctx:
        sb = lambda n, s, d=F32: ctx.enter_context(nc.sbuf_tensor(n, s, d))
        sem = lambda n: ctx.enter_context(nc.semaphore(n))
        tables = sb("bias_tables", [P, 2, 3, NH, KEYS])
        k_strip = sb("k_strip", [P, 2, 4, KR * W])
        q_strip = sb("q_strip", [P, 2, 4, QR * W])
        q_block = sb("q_block", [P, 2, NH, P])
        v_block = sb("v_block", [P, 2, 4, HALF])
        gate = sb("na_gate", [P, 2, HALF])
        out = sb("na_out", [P, 2, HALF])
        biased = sb("biased", [P, 4, KEYS])
        probs = sb("probs", [P, 4, 512])
        probs_T = sb("probs_T", [P, 2, 4, P])
        neg_max = sb("neg_max", [P, 4])
        masked = sb("masked", [P, KEYS])
        sums = sb("sums", [P, 2, NH])
        inverse = sb("inverse", [P, 2, NH])
        s_banks = [ctx.enter_context(nc.psum_tensor(f"s_bank{j}", [P, 512], F32)) for j in range(4)]
        t_banks = [ctx.enter_context(nc.psum_tensor(f"t_bank{j}", [P, 4, P], F32)) for j in range(2)]
        o_banks = [ctx.enter_context(nc.psum_tensor(f"o_bank{j}", [P, 512], F32)) for j in range(2)]
        wait_apart = apart(sem("n_passed"))
        cleared, cleared_tables, masked_placed = sem("cleared"), sem("cleared_tables"), sem("masked_placed")
        tables_in = [sem(f"{edge}_table_in") for edge in ("top", "inner", "bottom")]
        strip_in = [sem("strip_in0"), sem("strip_in1")]
        v_in, gate_in = [sem("v_in0"), sem("v_in1")], [sem("gate_in0"), sem("gate_in1")]
        q_placed, scored, biased_made, exped = sem("q_placed"), sem("na_scored"), sem("biased_made"), sem("exped")
        probs_turned, turned_act, turned_dve = sem("probs_turned"), sem("turned_act"), sem("turned_dve")
        valued, inverted, scaled, gated = sem("valued"), sem("inverted"), sem("scaled"), sem("gated")
        out_stored = [sem("out_stored0"), sem("out_stored1")]
        block = ctx.enter_context(nc.Block())

        UNITS = 2 * COLS
        STEPS = UNITS * NH
        LAST = BODIES * UNITS - 1

        def load_tables(eng, slot, edge, landed):
            for r in range(QR):
                if edge == "top":
                    key0, dr0 = max(r - 4, 0), max(r - 4, 0) - r + WIN_H - 1
                elif edge == "inner":
                    key0, dr0 = r, 3
                else:
                    key0, dr0 = min(r - 4, 0) + KR - QR, min(r - 4, 0) - r + WIN_H - 1
                rows = bias_rows.rearrange("c k (h r) x -> c (k h) (r x)", h=NH)
                eng.dma_start(tables[r * QC:(r + 1) * QC, slot, :, :, key0 * KC:(key0 + WIN_H) * KC]
                             .rearrange("p k h n -> p (k h) n"),
                             rows[:, :, dr0 * KC:(dr0 + WIN_H) * KC]).then_inc(landed, 16)

        def bodies(eng, body):
            body(0, 0, False)
            with eng.Fori(1, BODIES - 1) as b:
                body(b, 1, False)
            body(BODIES - 1, 0, True)

        @block.sync
        def _(sp):
            def rows_of(b, half):
                if isinstance(b, int) and b in (0, BODIES - 1):
                    return STRIPS[2 * b + half]
                q0, k0 = STRIPS[2]
                return q0 + QR * (2 * b + half - 2), k0 + QR * (2 * b + half - 2)

            def load_strip(b, half):
                q0, k0 = rows_of(b, half)
                wait_apart(sp, scored, STEPS * b + 32 * (half - 1))
                sp.dma_start(k_strip[:, half], kT_d[:, :, bass.ds(k0 * W, KR * W)]).then_inc(strip_in[half], 16)
                sp.dma_start(q_strip[:, half], qT_d[:, :, bass.ds(q0 * W, QR * W)]).then_inc(strip_in[half], 16)

            def load_unit(b, u):
                q0, k0 = rows_of(b, u // COLS)
                n = u % COLS
                wait_apart(sp, valued, STEPS * b + NH * (u - 1))
                for r in range(KR):
                    sp.dma_start(v_block[r % 4 * KC:(r % 4 + 1) * KC, u % 2, r // 4, :],
                                 vg_rows[k0 + r, K0[n]:K0[n] + KC, 0:HALF]).then_inc(v_in[u % 2], 16)
                wait_apart(sp, gated, UNITS * b + u - 1)
                for r in range(QR):
                    sp.dma_start(gate[r * QC:(r + 1) * QC, u % 2, :],
                                 vg_rows[q0 + r, QC * n:QC * (n + 1), HALF:D]).then_inc(gate_in[u % 2], 16)

            def store_unit(b, u):
                q0, _ = rows_of(b, u // COLS)
                n = u % COLS
                wait_apart(sp, gated, UNITS * b + u + 1)
                for r in range(QR):
                    sp.dma_start(na_rows[q0 + r, QC * n:QC * (n + 1), :],
                                 out[r * QC:(r + 1) * QC, u % 2, :]).then_inc(out_stored[u % 2], 16)

            vg_rows = vg_d.rearrange("t (r w) n -> (t r) w n", w=W)
            na_rows = na_d.rearrange("t (r w) n -> (t r) w n", w=W)
            load_strip(0, 0)
            wait_apart(sp, cleared_tables, 2)
            load_tables(sp, 0, "top", tables_in[0])
            load_unit(0, 0)
            load_unit(0, 1)

            def body(b, kind, last):
                for u in range(UNITS):
                    if u == 0:
                        load_strip(b, 1)
                    if u == COLS and not last:
                        load_strip(b + 1, 0)
                    if u > 0:
                        store_unit(b, u - 1)
                    if 0 < u < UNITS - 1:
                        load_unit(b, u + 1)
                    if isinstance(b, int) and b == 0 and u == 1:
                        load_tables(sp, 1, "inner", tables_in[1])
                if not last:
                    load_unit(b + 1, 0)
                store_unit(b, UNITS - 1)
                if not last:
                    load_unit(b + 1, 1)

            body(0, 0, False)
            with sp.Fori(1, BODIES - 2) as b:
                body(b, 1, False)
            body(BODIES - 2, 1, False)
            body(BODIES - 1, 0, True)
            for par in range(2):
                wait_apart(sp, out_stored[par], 16 * QR * (LAST + 1) // 2)

        @block.gpsimd
        def _(pool):
            nc.gpsimd.memset(q_block[:], 0.0).then_inc(cleared, 1)
            nc.gpsimd.memset(probs[:, :, KEYS:], 0.0).then_inc(cleared, 1)
            pool.wait_ge(cleared, 2)
            nc.gpsimd.memset(v_block[96:P, :, 3, :], 0.0).then_inc(cleared, 1)
            pool.wait_ge(cleared, 3)
            nc.gpsimd.memset(masked[:], MASKED).then_inc(cleared, 1)

            def place_q(b, u):
                if u % COLS == 0:
                    wait_apart(pool, strip_in[u // COLS], 32 * (b + 1))
                wait_apart(pool, scored, STEPS * b + NH * (u - 1))
                for half in range(2):
                    rows = slice(half * NHD, (half + 1) * NHD)
                    dst = q_block[rows, u % 2].rearrange("p (j x) (r w) -> p x j r w", x=2, r=QR)[:, half]
                    src = q_strip[rows, u // COLS].rearrange("p j (r w) -> p j r w", r=QR)
                    c0 = QC * (u % COLS)
                    nc.gpsimd.tensor_copy(dst, src[:, :, :, c0:c0 + QC]).then_inc(q_placed, 1)
                    wait_apart(pool, q_placed, 2 * (UNITS * b + u) + half + 1)

            def gate_unit(b, u):
                wait_apart(pool, scaled, UNITS * b + u + 1)
                wait_apart(pool, gate_in[u % 2], 16 * QR * (UNITS // 2 * b + u // 2 + 1))
                nc.gpsimd.tensor_tensor(out[:, u % 2], out[:, u % 2], gate[:, u % 2], ALU.mult).then_inc(gated, 1)

            def body(b, kind, last):
                for u in range(UNITS):
                    if u < UNITS - 1:
                        place_q(b, u + 1)
                    elif not last:
                        place_q(b + 1, 0)
                    if u > 0:
                        gate_unit(b, u - 1)
                    elif not (isinstance(b, int) and b == 0):
                        gate_unit(b - 1, UNITS - 1)

            wait_apart(pool, cleared, 4)
            place_q(0, 0)
            body(0, 0, False)
            wait_apart(pool, biased_made, STEPS)
            pool.dma_start(tables[:, 0].rearrange("p k h n -> p (k h) n"),
                           masked[:].unsqueeze(1).to_broadcast([P, 3 * NH, KEYS])).then_inc(masked_placed, 16)
            with pool.Fori(1, BODIES - 2) as b:
                body(b, 1, False)
            wait_apart(pool, masked_placed, 16)
            load_tables(pool, 0, "bottom", tables_in[2])
            body(BODIES - 2, 1, False)
            body(BODIES - 1, 0, True)
            gate_unit(BODIES - 1, UNITS - 1)

        @block.scalar
        def _(act):
            def exponentiate(b, j):
                act.wait_ge(biased_made, STEPS * b + j + 1)
                at_least(act, probs_turned, STEPS * b + j - 3)
                if j % NH == 0:
                    at_least(act, inverted, UNITS * b + j // NH - 1)
                nc.scalar.activation(probs[:, j % 4, 0:KEYS], biased[:, j % 4, :], ACT.Exp, scale=-1.0,
                                     bias=neg_max[:, j % 4:j % 4 + 1],
                                     accum_out=sums[:, j // NH % 2, j % NH:j % NH + 1]).then_inc(exped, 1)

            def take_out(b, j):
                act.wait_ge(probs_turned, STEPS * b + j + 1)
                at_least(act, valued, STEPS * b + j - 1)
                nc.scalar.activation(probs_T[:, 0].rearrange("p c q -> p (c q)"),
                                     t_banks[0][:].rearrange("p c q -> p (c q)"), ACT.Copy).then_inc(turned_act, 1)

            exponentiate(0, 0)
            exponentiate(0, 1)
            take_out(0, 0)

            def body(b, kind, last):
                for k in range(STEPS):
                    if k + 2 < STEPS:
                        exponentiate(b, k + 2)
                    elif not last:
                        exponentiate(b + 1, k + 2 - STEPS)
                    if (k + 1) % 2 == 0:
                        if k + 1 < STEPS:
                            take_out(b, k + 1)
                        elif not last:
                            take_out(b + 1, 0)

            bodies(act, body)

        @block.vector
        def _(dve):
            def clear(slot):
                nc.vector.memset(tables[:, slot], MASKED).then_inc(cleared_tables, 1)

            def add_bias(b, kind, j):
                u, h = j // NH, j % NH
                at_least(dve, exped, STEPS * b + j - 3)
                wait_apart(dve, scored, STEPS * b + j + 1)
                nc.vector.tensor_tensor_reduce(out=biased[:, j % 4, :], in0=s_banks[j % 4][:, 0:KEYS],
                                               in1=tables[:, kind, KIND[u % COLS], h, :], scale=1.0,
                                               scalar=3.0e38, op0=ALU.add, op1=ALU.min,
                                               accum_out=neg_max[:, j % 4:j % 4 + 1]).then_inc(biased_made, 1)

            def take_out(b, j):
                dve.wait_ge(probs_turned, STEPS * b + j + 1)
                at_least(dve, valued, STEPS * b + j - 1)
                nc.vector.tensor_copy(probs_T[:, 1], t_banks[1][:]).then_inc(turned_dve, 1)

            def scale_unit(b, u):
                n = UNITS * b + u + 1
                dve.wait_ge(valued, NH * n)
                nc.vector.reciprocal(inverse[:, u % 2, :], sums[:, u % 2, :]).then_inc(inverted, 1)
                dve.wait_ge(inverted, n)
                at_least(dve, out_stored[u % 2], 16 * QR * (UNITS // 2 * b + u // 2))
                nc.vector.tensor_tensor(out[:, u % 2].rearrange("p (h d) -> p h d", h=NH),
                                        o_banks[u % 2][:].rearrange("p (h d) -> p h d", h=NH),
                                        inverse[:, u % 2, :].unsqueeze(2).to_broadcast([P, NH, NHD]),
                                        ALU.mult).then_inc(scaled, 1)

            def body(b, kind, last):
                for k in range(STEPS):
                    if k + 3 < STEPS:
                        add_bias(b, kind, k + 3)
                    elif not last:
                        next_kind = kind if not isinstance(b, int) else [1, 1, 1, 0][b]
                        if isinstance(b, int) and b in (0, BODIES - 2):
                            dve.wait_ge(tables_in[1 if b == 0 else 2], 16 * QR)
                        add_bias(b + 1, next_kind, k + 3 - STEPS)
                    if k % NH == 2:
                        if k > NH:
                            scale_unit(b, k // NH - 1)
                        elif not (isinstance(b, int) and b == 0):
                            scale_unit(b - 1, UNITS - 1)
                    if (k + 1) % 2 == 1 and k + 1 < STEPS:
                        take_out(b, k + 1)

            clear(0)
            clear(1)
            dve.wait_ge(tables_in[0], 16 * QR)
            for j in range(3):
                add_bias(0, 0, j)
            body(0, 0, False)
            with dve.Fori(1, BODIES - 2) as b:
                body(b, 1, False)
            body(BODIES - 2, 1, False)
            body(BODIES - 1, 0, True)
            scale_unit(BODIES - 1, UNITS - 1)

        @block.tensor
        def _(pe):
            def score(b, j):
                u, h = j // NH, j % NH
                if h == 0:
                    pe.wait_ge(q_placed, 2 * (UNITS * b + u + 1))
                    if u % COLS == 0:
                        pe.wait_ge(strip_in[u // COLS], 32 * (b + 1))
                at_least(pe, biased_made, STEPS * b + j - 3)
                keys = k_strip[:, u // COLS, h // 2, :].rearrange("p (r w) -> p r w", w=W)
                k0 = K0[u % COLS]
                nc.tensor.matmul(s_banks[j % 4][:, 0:KEYS], q_block[:, u % 2, h, :], keys[:, :, k0:k0 + KC],
                                 start=True, stop=True).then_inc(scored, 1)

            def turn(b, j):
                pe.wait_ge(exped, STEPS * b + j + 1)
                at_least(pe, turned_act if j % 2 == 0 else turned_dve, STEPS // 2 * b + j // 2)
                for c in range(4):
                    last = nc.tensor.transpose(t_banks[j % 2][:, c, :], probs[:, j % 4, c * P:(c + 1) * P], ident[:])
                last.then_inc(probs_turned, 1)

            def value(b, j):
                u, h = j // NH, j % NH
                pe.wait_ge(turned_act if j % 2 == 0 else turned_dve, STEPS // 2 * b + j // 2 + 1)
                if h == 0:
                    pe.wait_ge(v_in[u % 2], 16 * KR * (UNITS // 2 * b + u // 2 + 1))
                    at_least(pe, scaled, UNITS * b + u - 1)
                cols = slice(h * NHD, (h + 1) * NHD)
                for c in range(4):
                    last = nc.tensor.matmul(o_banks[u % 2][:, cols], probs_T[:, j % 2, c, :],
                                            v_block[:, u % 2, c, cols], start=(c == 0), stop=(c == 3))
                last.then_inc(valued, 1)

            pe.wait_ge(cleared, 4)
            for j in range(3):
                score(0, j)
            turn(0, 0)

            def body(b, kind, last):
                for k in range(STEPS):
                    if k + 3 < STEPS:
                        score(b, k + 3)
                    elif not last:
                        score(b + 1, k + 3 - STEPS)
                    if k + 1 < STEPS:
                        turn(b, k + 1)
                    elif not last:
                        turn(b + 1, 0)
                    value(b, k)

            bodies(pe, body)


def out_stage(nc, x_tiles, w_out, ret_gain, gate_rows, decays, na_d, part_d, qf_d, kv_d, gate_d, ident, exps, y_tiles):
    with ExitStack() as ctx:
        sb = lambda n, s, d=F32: ctx.enter_context(nc.sbuf_tensor(f"o_{n}", s, d))
        sem = lambda n: ctx.enter_context(nc.semaphore(f"o_{n}"))
        w_hi, w_lo = sb("w_hi", [P, KB, D], F32R), sb("w_lo", [P, KB, D], F32R)
        w_raw = sb("w_raw", [P, 2, D])
        lg = sb("lg", [P, 2 * RH])
        chunk_decay = sb("chunk_decay", [P, RH])
        gain = sb("gain", [P, HALF])
        out_gate = sb("out_gate", [P, 2, D])
        x = sb("x", [P, 2, D])
        part, qf, kv, gate = (sb(n, [P, 2, HALF]) for n in ("part", "qf", "kv", "gate"))
        mix = sb("mix", [P, 2, D])
        state = sb("state_f", [P, 2, HALF])
        total = sb("total", [P, HALF])
        squares = sb("squares", [P, HALF])
        stat = sb("stat", [P, 3, RH])
        m_hi, m_lo = sb("m_hi", [P, 2, KB, P], F32R), sb("m_lo", [P, 2, KB, P], F32R)
        y = sb("y", [P, 2, D])
        cross_bank = ctx.enter_context(nc.psum_tensor("o_cross", [P, 512], F32))
        turn_banks = [ctx.enter_context(nc.psum_tensor(f"o_turn{j}", [P, 4, P], F32)) for j in range(2)]
        banks = [ctx.enter_context(nc.psum_tensor(f"o_proj{j}", [P, 512], F32)) for j in range(4)]
        wait_apart = apart(sem("passed"))
        const_in, w_in = sem("const_in"), [sem("w_in0"), sem("w_in1")]
        w_hi_made, w_lo_made, lg_made, decay_made = sem("w_hi_made"), sem("w_lo_made"), sem("lg_made"), sem("decay_made")
        tile_in, x_in = [sem("tile_in0"), sem("tile_in1")], [sem("x_in0"), sem("x_in1")]
        state_decayed, state_made, crossed = sem("state_decayed"), sem("state_made"), sem("crossed")
        totalled, squared, summed, meaned, rstd_made = sem("totalled"), sem("squared"), sem("summed"), sem("meaned"), sem("rstd")
        gained, normed, mixed, mix_turned = sem("gained"), sem("normed"), sem("mixed"), sem("mix_turned")
        hi_made, lo_made, projected, scaled, added = sem("hi_made"), sem("lo_made"), sem("projected"), sem("scaled"), sem("added")
        y_stored = [sem("y_stored0"), sem("y_stored1")]
        block = ctx.enter_context(nc.Block())

        @block.sync
        def _(sp):
            def load_tile(t, par):
                wait_apart(sp, mixed, t - 1)
                wait_apart(sp, mix_turned, t - 1)
                for dst, src in ((kv, kv_d), (qf, qf_d), (part, part_d), (gate, gate_d)):
                    sp.dma_start(dst[:, par], src[t]).then_inc(tile_in[par], 16)
                sp.dma_start(mix[:, par, 0:HALF], na_d[t]).then_inc(tile_in[par], 16)

            def load_x(t, par):
                wait_apart(sp, added, 2 * (t - 1))
                sp.dma_start(x[:, par], x_tiles[t]).then_inc(x_in[par], 16)

            def store_y(t, par):
                wait_apart(sp, added, 2 * t + 2)
                sp.dma_start(y_tiles[t], y[:, par]).then_inc(y_stored[par], 16)

            sp.dma_start(lg[:], decays.partition_broadcast(P)).then_inc(const_in, 16)
            sp.dma_start(gain[:], ret_gain.partition_broadcast(P)).then_inc(const_in, 16)
            for s in range(2):
                sp.dma_start(out_gate[:, s], gate_rows[s].partition_broadcast(P)).then_inc(const_in, 16)
            load_tile(0, 0)
            load_tile(1, 1)
            for k in range(KB):
                if k >= 2:
                    wait_apart(sp, w_lo_made, k - 1)
                sp.dma_start(w_raw[:, k % 2], w_out[k * P:(k + 1) * P, :]).then_inc(w_in[k % 2], 16)
            load_x(0, 0)
            load_x(1, 1)

            def body(i, last):
                for par in range(2):
                    t = 2 * i + par
                    if not last:
                        load_tile(t + 2, par)
                    store_y(t, par)
                    if not last:
                        load_x(t + 2, par)

            over_pairs(sp, body)
            for par in range(2):
                wait_apart(sp, y_stored[par], 16 * PAIRS)

        def ahead(body, i, last):
            body(2 * i + 1, 1, i)
            if not last:
                body(2 * i + 2, 0, i + 1)

        @block.gpsimd
        def _(pool):
            def gate_and_rstd(t, par, i):
                wait_apart(pool, tile_in[par], 80 * (i + 1))
                nc.gpsimd.tensor_tensor(gate[:, par], gate[:, par], gain[:], ALU.mult).then_inc(gained, 1)
                wait_apart(pool, meaned, t + 1)
                nc.gpsimd.tensor_tensor(stat[:, 2, :], stat[:, 1, :], exps[:, 0:RH], ALU.pow).then_inc(rstd_made, 1)

            def add_x(t, par, i):
                wait_apart(pool, x_in[par], 16 * (i + 1))
                for n in range(2):
                    cols = slice(n * 512, (n + 1) * 512)
                    wait_apart(pool, scaled, 2 * t + n + 1)
                    nc.gpsimd.tensor_tensor(y[:, par, cols], y[:, par, cols], x[:, par, cols],
                                            ALU.add).then_inc(added, 1)

            wait_apart(pool, const_in, 64)
            gate_and_rstd(0, 0, 0)

            def body(i, last):
                gate_and_rstd(2 * i + 1, 1, i)
                add_x(2 * i, 0, i)
                if not last:
                    gate_and_rstd(2 * i + 2, 0, i + 1)
                add_x(2 * i + 1, 1, i)

            over_pairs(pool, body)

        @block.scalar
        def _(act):
            act.wait_ge(const_in, 64)
            nc.scalar.activation(lg[:], lg[:], ACT.Exp).then_inc(lg_made, 1)
            act.wait_ge(lg_made, 2)
            nc.scalar.activation(chunk_decay[:], lg[:, 0:RH], ACT.Exp, scale=float(C)).then_inc(decay_made, 1)
            for k in range(KB):
                act.wait_ge(w_in[k % 2], 16 * (k // 2 + 1))
                nc.scalar.activation(w_hi[:, k, :], w_raw[:, k % 2], ACT.Copy).then_inc(w_hi_made, 1)

            def square(t):
                act.wait_ge(totalled, t + 1)
                at_least(act, summed, t)
                nc.scalar.activation(squares[:], total[:], ACT.Square).then_inc(squared, 1)

            def high(t, par):
                act.wait_ge(mix_turned, t + 1)
                at_least(act, projected, 2 * (t - 1))
                for j in range(2):
                    last = nc.scalar.activation(m_hi[:, par, 4 * j:4 * j + 4].rearrange("p k t -> p (k t)"),
                                                turn_banks[j][:].rearrange("p k t -> p (k t)"), ACT.Copy)
                last.then_inc(hi_made, 1)

            square(0)
            high(0, 0)

            def body(i, last):
                square(2 * i + 1)
                high(2 * i + 1, 1)
                if not last:
                    square(2 * i + 2)
                    high(2 * i + 2, 0)

            over_pairs(act, body)

        @block.vector
        def _(dve):
            dve.wait_ge(lg_made, 1)
            nc.vector.tensor_scalar(lg[:], lg[:], -1.0, None, ALU.mult).then_inc(lg_made, 1)
            nc.vector.memset(state[:, 1], 0.0).then_inc(state_made, 1)

            def carry(t, par, i):
                dve.wait_ge(tile_in[par], 80 * (i + 1))
                dve.wait_ge(state_made, t + 1)
                at_least(dve, crossed, t)
                if isinstance(t, int) and t == T_SAMPLE // P - 1:
                    nc.vector.memset(state[:, par], 0.0).then_inc(state_made, 1)
                    return
                for h in range(RH):
                    cols = slice(h * RHD, (h + 1) * RHD)
                    last = nc.vector.scalar_tensor_tensor(out=state[:, par, cols], in0=state[:, 1 - par, cols],
                                                          scalar=chunk_decay[:, h:h + 1], in1=kv[:, par, cols],
                                                          op0=ALU.mult, op1=ALU.add)
                last.then_inc(state_made, 1)

            def norm(t, par):
                dve.wait_ge(crossed, t + 1)
                nc.vector.tensor_tensor(total[:], cross_bank[:], part[:, par], ALU.add).then_inc(totalled, 1)
                dve.wait_ge(squared, t + 1)
                nc.vector.tensor_reduce(stat[:, 0, :], squares[:].rearrange("p (h d) -> p h d", h=RH), AX.X,
                                        ALU.add).then_inc(summed, 1)
                dve.wait_ge(summed, t + 1)
                nc.vector.tensor_scalar(stat[:, 1, :], stat[:, 0, :], 1.0 / RHD, EPS, ALU.mult,
                                        ALU.add).then_inc(meaned, 1)
                dve.wait_ge(rstd_made, t + 1)
                at_least(dve, mix_turned, t - 1)
                dve.wait_ge(gained, t + 1)
                for h in range(RH):
                    cols = slice(h * RHD, (h + 1) * RHD)
                    last = nc.vector.scalar_tensor_tensor(out=mix[:, par, HALF + h * RHD:HALF + (h + 1) * RHD],
                                                          in0=total[:, cols], scalar=stat[:, 2, h:h + 1],
                                                          in1=gate[:, par, cols], op0=ALU.mult, op1=ALU.mult)
                last.then_inc(mixed, 1)

            def low(t, par):
                dve.wait_ge(hi_made, t + 1)
                for j in range(2):
                    hi = m_hi[:, par, 4 * j:4 * j + 4].bitcast(F32)
                    last = nc.vector.tensor_tensor(m_lo[:, par, 4 * j:4 * j + 4], turn_banks[j][:], hi, ALU.subtract)
                last.then_inc(lo_made, 1)

            def scale(t, par, n, seq, i):
                dve.wait_ge(projected, 2 * t + n + 1)
                if n == 0:
                    at_least(dve, y_stored[par], 16 * i)
                cols = slice(n * 512, (n + 1) * 512)
                nc.vector.tensor_tensor(y[:, par, cols], banks[2 * par + n][:], out_gate[:, seq, cols],
                                        ALU.mult).then_inc(scaled, 1)

            def step(t, par, i):
                carry(t, par, i)
                norm(t, par)

            dve.wait_ge(decay_made, 1)
            dve.wait_ge(const_in, 64)
            for k in range(KB):
                dve.wait_ge(w_hi_made, k + 1)
                nc.vector.tensor_tensor(w_lo[:, k, :], w_raw[:, k % 2], w_hi[:, k, :].bitcast(F32),
                                        ALU.subtract).then_inc(w_lo_made, 1)
            carry(0, 0, 0)
            norm(0, 0)
            low(0, 0)
            carry(1, 1, 0)

            def body(i, last, seq):
                for par in range(2):
                    t = 2 * i + par
                    if not (last and par == 1):
                        norm(t + 1, 1 - par)
                        if not last:
                            carry(t + 2, par, i + 1)
                    scale(t, par, 0, seq, i)
                    if not (last and par == 1):
                        low(t + 1, 1 - par)
                    scale(t, par, 1, seq, i)

            seam = T_SAMPLE // P // 2
            body(0, False, 0)
            with dve.Fori(1, seam - 2) as i:
                body(i, False, 0)
            body(seam - 2, False, 0)
            body(seam - 1, False, 0)
            with dve.Fori(seam, PAIRS - 1) as i:
                body(i, False, 1)
            body(PAIRS - 1, True, 1)

        @block.tensor
        def _(pe):
            def cross(t, par, i):
                pe.wait_ge(state_made, t + 1)
                pe.wait_ge(tile_in[par], 80 * (i + 1))
                at_least(pe, totalled, t)
                for h in range(RH):
                    cols = slice(h * C, (h + 1) * C)
                    last = nc.tensor.matmul(cross_bank[:, cols], qf[:, par, cols], state[:, 1 - par, cols],
                                            start=True, stop=True)
                last.then_inc(crossed, 1)

            def turn(t, par):
                pe.wait_ge(mixed, t + 1)
                at_least(pe, lo_made, t)
                for k in range(KB):
                    last = nc.tensor.transpose(turn_banks[k // 4][:, k % 4, :], mix[:, par, k * P:(k + 1) * P],
                                               ident[:])
                last.then_inc(mix_turned, 1)

            def project(t, par, n):
                pe.wait_ge(lo_made, t + 1)
                at_least(pe, scaled, 2 * (t - 2) + n + 1)
                for k in range(KB):
                    if isinstance(t, int) and t == 0 and n == 0:
                        pe.wait_ge(w_lo_made, k + 1)
                    for j, (m, w) in enumerate([(m_hi, w_hi), (m_hi, w_lo), (m_lo, w_hi)]):
                        last = nc.tensor.matmul(banks[2 * par + n][:], m[:, par, k, :], w[:, k, n * 512:(n + 1) * 512],
                                                start=(k == 0 and j == 0), stop=(k == KB - 1 and j == 2))
                last.then_inc(projected, 1)

            cross(0, 0, 0)
            turn(0, 0)
            cross(1, 1, 0)

            def body(i, last):
                for par in range(2):
                    t = 2 * i + par
                    project(t, par, 0)
                    if not (last and par == 1):
                        turn(t + 1, 1 - par)
                    project(t, par, 1)
                    if not last:
                        cross(t + 2, par, i + 1)

            over_pairs(pe, body)


def build(nc, a, y):
    dram = lambda n, s: nc.dram_tensor(n, s, F32, kind="Internal").ap()
    with ExitStack() as ctx:
        sb = lambda n, s: ctx.enter_context(nc.sbuf_tensor(n, s, F32))
        ident = sb("ident", [P, P])
        modx = sb("modx", [P, TILES, 16])
        exps = sb("minus_half", [P, NH])
        gate_rows = dram("gate_rows", (2, D))
        bias_rows = dram("bias_rows", (QC, 3, NH * NDR, KC))
        qT_d, kT_d = dram("qT_d", (P, 4, T)), dram("kT_d", (P, 4, T))
        vg_d = dram("vg_d", (TILES, P, D))
        na_d = dram("na_d", (TILES, P, HALF))
        part_d, qf_d, kv_d, rg_d = (dram(n, (TILES, P, HALF)) for n in ("part_d", "qf_d", "kv_d", "rg_d"))
        x_tiles, y_tiles = a["x"], y
        modulation_stage(nc, a["cT"], a["w_ada"], a["b_ada"], a["norm_gain"], a["rpb"], ident, modx, exps, gate_rows,
                         bias_rows)
        attention_in_stage(nc, x_tiles, a["w_in"][:, 0:4 * HALF], a["qk_gain"], modx, ident, exps, qT_d, kT_d, vg_d)
        retention_in_stage(nc, x_tiles, a["w_in"][:, 4 * HALF:8 * HALF], a["decays"], a["rope"], modx, ident, exps,
                           part_d, qf_d, kv_d, rg_d)
        attention_stage(nc, qT_d, kT_d, vg_d, bias_rows, ident, na_d)
        out_stage(nc, x_tiles, a["w_out"], a["ret_gain"], gate_rows, a["decays"], na_d, part_d, qf_d, kv_d, rg_d,
                  ident, exps, y_tiles)


def rope_table():
    half = RHD // 2
    inv = np.float32(10000.0) ** (-np.arange(half, dtype=np.float32) / np.float32(half))
    pos = np.concatenate([np.arange(T_SAMPLE), np.arange(T_PROMPT)]).astype(np.float32)
    angle = pos[:, None] * inv[None, :]
    return np.stack([np.cos(angle), np.sin(angle)], axis=1).astype(np.float32).reshape(TILES, P, 2, half)


def kernel(x_prompt, x_sample, c_prompt, c_sample, norm_gain, w_ada, b_ada, w_in, na_q_gain, na_k_gain, na_rpb,
           ret_decay_f, ret_decay_b, ret_out_gain, w_out):
    import concourse.bacc as bacc
    from concourse.bass_utils import run_bass_kernel_spmd

    c_both = np.concatenate([np.asarray(c_sample), np.asarray(c_prompt)])
    arrays = {
        "x": np.concatenate([np.asarray(x_sample)[0], np.asarray(x_prompt)[0]]).reshape(TILES, P, D),
        "cT": c_both.T.reshape(KB, P, 2).transpose(1, 0, 2),
        "norm_gain": np.asarray(norm_gain)[0].reshape(KB, P).T,
        "w_ada": np.asarray(w_ada)[0],
        "b_ada": np.asarray(b_ada),
        "w_in": np.asarray(w_in)[0],
        "qk_gain": np.stack([np.tile(np.asarray(g)[0], 2) for g in (na_q_gain, na_k_gain)], axis=1),
        "rpb": np.asarray(na_rpb)[0].reshape(NH * NDR, NDC),
        "decays": np.concatenate([np.asarray(ret_decay_f)[0], np.asarray(ret_decay_b)[0]]),
        "ret_gain": np.asarray(ret_out_gain)[0].reshape(HALF),
        "w_out": np.asarray(w_out)[0],
        "rope": rope_table(),
    }
    nc = bacc.Bacc("TRN2", target_bir_lowering=False, num_devices=1)
    arrays = {f"in_{n}": np.ascontiguousarray(v) for n, v in arrays.items()}
    aps = {n[3:]: nc.dram_tensor(n, v.shape, mybir.dt.from_np(v.dtype), kind="ExternalInput").ap()
           for n, v in arrays.items()}
    y = nc.dram_tensor("y", (TILES, P, D), F32, kind="ExternalOutput").ap()
    build(nc, aps, y)
    got = run_bass_kernel_spmd(nc, [arrays], core_ids=[0]).results[0]["y"].reshape(T, D)
    return got[T_SAMPLE:].reshape(1, T_PROMPT, D), got[:T_SAMPLE].reshape(1, T_SAMPLE, D)
```

```python
from contextlib import ExitStack

import concourse.bass as bass
import numpy as np
from concourse import mybir

F32 = mybir.dt.float32
F32R = mybir.dt.float32r
BF16 = mybir.dt.bfloat16
ALU = mybir.AluOpType
ACT = mybir.ActivationFunctionType
AX = mybir.AxisListType

P = 128
D = 1024
KB = D // P
T_SAMPLE, T_PROMPT = 4096, 1024
T = T_SAMPLE + T_PROMPT
TILES = T // P
PAIRS = TILES // 2
HALF = D // 2
NH, NHD = 8, 64
RH, RHD = 4, 128
C = 128
EPS = 1e-6
W = 64
QR, QC = 8, 16
KR, KC = 15, 32
KEYS = KR * KC
WIN_H, WIN_W = 8, 16
NDR, NDC = 2 * WIN_H - 1, 2 * WIN_W - 1
MASKED = 1.0e30
COLS = W // QC
K0 = [0, 8, 24, 32]
KIND = [0, 1, 1, 2]
S_ROWS, P_ROWS = T_SAMPLE // W, T_PROMPT // W
STRIPS = (
    [(0, 0), (S_ROWS, S_ROWS)]
    + [(QR * b, QR * b - 4) for b in range(1, S_ROWS // QR - 1)]
    + [(S_ROWS - QR, S_ROWS - KR), (S_ROWS + P_ROWS - QR, S_ROWS + P_ROWS - KR)]
)
GH = 4
GW = GH * NHD


def at_least(eng, sem, count):
    if isinstance(count, int) and count <= 0:
        return
    eng.wait_ge(sem, count)


def apart(passed):

    def wait_apart(eng, sem, count):
        at_least(eng, sem, count)
        if not isinstance(count, int):
            eng.sem_inc(passed, 1)

    return wait_apart


def over_pairs(eng, body):
    body(0, False)
    with eng.Fori(1, PAIRS - 1) as i:
        body(i, False)
    body(PAIRS - 1, True)


def modulation_stage(nc, cT, w_ada, b_ada, norm_gain, rpb, ident, modx, exps, gate_rows,
                     bias_rows):
    with ExitStack() as ctx:
        sb = lambda n, s, d=F32: ctx.enter_context(nc.sbuf_tensor(n, s, d))
        sem = lambda n: ctx.enter_context(nc.semaphore(n))
        ada = sb("ada", [P, KB, 3 * D])
        cond = sb("cond", [P, KB, 2])
        silu_c = sb("silu_c", [P, KB, 2])
        b_rows = sb("b_rows", [2, 3 * D])
        mod = sb("mod", [2, 3 * D])
        gain = sb("gain", [P, KB])
        mod_cols = sb("mod_cols", [P, 16, 2])
        one_seq = sb("one_seq", [P, 2, 16])
        rpb_rows = sb("rpb_rows", [NH * NDR, NDC])
        spread = sb("spread", [NH * NDR, 3, QC, KC])
        banks = [ctx.enter_context(nc.psum_tensor(f"mod_bank{j}", [P, 512], F32)) for j in range(6)]
        cols_bank = ctx.enter_context(nc.psum_tensor("cols_bank", [P, 16, 2], F32))
        wait_apart = apart(sem("m_passed"))
        small_in, ada_in = sem("small_in"), [sem(f"ada_in{k}") for k in range(KB)]
        ident_made, silu_made, mod_summed = sem("ident_made"), sem("silu_made"), sem("mod_summed")
        mod_made, cols_turned, modx_made = sem("mod_made"), sem("cols_turned"), sem("modx_made")
        spread_made, mod_stored = sem("spread_made"), sem("mod_stored")
        block = ctx.enter_context(nc.Block())

        @block.sync
        def _(sp):
            sp.dma_start(cond[:], cT).then_inc(small_in, 16)
            sp.dma_start(b_rows[0:1, :], b_ada).then_inc(small_in, 16)
            sp.dma_start(b_rows[1:2, :], b_ada).then_inc(small_in, 16)
            sp.dma_start(gain[:], norm_gain).then_inc(small_in, 16)
            sp.dma_start(rpb_rows[:], rpb).then_inc(small_in, 16)
            for k in range(KB):
                sp.dma_start(ada[:, k, :], w_ada[k * P:(k + 1) * P, :]).then_inc(ada_in[k], 16)
            wait_apart(sp, spread_made, 6)
            for k in range(3):
                sp.dma_start(bias_rows[:, k].rearrange("c hd x -> hd c x"), spread[:, k]).then_inc(mod_stored, 16)
            wait_apart(sp, mod_made, 6)
            sp.dma_start(gate_rows, mod[:, 2 * D:3 * D]).then_inc(mod_stored, 16)
            wait_apart(sp, mod_stored, 64)

        @block.gpsimd
        def _(pool):
            nc.gpsimd.memset(ident[:], 0.0).then_inc(ident_made, 1)
            wait_apart(pool, ident_made, 1)
            nc.gpsimd.affine_select(out=ident[:], in_=ident[:], compare_op=ALU.not_equal, fill=1.0, base=0,
                                    pattern=[[-1, P]], channel_multiplier=1).then_inc(ident_made, 1)
            nc.gpsimd.memset(exps[:], -0.5).then_inc(ident_made, 1)

        @block.scalar
        def _(act):
            act.wait_ge(small_in, 80)
            nc.scalar.activation(silu_c[:], cond[:], ACT.Silu).then_inc(silu_made, 1)

        @block.vector
        def _(dve):
            nc.vector.memset(spread[:], MASKED).then_inc(spread_made, 1)
            dve.wait_ge(small_in, 80)
            dve.wait_ge(spread_made, 1)
            mid = NDC // 2

            def put(kind, c0, c1, key0, key_step, dc0, dc_step):
                flat = spread[:].rearrange("q k c x -> q (k c x)")
                src = rpb_rows[:]
                for c in range(c0, c1):
                    k_at = (kind * QC + c) * KC + key0 + key_step * (c - c0)
                    d_at = dc0 + dc_step * (c - c0)
                    last = nc.vector.tensor_scalar(flat[:, k_at:k_at + WIN_W], src[:, d_at:d_at + WIN_W], -1.0,
                                                   None, ALU.mult)
                last.then_inc(spread_made, 1)

            put(0, 0, 8, 0, 0, mid, -1)
            put(0, 8, QC, 0, 1, mid - 8, 0)
            put(1, 0, QC, 0, 1, mid - 8, 0)
            put(2, 0, 9, 8, 1, mid - 8, 0)
            put(2, 9, QC, 16, 0, mid - 9, -1)
            dve.wait_ge(mod_summed, 1)
            for n in range(6):
                nc.vector.tensor_tensor(mod[:, 512 * n:512 * (n + 1)], banks[n][0:2, :],
                                        b_rows[:, 512 * n:512 * (n + 1)], ALU.add).then_inc(mod_made, 1)
            dve.wait_ge(cols_turned, 1)
            nc.vector.tensor_copy(mod_cols[:], cols_bank[:]).then_inc(modx_made, 1)
            dve.wait_ge(modx_made, 1)
            for s in range(2):
                nc.vector.scalar_tensor_tensor(out=one_seq[:, s, 0:8], in0=mod_cols[:, 8:16, s], scalar=1.0,
                                               in1=gain[:], op0=ALU.add, op1=ALU.mult)
                nc.vector.tensor_copy(one_seq[:, s, 8:16], mod_cols[:, 0:8, s]).then_inc(modx_made, 1)
            dve.wait_ge(modx_made, 3)
            t_s = T_SAMPLE // P
            nc.vector.tensor_copy(modx[:, 0:t_s, :], one_seq[:, 0:1, :].to_broadcast([P, t_s, 16]))
            nc.vector.tensor_copy(modx[:, t_s:TILES, :],
                                  one_seq[:, 1:2, :].to_broadcast([P, TILES - t_s, 16])).then_inc(modx_made, 1)

        @block.tensor
        def _(pe):
            pe.wait_ge(silu_made, 1)
            for k in range(KB):
                pe.wait_ge(ada_in[k], 16)
                for n in range(6):
                    last = nc.tensor.matmul(banks[n][0:2, :], silu_c[:, k, :], ada[:, k, 512 * n:512 * (n + 1)],
                                            start=(k == 0), stop=(k == KB - 1))
            last.then_inc(mod_summed, 1)
            pe.wait_ge(ident_made, 2)
            pe.wait_ge(mod_made, 6)
            for j in range(16):
                last = nc.tensor.transpose(cols_bank[:, j, :], mod[:, j * P:(j + 1) * P], ident[0:2, 0:2])
            last.then_inc(cols_turned, 1)


class Weights:

    def __init__(self, nc, ctx, tag, w, width):
        self.nc, self.w = nc, w
        with nc.sbuf_tensor(f"{tag}_raw", [P, KB, width], F32) as self.raw:
            pass
        self.lo, self.hi = (ctx.enter_context(nc.sbuf_tensor(f"{tag}_{n}", [P, KB, width], F32R)) for n in ("lo", "hi"))
        self.landed = [ctx.enter_context(nc.semaphore(f"{tag}_landed{j}")) for j in range(2)]
        self.hi_made, self.lo_made = (ctx.enter_context(nc.semaphore(f"{tag}_{n}")) for n in ("hi_made", "lo_made"))

    def load(self, eng, k):
        eng.dma_start(self.raw[:, k], self.w[k * P:(k + 1) * P, :]).then_inc(self.landed[k // 4], 16)

    def make_hi(self, act, k):
        act.wait_ge(self.landed[k // 4], 64)
        self.nc.scalar.activation(self.hi[:, k], self.raw[:, k], ACT.Copy).then_inc(self.hi_made, 1)

    def make_lo(self, dve, k):
        dve.wait_ge(self.hi_made, k + 1)
        self.nc.vector.tensor_tensor(self.lo[:, k], self.raw[:, k], self.hi[:, k].bitcast(F32),
                                     ALU.subtract).then_inc(self.lo_made, 1)


class Front:

    def __init__(self, nc, ctx, tag, x_tiles, w, modx, ident, half_eps, reverse):
        sb = lambda n, s, d=F32: ctx.enter_context(nc.sbuf_tensor(f"{tag}_{n}", s, d))
        sem = lambda n: ctx.enter_context(nc.semaphore(f"{tag}_{n}"))
        self.nc, self.x_tiles, self.w, self.modx, self.ident = nc, x_tiles, w, modx, ident
        self.half, self.reverse = half_eps, reverse
        self.w_hi, self.w_lo = sb("w_hi", [P, KB, 4 * HALF], F32R), sb("w_lo", [P, KB, 4 * HALF], F32R)
        self.x = sb("x", [P, 2, D])
        self.h_full = sb("h_full", [P, D])
        self.h_hi, self.h_lo = sb("h_hi", [P, 2, KB, P], F32R), sb("h_lo", [P, 2, KB, P], F32R)
        self.junk = sb("junk", [P, D], BF16)
        self.work = sb("work", [P, 4096])
        self.x_stat = sb("x_stat", [P, 4])
        self.mod_now = sb("mod_now", [P, 2, 16])
        self.turn_banks = [ctx.enter_context(nc.psum_tensor(f"{tag}_turn{j}", [P, 4, P], F32)) for j in range(2)]
        self.wait_apart = apart(sem("passed"))
        self.x_in = [sem("x_in0"), sem("x_in1")]
        self.w_in = [sem("w_in0"), sem("w_in1")]
        self.w_hi_made, self.w_lo_made = sem("w_hi_made"), sem("w_lo_made")
        self.x_squared, self.x_mean, self.x_rstd = sem("x_squared"), sem("x_mean"), sem("x_rstd")
        self.x_normed, self.x_turned, self.mod_placed = sem("x_normed"), sem("x_turned"), sem("mod_placed")
        self.h_modulated, self.h_hi_made, self.h_split = sem("h_modulated"), sem("h_hi_made"), sem("h_split")
        self.projected = sem("projected")

    def tile(self, s):
        return TILES - 1 - s if self.reverse else s

    def load_x(self, sp, s, par):
        self.wait_apart(sp, self.x_normed, s - 1)
        sp.dma_start(self.x[:, par, :], self.x_tiles[self.tile(s)]).then_inc(self.x_in[par], 16)

    def load_w(self, sp):
        for k in range(KB):
            if k >= 2:
                self.wait_apart(sp, self.w_lo_made, k - 1)
            sp.dma_start(self.work[:, 2048 * (k % 2):2048 * (k % 2 + 1)],
                         self.w[k * P:(k + 1) * P, :]).then_inc(self.w_in[k % 2], 16)

    def split_w_hi(self, act, k):
        act.wait_ge(self.w_in[k % 2], 16 * (k // 2 + 1))
        self.nc.scalar.activation(self.w_hi[:, k, :], self.work[:, 2048 * (k % 2):2048 * (k % 2 + 1)],
                                  ACT.Copy).then_inc(self.w_hi_made, 1)

    def split_w_lo(self, dve, k):
        dve.wait_ge(self.w_hi_made, k + 1)
        self.nc.vector.tensor_tensor(self.w_lo[:, k, :], self.work[:, 2048 * (k % 2):2048 * (k % 2 + 1)],
                                     self.w_hi[:, k, :].bitcast(F32), ALU.subtract).then_inc(self.w_lo_made, 1)

    def square_x(self, act, s, par, i):
        act.wait_ge(self.x_in[par], 16 * (i + 1))
        at_least(act, self.x_mean, s)
        self.nc.scalar.activation(self.junk[:], self.x[:, par, :], ACT.Square,
                                  accum_out=self.x_stat[:, 0:1]).then_inc(self.x_squared, 1)

    def mean_x(self, dve, s):
        dve.wait_ge(self.x_squared, s + 1)
        self.nc.vector.tensor_scalar(self.x_stat[:, 1:2], self.x_stat[:, 0:1], 1.0 / D, EPS, ALU.mult,
                                     ALU.add).then_inc(self.x_mean, 1)

    def rstd_x(self, pool, s):
        self.wait_apart(pool, self.x_mean, s + 1)
        self.nc.gpsimd.tensor_tensor(self.x_stat[:, 2:3], self.x_stat[:, 1:2], self.half[:, 0:1],
                                     ALU.pow).then_inc(self.x_rstd, 1)

    def norm_x(self, dve, s, par):
        dve.wait_ge(self.x_rstd, s + 1)
        at_least(dve, self.x_turned, s)
        at_least(dve, self.h_split, s)
        self.nc.vector.tensor_scalar(self.h_full[:], self.x[:, par, :], self.x_stat[:, 2:3], None,
                                     ALU.mult).then_inc(self.x_normed, 1)

    def place_mod(self, pool, s, par):
        self.wait_apart(pool, self.h_modulated, s - 1)
        self.nc.gpsimd.tensor_copy(self.mod_now[:, par, :], self.modx[:, bass.ds(self.tile(s), 1), :]
                                   .rearrange("p a b -> p (a b)")).then_inc(self.mod_placed, 1)

    def turn_x(self, pe, s):
        pe.wait_ge(self.x_normed, s + 1)
        at_least(pe, self.h_modulated, s)
        for k in range(KB):
            last = self.nc.tensor.transpose(self.turn_banks[k // 4][:, k % 4, :],
                                            self.h_full[:, k * P:(k + 1) * P], self.ident[:])
        last.then_inc(self.x_turned, 1)

    def modulate(self, act, s, par):
        act.wait_ge(self.x_turned, s + 1)
        act.wait_ge(self.mod_placed, s + 1)
        for k in range(KB):
            last = self.nc.scalar.activation(self.h_full[:, k * P:(k + 1) * P], self.turn_banks[k // 4][:, k % 4, :],
                                             ACT.Identity, scale=self.mod_now[:, par, k:k + 1],
                                             bias=self.mod_now[:, par, KB + k:KB + k + 1])
        last.then_inc(self.h_modulated, 1)

    def split_h(self, dve, s, par):
        dve.wait_ge(self.h_modulated, s + 1)
        at_least(dve, self.projected, 4 * (s - 1))
        hi = self.h_hi[:, par].rearrange("p k t -> p (k t)")
        lo = self.h_lo[:, par].rearrange("p k t -> p (k t)")
        self.nc.vector.tensor_copy(hi, self.h_full[:]).then_inc(self.h_hi_made, 1)
        dve.wait_ge(self.h_hi_made, s + 1)
        self.nc.vector.tensor_tensor(lo, self.h_full[:], hi.bitcast(F32), ALU.subtract).then_inc(self.h_split, 1)

    def project(self, pe, s, par, n, bank):
        if n == 0:
            pe.wait_ge(self.h_split, s + 1)
        cols = slice(n * HALF, (n + 1) * HALF)
        for k in range(KB):
            if isinstance(s, int) and s == 0 and n == 0:
                pe.wait_ge(self.w_lo_made, k + 1)
            for j, (h, w) in enumerate([(self.h_hi, self.w_hi), (self.h_hi, self.w_lo), (self.h_lo, self.w_hi)]):
                last = self.nc.tensor.matmul(bank, h[:, par, k, :], w[:, k, cols], start=(k == 0 and j == 0),
                                             stop=(k == KB - 1 and j == 2))
        last.then_inc(self.projected, 1)


def attention_in_stage(nc, x_tiles, w, gains, modx, ident, exps, qT_d, kT_d, vg_d):
    with ExitStack() as ctx:
        f = Front(nc, ctx, "a", x_tiles, w, modx, ident, exps, False)
        sb = lambda n, s, d=F32: ctx.enter_context(nc.sbuf_tensor(n, s, d))
        sem = lambda n: ctx.enter_context(nc.semaphore(n))
        gain = sb("qk_gain", [P, 2])
        normed = f.work[:, 0:1024].rearrange("p (a n) -> p a n", a=2)
        squares = f.work[:, 1024:2048].rearrange("p (a n) -> p a n", a=2)
        vg = f.work[:, 2048:4096].rearrange("p (a n) -> p a n", a=2)
        turned = sb("qkT", [P, 2, 4, 2 * P])
        k_parts = sb("k_parts", [P, 2, 4, 2 * P], F32R)
        stat = sb("qk_stat", [P, 3, 2, NH])
        banks = [ctx.enter_context(nc.psum_tensor(f"a_proj{j}", [P, 512], F32)) for j in range(4)]
        qk_banks = [ctx.enter_context(nc.psum_tensor(f"a_qkT{j}", [P, 4, P], F32)) for j in range(2)]
        wait_apart = f.wait_apart
        gain_in, gain_made = sem("gain_in"), sem("gain_made")
        squared, summed, meaned, rstd_made = sem("qk_squared"), sem("qk_summed"), sem("qk_meaned"), sem("qk_rstd")
        qk_normed, qk_turned, qk_out = sem("qk_normed"), sem("qk_turned"), sem("qk_out")
        vg_made, k_split = sem("vg_made"), sem("k_split")
        vg_stored, qk_stored = [sem("vg_stored0"), sem("vg_stored1")], sem("qk_stored")
        block = ctx.enter_context(nc.Block())

        @block.sync
        def _(sp):
            for par in range(2):
                f.load_x(sp, par, par)
            sp.dma_start(gain[:], gains).then_inc(gain_in, 16)
            f.load_w(sp)

            def store_vg(t, par):
                wait_apart(sp, vg_made, 2 * t + 2)
                sp.dma_start(vg_d[t], vg[:, par, :]).then_inc(vg_stored[par], 16)

            def store_qk(i):
                tokens = bass.ds(i * 2 * P, 2 * P)
                wait_apart(sp, k_split, 4 * i + 4)
                for odd in range(2):
                    rows = slice(odd * NHD, (odd + 1) * NHD)
                    sp.dma_start(qT_d.rearrange("d (j x) t -> d j x t", x=2)[:, :, odd, tokens],
                                 turned[rows, 0]).then_inc(qk_stored, 16)
                    for part in range(2):
                        sp.dma_start(kT_d.rearrange("d (j x) t -> d j x t", x=2)
                                     [part * NHD:(part + 1) * NHD, :, odd, tokens],
                                     k_parts[rows, part].bitcast(F32)).then_inc(qk_stored, 16)

            def body(i, last):
                for par in range(2):
                    t = 2 * i + par
                    if not last:
                        f.load_x(sp, t + 2, par)
                    store_vg(t, par)
                store_qk(i)

            over_pairs(sp, body)
            wait_apart(sp, vg_stored[0], 16 * PAIRS)
            wait_apart(sp, vg_stored[1], 16 * PAIRS)
            wait_apart(sp, qk_stored, 96 * PAIRS)

        @block.gpsimd
        def _(pool):
            f.rstd_x(pool, 0)
            f.place_mod(pool, 0, 0)
            f.rstd_x(pool, 1)

            def body(i, last):
                for par in range(2):
                    t = 2 * i + par
                    for a in range(2):
                        wait_apart(pool, meaned, 2 * t + a + 1)
                        nc.gpsimd.tensor_tensor(stat[:, 2, a, :], stat[:, 1, a, :], exps[:, 0:NH],
                                                ALU.pow).then_inc(rstd_made, 1)
                    if not (last and par == 1):
                        f.place_mod(pool, t + 1, 1 - par)
                    if not last:
                        f.rstd_x(pool, t + 2)

            over_pairs(pool, body)

        @block.scalar
        def _(act):
            f.square_x(act, 0, 0, 0)
            f.modulate(act, 0, 0)
            f.square_x(act, 1, 1, 0)
            for k in range(KB):
                f.split_w_hi(act, k)

            def body(i, last):
                for par in range(2):
                    t = 2 * i + par
                    for a in range(2):
                        act.wait_ge(f.projected, 4 * t + a + 1)
                        at_least(act, summed, 2 * t + a - 1)
                        nc.scalar.activation(squares[:, a, :], banks[a][:], ACT.Square).then_inc(squared, 1)
                    if not (last and par == 1):
                        f.modulate(act, t + 1, 1 - par)
                    act.wait_ge(f.projected, 4 * t + 3)
                    at_least(act, vg_stored[par], 16 * i)
                    nc.scalar.activation(vg[:, par, 0:HALF], banks[2][:], ACT.Copy).then_inc(vg_made, 1)
                    if not last:
                        f.square_x(act, t + 2, par, i + 1)
                    act.wait_ge(f.projected, 4 * t + 4)
                    nc.scalar.activation(vg[:, par, HALF:D], banks[3][:], ACT.Silu).then_inc(vg_made, 1)

            over_pairs(act, body)

        @block.vector
        def _(dve):
            f.mean_x(dve, 0)
            f.norm_x(dve, 0, 0)
            f.split_h(dve, 0, 0)
            f.mean_x(dve, 1)
            f.norm_x(dve, 1, 1)
            for k in range(KB):
                f.split_w_lo(dve, k)
            dve.wait_ge(gain_in, 16)
            nc.vector.tensor_scalar(gain[:, 0:1], gain[:, 0:1], -(NHD ** -0.5), None, ALU.mult).then_inc(gain_made, 1)
            dve.wait_ge(gain_made, 1)

            def norm_heads(t, a):
                n = 2 * t + a
                dve.wait_ge(squared, n + 1)
                nc.vector.tensor_reduce(stat[:, 0, a, :], squares[:, a, :].rearrange("p (h d) -> p h d", h=NH),
                                        AX.X, ALU.add).then_inc(summed, 1)
                dve.wait_ge(summed, n + 1)
                nc.vector.tensor_scalar(stat[:, 1, a, :], stat[:, 0, a, :], 1.0 / NHD, EPS, ALU.mult,
                                        ALU.add).then_inc(meaned, 1)
                dve.wait_ge(rstd_made, n + 1)
                at_least(dve, qk_turned, n - 1)
                nc.vector.tensor_tensor(normed[:, a, :].rearrange("p (h d) -> p h d", h=NH),
                                        banks[a][:].rearrange("p (h d) -> p h d", h=NH),
                                        stat[:, 2, a, :].unsqueeze(2).to_broadcast([P, NH, NHD]),
                                        ALU.mult).then_inc(qk_normed, 1)

            def heads_out(i, t, par, a):
                dve.wait_ge(qk_turned, 2 * t + a + 1)
                if par == 0:
                    at_least(dve, qk_stored, 96 * i)
                nc.vector.tensor_scalar(turned[:, a, :, par * P:(par + 1) * P], qk_banks[a][:], gain[:, a:a + 1],
                                        None, ALU.mult).then_inc(qk_out, 1)

            def split_k(t, par):
                tokens = slice(par * P, (par + 1) * P)
                dve.wait_ge(qk_out, 2 * t + 2)
                nc.vector.tensor_copy(k_parts[:, 0, :, tokens], turned[:, 1, :, tokens]).then_inc(k_split, 1)
                dve.wait_ge(k_split, 2 * t + 1)
                nc.vector.tensor_tensor(k_parts[:, 1, :, tokens], turned[:, 1, :, tokens],
                                        k_parts[:, 0, :, tokens].bitcast(F32), ALU.subtract).then_inc(k_split, 1)

            def body(i, last):
                for par in range(2):
                    t = 2 * i + par
                    norm_heads(t, 0)
                    norm_heads(t, 1)
                    if not (last and par == 1):
                        f.split_h(dve, t + 1, 1 - par)
                    if not last:
                        f.mean_x(dve, t + 2)
                        f.norm_x(dve, t + 2, par)
                    heads_out(i, t, par, 0)
                    heads_out(i, t, par, 1)
                    split_k(t, par)

            over_pairs(dve, body)

        @block.tensor
        def _(pe):
            f.turn_x(pe, 0)

            def turn_heads(t, a):
                pe.wait_ge(qk_normed, 2 * t + a + 1)
                at_least(pe, qk_out, 2 * t + a - 1)
                for j in range(4):
                    last = nc.tensor.transpose(qk_banks[a][:, j, :], normed[:, a, j * P:(j + 1) * P], ident[:])
                last.then_inc(qk_turned, 1)

            def body(i, last):
                for par in range(2):
                    t = 2 * i + par
                    for n in range(4):
                        if n < 2:
                            at_least(pe, qk_normed, 2 * t + n - 1)
                        else:
                            at_least(pe, vg_made, 2 * t + n - 3)
                        f.project(pe, t, par, n, banks[n][:])
                        if n == 1 and not (last and par == 1):
                            f.turn_x(pe, t + 1)
                        if n == 2:
                            turn_heads(t, 0)
                    turn_heads(t, 1)

            over_pairs(pe, body)


def retention_in_stage(nc, x_tiles, w, decays, rope, modx, ident, exps, part_d, qf_d, kv_d, gate_d):
    with ExitStack() as ctx:
        f = Front(nc, ctx, "r", x_tiles, w, modx, ident, exps, True)
        sb = lambda n, s, d=F32: ctx.enter_context(nc.sbuf_tensor(n, s, d))
        sem = lambda n: ctx.enter_context(nc.semaphore(n))
        raw = f.work[:, 0:1024].rearrange("p (a n) -> p a n", a=2)
        rot = f.work[:, 1024:2048].rearrange("p (a n) -> p a n", a=2)
        v = f.work[:, 2048:2560]
        gate = f.work[:, 2560:3072]
        turned = f.work[:, 3072:4096].rearrange("p (a n) -> p a n", a=2)
        cs = sb("cos_sin", [P, 2, 2, 64])
        product = sb("rot_product", [P, 2, 256])
        q_dec = sb("q_dec", [P, 2, HALF])
        k_dec = sb("k_dec", [P, 2, HALF])
        weighted = sb("weighted", [P, HALF])
        state = sb("state_b", [P, 2, HALF])
        kv_out = sb("kv_out", [P, HALF])
        part = sb("part", [P, HALF])
        within = sb("within", [P, RH, C])
        q_scale = sb("q_scale", [P, 2, RH, C])
        lg = sb("lg", [P, 2 * RH])
        k_scale = sb("k_scale", [P, 2 * RH])
        chunk_decay = sb("chunk_decay", [P, 2 * RH])
        pos = sb("pos", [P, 2])
        proj = [ctx.enter_context(nc.psum_tensor(f"r_proj{j}", [P, 512], F32)) for j in range(2)]
        qk_banks = [ctx.enter_context(nc.psum_tensor(f"r_qkT{j}", [P, 4, P], F32)) for j in range(2)]
        so_bank = ctx.enter_context(nc.psum_tensor("r_so", [P, 512], F32))
        kv_bank = ctx.enter_context(nc.psum_tensor("r_kv", [P, 512], F32))
        wait_apart = f.wait_apart
        decay_in, lg_made, pos_made = sem("decay_in"), sem("lg_made"), sem("pos_made")
        const_made, expo_made = sem("const_made"), sem("expo_made")
        cs_in = [sem("cs_in0"), sem("cs_in1")]
        raw_made, multiplied, rotated = sem("raw_made"), sem("multiplied"), sem("rotated")
        v_made, gate_made = sem("v_made"), sem("gate_made")
        qk_turned, turned_out, q_decayed, k_decayed = sem("rqk_turned"), sem("turned_out"), sem("q_decayed"), sem("k_decayed")
        scored, kv_b_done, kv_f_done, part_done = sem("scored"), sem("kv_b_done"), sem("kv_f_done"), sem("part_done")
        weighted_made, state_decayed, state_made = sem("weighted_made"), sem("state_decayed"), sem("state_made")
        kv_out_made, part_made = sem("kv_out_made"), sem("part_made")
        kv_stored, part_stored, qf_stored, gate_stored = sem("kv_stored"), sem("part_stored"), sem("qf_stored"), sem("gate_stored")
        block = ctx.enter_context(nc.Block())

        def heads(ap):
            return ap.rearrange("p (h n) -> p h n", h=RH)

        @block.sync
        def _(sp):
            sp.dma_start(lg[:], decays.partition_broadcast(P)).then_inc(decay_in, 16)

            def load_cs(s, par):
                wait_apart(sp, rotated, 4 * (s - 1))
                sp.dma_start(cs[:, par], rope[f.tile(s)]).then_inc(cs_in[par], 16)

            for par in range(2):
                f.load_x(sp, par, par)
                load_cs(par, par)
            f.load_w(sp)

            def store_late(s):
                wait_apart(sp, kv_out_made, s + 1)
                sp.dma_start(kv_d[f.tile(s)], kv_out[:]).then_inc(kv_stored, 16)
                wait_apart(sp, part_made, s + 1)
                sp.dma_start(part_d[f.tile(s)], part[:]).then_inc(part_stored, 16)

            def body(i, last):
                for par in range(2):
                    s = 2 * i + par
                    if not last:
                        f.load_x(sp, s + 2, par)
                    if not (isinstance(i, int) and s == 0):
                        store_late(s - 1)
                    wait_apart(sp, q_decayed, 2 * s + 1)
                    sp.dma_start(qf_d[f.tile(s)], q_dec[:, 0]).then_inc(qf_stored, 16)
                    wait_apart(sp, gate_made, s + 1)
                    sp.dma_start(gate_d[f.tile(s)], gate).then_inc(gate_stored, 16)
                    if not last:
                        load_cs(s + 2, par)

            over_pairs(sp, body)
            store_late(TILES - 1)
            for q in (kv_stored, part_stored, qf_stored, gate_stored):
                wait_apart(sp, q, 16 * TILES)

        @block.gpsimd
        def _(pool):
            nc.gpsimd.iota(within[:], pattern=[[0, RH], [1, C]], base=0, channel_multiplier=-1,
                           allow_small_or_imprecise_dtypes=True).then_inc(pos_made, 1)
            nc.gpsimd.iota(q_scale[:, 0], pattern=[[0, RH], [1, C]], base=1, channel_multiplier=0,
                           allow_small_or_imprecise_dtypes=True).then_inc(pos_made, 1)
            nc.gpsimd.iota(q_scale[:, 1], pattern=[[0, RH], [-1, C]], base=C, channel_multiplier=0,
                           allow_small_or_imprecise_dtypes=True).then_inc(pos_made, 1)
            nc.gpsimd.iota(pos[:, 0:1], pattern=[[0, 1]], base=C - 1, channel_multiplier=-1,
                           allow_small_or_imprecise_dtypes=True).then_inc(pos_made, 1)
            nc.gpsimd.iota(pos[:, 1:2], pattern=[[0, 1]], base=0, channel_multiplier=1,
                           allow_small_or_imprecise_dtypes=True).then_inc(pos_made, 1)
            f.rstd_x(pool, 0)
            f.place_mod(pool, 0, 0)
            f.rstd_x(pool, 1)

            def body(i, last):
                for par in range(2):
                    s = 2 * i + par
                    if not (last and par == 1):
                        f.place_mod(pool, s + 1, 1 - par)
                    if not last:
                        f.rstd_x(pool, s + 2)

            over_pairs(pool, body)

        @block.scalar
        def _(act):
            act.wait_ge(decay_in, 16)
            nc.scalar.activation(lg[:], lg[:], ACT.Exp).then_inc(lg_made, 1)
            act.wait_ge(expo_made, 12)
            nc.scalar.activation(within[:], within[:], ACT.Exp).then_inc(const_made, 1)
            nc.scalar.activation(q_scale[:], q_scale[:], ACT.Exp).then_inc(const_made, 1)
            nc.scalar.activation(k_scale[:], k_scale[:], ACT.Exp).then_inc(const_made, 1)
            nc.scalar.activation(chunk_decay[:], lg[:], ACT.Exp, scale=float(C)).then_inc(const_made, 1)
            f.square_x(act, 0, 0, 0)
            f.modulate(act, 0, 0)
            f.square_x(act, 1, 1, 0)
            for k in range(KB):
                f.split_w_hi(act, k)

            def late(s):
                act.wait_ge(kv_f_done, s + 1)
                at_least(act, kv_stored, 16 * s)
                nc.scalar.activation(kv_out[:], kv_bank[:], ACT.Copy).then_inc(kv_out_made, 1)
                act.wait_ge(part_done, s + 1)
                at_least(act, part_stored, 16 * s)
                nc.scalar.activation(part[:], so_bank[:], ACT.Copy).then_inc(part_made, 1)

            def body(i, last):
                for par in range(2):
                    s = 2 * i + par
                    for a in range(2):
                        act.wait_ge(f.projected, 4 * s + a + 1)
                        at_least(act, rotated, 4 * s + 2 * a - 2)
                        nc.scalar.activation(raw[:, a], proj[a][:], ACT.Copy,
                                             scale=(1.0 if a == 0 else RHD ** -0.5)).then_inc(raw_made, 1)
                    if not (last and par == 1):
                        f.modulate(act, s + 1, 1 - par)
                    if not (isinstance(i, int) and s == 0):
                        late(s - 1)
                    act.wait_ge(f.projected, 4 * s + 3)
                    nc.scalar.activation(v, proj[0][:], ACT.Copy).then_inc(v_made, 1)
                    act.wait_ge(qk_turned, 2 * s + 1)
                    at_least(act, q_decayed, 2 * s)
                    nc.scalar.activation(turned[:, 0], qk_banks[0][:].rearrange("p h n -> p (h n)"),
                                         ACT.Copy).then_inc(turned_out, 1)
                    if not last:
                        f.square_x(act, s + 2, par, i + 1)
                    act.wait_ge(f.projected, 4 * s + 4)
                    at_least(act, gate_stored, 16 * s)
                    nc.scalar.activation(gate, proj[1][:], ACT.Silu).then_inc(gate_made, 1)
                    act.wait_ge(qk_turned, 2 * s + 2)
                    nc.scalar.activation(turned[:, 1], qk_banks[1][:].rearrange("p h n -> p (h n)"),
                                         ACT.Copy).then_inc(turned_out, 1)

            over_pairs(act, body)
            late(TILES - 1)

        @block.vector
        def _(dve):
            dve.wait_ge(lg_made, 1)
            nc.vector.tensor_scalar(lg[:], lg[:], -1.0, None, ALU.mult).then_inc(expo_made, 1)
            dve.wait_ge(pos_made, 5)
            dve.wait_ge(expo_made, 1)
            for h in range(RH):
                nc.vector.tensor_scalar(weighted[:, h * C:(h + 1) * C], within[:, h, :], 0.0, lg[:, h:h + 1],
                                        ALU.max, ALU.mult)
                last = nc.vector.tensor_scalar(part[:, h * C:(h + 1) * C], within[:, h, :], 0.0,
                                               lg[:, RH + h:RH + h + 1], ALU.min, ALU.mult)
            last.then_inc(expo_made, 1)
            dve.wait_ge(expo_made, 2)
            nc.vector.tensor_tensor(within[:].rearrange("p h n -> p (h n)"), weighted[:], part[:],
                                    ALU.subtract).then_inc(expo_made, 1)
            for a in range(2):
                for h in range(RH):
                    nc.vector.tensor_scalar(q_scale[:, a, h, :], q_scale[:, a, h, :], lg[:, a * RH + h:a * RH + h + 1],
                                            None, ALU.mult).then_inc(expo_made, 1)
                last = nc.vector.tensor_scalar(k_scale[:, a * RH:(a + 1) * RH], lg[:, a * RH:(a + 1) * RH],
                                               pos[:, a:a + 1], None, ALU.mult)
            last.then_inc(expo_made, 1)
            nc.vector.memset(state[:, 1], 0.0).then_inc(state_made, 1)

            f.mean_x(dve, 0)
            f.norm_x(dve, 0, 0)
            f.split_h(dve, 0, 0)
            f.mean_x(dve, 1)
            f.norm_x(dve, 1, 1)
            for k in range(KB):
                f.split_w_lo(dve, k)
            dve.wait_ge(const_made, 4)

            def late(s, par):
                dve.wait_ge(scored, s + 1)
                at_least(dve, part_done, s)
                nc.vector.tensor_tensor(weighted[:], so_bank[:], within[:].rearrange("p h n -> p (h n)"),
                                        ALU.mult).then_inc(weighted_made, 1)
                dve.wait_ge(state_made, s + 1)
                at_least(dve, part_done, s)
                if isinstance(s, int) and s == T_PROMPT // P - 1:
                    nc.vector.memset(state[:, par, 0:HALF // 2], 0.0).then_inc(state_decayed, 1)
                    dve.wait_ge(state_decayed, s + 1)
                    dve.wait_ge(kv_b_done, s + 1)
                    nc.vector.memset(state[:, par, HALF // 2:], 0.0).then_inc(state_made, 1)
                    return
                for h in range(RH):
                    last = nc.vector.tensor_scalar(state[:, par, h * RHD:(h + 1) * RHD],
                                                   state[:, 1 - par, h * RHD:(h + 1) * RHD],
                                                   chunk_decay[:, RH + h:RH + h + 1], None, ALU.mult)
                last.then_inc(state_decayed, 1)
                dve.wait_ge(state_decayed, s + 1)
                dve.wait_ge(kv_b_done, s + 1)
                nc.vector.tensor_tensor(state[:, par], state[:, par], kv_bank[:], ALU.add).then_inc(state_made, 1)

            def rotate(s, par, a, i):
                n = 2 * s + a
                dve.wait_ge(raw_made, n + 1)
                dve.wait_ge(cs_in[par], 16 * (i + 1))
                at_least(dve, qk_turned, n - 1)
                src = raw[:, a].rearrange("p (h x n) -> p x h n", h=RH, x=2)
                dst = rot[:, a].rearrange("p (h x n) -> p x h n", h=RH, x=2)
                prod = [product[:, j].rearrange("p (h n) -> p h n", h=RH) for j in range(2)]
                trig = [cs[:, par, j:j + 1, :].to_broadcast([P, RH, 64]) for j in range(2)]
                for x, (first, second, op) in enumerate([(0, 1, ALU.subtract), (1, 0, ALU.add)]):
                    at_least(dve, rotated, 2 * n + x)
                    nc.vector.tensor_tensor(prod[0], src[:, 0], trig[first], ALU.mult)
                    nc.vector.tensor_tensor(prod[1], src[:, 1], trig[second], ALU.mult).then_inc(multiplied, 1)
                    dve.wait_ge(multiplied, 2 * n + x + 1)
                    nc.vector.tensor_tensor(dst[:, x], prod[0], prod[1], op).then_inc(rotated, 1)

            def body(i, last):
                for par in range(2):
                    s = 2 * i + par
                    if not (isinstance(i, int) and s == 0):
                        late(s - 1, 1 - par)
                    rotate(s, par, 0, i)
                    rotate(s, par, 1, i)
                    if not (last and par == 1):
                        f.split_h(dve, s + 1, 1 - par)
                    dve.wait_ge(rotated, 4 * s + 4)
                    for a, done in enumerate((kv_f_done, kv_b_done)):
                        at_least(dve, done, s)
                        k = nc.vector.tensor_tensor(heads(k_dec[:, a]), heads(rot[:, 1]),
                                                    k_scale[:, a * RH:(a + 1) * RH].unsqueeze(2)
                                                    .to_broadcast([P, RH, RHD]), ALU.mult)
                    k.then_inc(k_decayed, 1)
                    if not last:
                        f.mean_x(dve, s + 2)
                        f.norm_x(dve, s + 2, par)
                    dve.wait_ge(turned_out, 2 * s + 1)
                    at_least(dve, qf_stored, 16 * s)
                    at_least(dve, part_done, s)
                    for a in range(2):
                        nc.vector.tensor_tensor(q_dec[:, a], turned[:, 0], q_scale[:, a].rearrange("p h n -> p (h n)"),
                                                ALU.mult).then_inc(q_decayed, 1)

            seam = T_PROMPT // P
            body(0, False)
            with dve.Fori(1, seam // 2) as i:
                body(i, False)
            body(seam // 2, False)
            with dve.Fori(seam // 2 + 1, PAIRS - 1) as i:
                body(i, False)
            body(PAIRS - 1, True)
            late(TILES - 1, 1)

        @block.tensor
        def _(pe):
            f.turn_x(pe, 0)
            pe.wait_ge(const_made, 4)

            def turn_heads(s, a):
                pe.wait_ge(rotated, 4 * s + 2 * a + 2)
                at_least(pe, turned_out, 2 * s + a - 1)
                for h in range(RH):
                    last = nc.tensor.transpose(qk_banks[a][:, h, :], rot[:, a, h * RHD:(h + 1) * RHD], ident[:])
                last.then_inc(qk_turned, 1)

            def scores(s):
                pe.wait_ge(turned_out, 2 * s + 2)
                at_least(pe, part_made, s)
                for h in range(RH):
                    cols = slice(h * C, (h + 1) * C)
                    last = nc.tensor.matmul(so_bank[:, cols], turned[:, 1, cols], turned[:, 0, cols],
                                            start=True, stop=True)
                last.then_inc(scored, 1)

            def key_values(s, a, done):
                pe.wait_ge(k_decayed, s + 1)
                if a == 1:
                    pe.wait_ge(v_made, s + 1)
                    at_least(pe, kv_out_made, s)
                else:
                    pe.wait_ge(state_made, s + 2)
                for h in range(RH):
                    cols = slice(h * RHD, (h + 1) * RHD)
                    last = nc.tensor.matmul(kv_bank[:, cols], k_dec[:, a, cols], v[:, cols], start=True, stop=True)
                last.then_inc(done, 1)

            def outputs(s, par):
                pe.wait_ge(weighted_made, s + 1)
                pe.wait_ge(q_decayed, 2 * s + 2)
                pe.wait_ge(state_made, s + 1)
                for h in range(RH):
                    cols = slice(h * C, (h + 1) * C)
                    nc.tensor.matmul(so_bank[:, cols], weighted[:, cols], v[:, cols], start=True, stop=False)
                    last = nc.tensor.matmul(so_bank[:, cols], q_dec[:, 1, cols], state[:, 1 - par, cols],
                                            start=False, stop=True)
                last.then_inc(part_done, 1)

            def body(i, last):
                for par in range(2):
                    s = 2 * i + par
                    late = not (isinstance(i, int) and s == 0)
                    at_least(pe, v_made, s)
                    f.project(pe, s, par, 0, proj[0][:])
                    if late:
                        scores(s - 1)
                        key_values(s - 1, 1, kv_b_done)
                    at_least(pe, gate_made, s)
                    f.project(pe, s, par, 1, proj[1][:])
                    if not (last and par == 1):
                        f.turn_x(pe, s + 1)
                    if late:
                        key_values(s - 1, 0, kv_f_done)
                        outputs(s - 1, 1 - par)
                    pe.wait_ge(raw_made, 2 * s + 1)
                    f.project(pe, s, par, 2, proj[0][:])
                    turn_heads(s, 0)
                    pe.wait_ge(raw_made, 2 * s + 2)
                    f.project(pe, s, par, 3, proj[1][:])
                    turn_heads(s, 1)

            over_pairs(pe, body)
            s = TILES - 1
            scores(s)
            key_values(s, 1, kv_b_done)
            key_values(s, 0, kv_f_done)
            outputs(s, 1)


def attention_stage(nc, qT_d, kT_d, vg_d, bias_rows, ident, masked_d, w_out, na_d):
    with ExitStack() as ctx:
        sb = lambda n, s, d=F32: ctx.enter_context(nc.sbuf_tensor(n, s, d))
        sem = lambda n: ctx.enter_context(nc.semaphore(n))
        tables = sb("bias_tables", [P, 2, 3, GH, KEYS])
        k_strip = sb("k_strip", [P, 2, GH, KR * W], F32R)
        q_strip = sb("q_strip", [P, 2, GH, QR * W])
        q_block = sb("q_block", [P, 2, 2, GH, P], F32R)
        v_strip = sb("v_strip", [P, 2, W // 8, GW])
        out = sb("na_out", [P, 2, COLS, GW])
        biased = sb("biased", [P, 4, KEYS])
        probs = sb("probs", [P, 4, KEYS])
        probs_T = sb("probs_T", [P, 2, 4, P])
        neg_max = sb("neg_max", [P, 4])
        sums = sb("sums", [P, 4, GH])
        inverse = sb("inverse", [P, 2, GH])
        s_banks = [ctx.enter_context(nc.psum_tensor(f"s_bank{j}", [P, 512], F32)) for j in range(4)]
        t_banks = [ctx.enter_context(nc.psum_tensor(f"t_bank{j}", [P, 4, P], F32)) for j in range(2)]
        o_banks = [ctx.enter_context(nc.psum_tensor(f"o_bank{j}", [P, 512], F32)) for j in range(2)]
        wait_apart = apart(sem("n_passed"))
        cleared, masked_placed = [sem("cleared0"), sem("cleared1")], sem("masked_placed")
        tables_in = [sem(f"tables_in{n}") for n in range(6)]
        strip_in, v_in = [sem("strip_in0"), sem("strip_in1")], [sem("v_in0"), sem("v_in1")]
        q_placed, scored, biased_made, exped = sem("q_placed"), sem("na_scored"), sem("biased_made"), sem("exped")
        probs_turned, turned_act, turned_dve = sem("probs_turned"), sem("turned_act"), sem("turned_dve")
        valued, inverted, scaled = sem("valued"), sem("inverted"), sem("scaled")
        out_stored = [sem("out_stored0"), sem("out_stored1")]
        block = ctx.enter_context(nc.Block())

        G_BODIES = len(STRIPS) // 2
        BODIES = NH // GH * G_BODIES
        UNITS = 2 * COLS
        STEPS = UNITS * GH
        HALF_STEPS = STEPS // 2
        GROUP_KEYS = KR * 8
        FILLS = [(g, edge) for g in range(NH // GH) for edge in ("top", "inner", "bottom")]

        @block.sync
        def _(sp):
            def rows_of(b, half):
                g = b // G_BODIES if isinstance(b, int) else b_group
                strip = 2 * (b - g * G_BODIES) + half
                if isinstance(b, int) and b % G_BODIES in (0, G_BODIES - 1):
                    return g, *STRIPS[strip]
                q0, k0 = STRIPS[2]
                return g, q0 + QR * (strip - 2), k0 + QR * (strip - 2)

            def load_pass(b, half):
                g, q0, k0 = rows_of(b, half)
                heads = slice(g * GH, (g + 1) * GH)
                wait_apart(sp, scored, STEPS * b + HALF_STEPS * (half - 1))
                sp.dma_start(k_strip[:, half].bitcast(F32), kT_d[:, heads, bass.ds(k0 * W, KR * W)]).then_inc(strip_in[half], 16)
                for rows in (slice(0, NHD), slice(NHD, P)):
                    sp.dma_start(q_strip[rows, half],
                                 qT_d[:, heads, bass.ds(q0 * W, QR * W)]).then_inc(strip_in[half], 16)
                wait_apart(sp, valued, STEPS * b + HALF_STEPS * (half - 1))
                for r in range(KR):
                    sp.dma_start(v_strip[r * 8:(r + 1) * 8, half],
                                 vg_rows[k0 + r, :, g * GW:(g + 1) * GW].rearrange("(c w) n -> w c n", w=8)
                                 ).then_inc(v_in[half], 16)

            def store_pass(b, half):
                g, q0, _ = rows_of(b, half)
                wait_apart(sp, scaled, UNITS * b + COLS * (half + 1))
                for r in range(QR):
                    sp.dma_start(na_rows[q0 + r, :, g * GW:(g + 1) * GW].rearrange("(c w) n -> w c n", w=QC),
                                 out[r * QC:(r + 1) * QC, half]).then_inc(out_stored[half], 16)

            def fill(n):
                g, edge = FILLS[n]
                for r in range(QR):
                    if edge == "top":
                        key0, dr0 = max(r - 4, 0), max(r - 4, 0) - r + WIN_H - 1
                    elif edge == "inner":
                        key0, dr0 = r, 3
                    else:
                        key0, dr0 = min(r - 4, 0) + KR - QR, min(r - 4, 0) - r + WIN_H - 1
                    for k in range(3):
                        rows = bias_rows[:, k].rearrange("c (h r) x -> c h (r x)", h=NH)
                        sp.dma_start(tables[r * QC:(r + 1) * QC, n % 2, k, :, key0 * KC:(key0 + WIN_H) * KC],
                                     rows[:, g * GH:(g + 1) * GH, dr0 * KC:(dr0 + WIN_H) * KC]
                                     ).then_inc(tables_in[n], 16)

            def refill(n, b):
                wait_apart(sp, biased_made, STEPS * (b + 1))
                sp.dma_start(tables[:, n % 2], masked_d).then_inc(masked_placed, 16)
                wait_apart(sp, masked_placed, 16 * n)
                fill(n)

            def body(b):
                for half in range(2):
                    load_pass(b, half)
                    store_pass(b - 1, half)

            vg_rows = vg_d.rearrange("t (r w) n -> (t r) w n", w=W)
            na_rows = na_d.rearrange("t (r w) n -> (t r) w n", w=W)
            load_pass(0, 0)
            wait_apart(sp, cleared[0], 1)
            fill(0)
            load_pass(0, 1)
            wait_apart(sp, cleared[1], 1)
            sp.dma_start(masked_d, tables[:, 1]).then_inc(masked_placed, 16)
            wait_apart(sp, masked_placed, 16)
            fill(1)
            for g in range(NH // GH):
                b0, b_group = g * G_BODIES, g
                if g > 0:
                    body(b0)
                    refill(3 * g + 1, b0 - 1)
                body(b0 + 1)
                refill(3 * g + 2, b0)
                with sp.Fori(b0 + 2, b0 + G_BODIES - 1) as b:
                    body(b)
                body(b0 + G_BODIES - 1)
                if g == 0:
                    refill(3, b0 + G_BODIES - 2)
            for half in range(2):
                store_pass(BODIES - 1, half)
            for half in range(2):
                wait_apart(sp, out_stored[half], 16 * QR * BODIES)

        @block.gpsimd
        def _(pool):
            def place_q(b, u):
                half, n = u // COLS, u % COLS
                if n == 0:
                    wait_apart(pool, strip_in[half], 48 * (b + 1))
                wait_apart(pool, scored, STEPS * b + GH * (u - 1))
                src = q_strip[:, half].rearrange("p h (r w) -> p h r w", r=QR)[:, :, :, QC * n:QC * (n + 1)]
                hi, lo = (q_block[:, u % 2, j].rearrange("p h (r w) -> p h r w", r=QR) for j in range(2))
                nc.gpsimd.tensor_copy(hi, src).then_inc(q_placed, 1)
                wait_apart(pool, q_placed, 2 * (UNITS * b + u) + 1)
                nc.gpsimd.tensor_tensor(lo, src, hi.bitcast(F32), ALU.subtract).then_inc(q_placed, 1)

            def body(b):
                for u in range(UNITS):
                    place_q(b, u)

            place_q(0, 0)
            place_q(0, 1)
            nc.gpsimd.memset(tables[:, 1], MASKED).then_inc(cleared[1], 1)
            for u in range(2, UNITS):
                place_q(0, u)
            with pool.Fori(1, BODIES - 4) as b:
                body(b)
            for k in range(KB // 2):
                w_out.load(pool, k)
            body(BODIES - 4)
            for k in range(KB // 2, KB):
                w_out.load(pool, k)
            with pool.Fori(BODIES - 3, BODIES) as b:
                body(b)

        @block.scalar
        def _(act):
            def exponentiate(b, j):
                act.wait_ge(biased_made, STEPS * b + j + 1)
                at_least(act, probs_turned, STEPS * b + j - 3)
                if j % GH == 0:
                    at_least(act, inverted, UNITS * b + j // GH - 3)
                nc.scalar.activation(probs[:, j % 4].rearrange("p (c r w) -> p c r w", r=KR, w=8),
                                     biased[:, j % 4].rearrange("p (r c w) -> p c r w", r=KR, w=8), ACT.Exp, scale=-1.0,
                                     bias=neg_max[:, j % 4:j % 4 + 1],
                                     accum_out=sums[:, j // GH % 4, j % GH:j % GH + 1]).then_inc(exped, 1)

            def take_out(b, j):
                act.wait_ge(probs_turned, STEPS * b + j + 1)
                at_least(act, valued, STEPS * b + j - 1)
                nc.scalar.activation(probs_T[0:GROUP_KEYS, 0].rearrange("p c q -> p (c q)"),
                                     t_banks[0][0:GROUP_KEYS].rearrange("p c q -> p (c q)"),
                                     ACT.Copy).then_inc(turned_act, 1)

            def body(b, first=False, last=False):
                for k in range(STEPS):
                    if k % 2 == 0 and not (first and k < 2):
                        take_out(b, k - 2)
                    exponentiate(b, k)
                    if last and k % (STEPS // KB) == 1:
                        w_out.make_hi(act, k // (STEPS // KB))

            body(0, first=True)
            with act.Fori(1, BODIES - 1) as b:
                body(b)
            body(BODIES - 1, last=True)
            take_out(BODIES, -2)

        @block.vector
        def _(dve):
            def add_bias(b, slot, j):
                at_least(dve, exped, STEPS * b + j - 3)
                wait_apart(dve, scored, STEPS * b + j + 1)
                nc.vector.tensor_tensor_reduce(out=biased[:, j % 4, :], in0=s_banks[j % 4][:, 0:KEYS],
                                               in1=tables[:, slot, KIND[j // GH % COLS], j % GH, :], scale=1.0,
                                               scalar=3.0e38, op0=ALU.add, op1=ALU.min,
                                               accum_out=neg_max[:, j % 4:j % 4 + 1]).then_inc(biased_made, 1)

            def take_out(b, j):
                dve.wait_ge(probs_turned, STEPS * b + j + 1)
                at_least(dve, valued, STEPS * b + j - 1)
                nc.vector.tensor_copy(probs_T[0:GROUP_KEYS, 1], t_banks[1][0:GROUP_KEYS]).then_inc(turned_dve, 1)

            def scale_unit(b, u):
                n = UNITS * b + u + 1
                dve.wait_ge(valued, GH * n)
                nc.vector.reciprocal(inverse[:, u % 2, :], sums[:, u % 4, :]).then_inc(inverted, 1)
                dve.wait_ge(inverted, n)
                if u % COLS == 0:
                    at_least(dve, out_stored[u // COLS], 16 * QR * b)
                nc.vector.tensor_tensor(out[:, u // COLS % 2, u % COLS].rearrange("p (h d) -> p h d", h=GH),
                                        o_banks[u % 2][:, 0:GW].rearrange("p (h d) -> p h d", h=GH),
                                        inverse[:, u % 2, :].unsqueeze(2).to_broadcast([P, GH, NHD]),
                                        ALU.mult).then_inc(scaled, 1)

            def body(b, slot, first=False, last=False):
                for k in range(STEPS):
                    if k % 2 == 1 and not (first and k < 2):
                        take_out(b, k - 2)
                    add_bias(b, slot, k)
                    if k % GH == 0 and not (first and k < 2 * GH):
                        scale_unit(b, k // GH - 2)
                    if last and k % (STEPS // KB) == 2:
                        w_out.make_lo(dve, k // (STEPS // KB))

            nc.vector.memset(tables[:, 0], MASKED).then_inc(cleared[0], 1)
            for g in range(NH // GH):
                b0, n0 = g * G_BODIES, 3 * g
                dve.wait_ge(tables_in[n0], 48 * QR)
                body(b0, n0 % 2, g == 0)
                dve.wait_ge(tables_in[n0 + 1], 48 * QR)
                with dve.Fori(b0 + 1, b0 + G_BODIES - 1) as b:
                    body(b, (n0 + 1) % 2)
                dve.wait_ge(tables_in[n0 + 2], 48 * QR)
                body(b0 + G_BODIES - 1, n0 % 2, last=g > 0)
            take_out(BODIES, -1)
            scale_unit(BODIES, -2)
            scale_unit(BODIES, -1)

        @block.tensor
        def _(pe):
            def score(b, j):
                u, h = j // GH, j % GH
                if h == 0:
                    pe.wait_ge(q_placed, 2 * (UNITS * b + u + 1))
                    if u % COLS == 0:
                        pe.wait_ge(strip_in[u // COLS], 48 * (b + 1))
                at_least(pe, biased_made, STEPS * b + j - 3)
                keys = k_strip[:, u // COLS, h, :].rearrange("p (r w) -> p r w", w=W)
                k0 = K0[u % COLS]
                for part in range(2):
                    last = nc.tensor.matmul(s_banks[j % 4][:, 0:KEYS], q_block[:, u % 2, part, h, :],
                                            keys[:, :, k0:k0 + KC], start=(part == 0), stop=(part == 1))
                last.then_inc(scored, 1)

            def turn(b, j):
                pe.wait_ge(exped, STEPS * b + j + 1)
                at_least(pe, turned_act if j % 2 == 0 else turned_dve, STEPS // 2 * b + j // 2)
                for c in range(4):
                    last = nc.tensor.transpose(t_banks[j % 2][0:GROUP_KEYS, c, :],
                                               probs[:, j % 4, c * GROUP_KEYS:(c + 1) * GROUP_KEYS], ident[:])
                last.then_inc(probs_turned, 1)

            def value(b, j):
                u, h = j // GH, j % GH
                pe.wait_ge(turned_act if j % 2 == 0 else turned_dve, STEPS // 2 * b + j // 2 + 1)
                if h == 0:
                    if u % COLS == 0:
                        pe.wait_ge(v_in[u // COLS], 16 * KR * (b + 1))
                    at_least(pe, scaled, UNITS * b + u - 1)
                cols = slice(h * NHD, (h + 1) * NHD)
                for c in range(4):
                    last = nc.tensor.matmul(o_banks[u % 2][:, cols], probs_T[0:GROUP_KEYS, j % 2, c, :],
                                            v_strip[0:GROUP_KEYS, u // COLS, K0[u % COLS] // 8 + c, cols],
                                            start=(c == 0), stop=(c == 3))
                last.then_inc(valued, 1)

            for j in range(3):
                score(0, j)
            turn(0, 0)

            def body(b, last):
                for k in range(STEPS):
                    if k + 3 < STEPS:
                        score(b, k + 3)
                    elif not last:
                        score(b + 1, k + 3 - STEPS)
                    if k + 1 < STEPS:
                        turn(b, k + 1)
                    elif not last:
                        turn(b + 1, 0)
                    value(b, k)

            body(0, False)
            with pe.Fori(1, BODIES - 1) as b:
                body(b, False)
            body(BODIES - 1, True)


def out_stage(nc, x_tiles, w_out, ret_gain, gate_rows, decays, na_d, vg_d, part_d, qf_d, kv_d, gate_d, ident, exps, y_tiles):
    with ExitStack() as ctx:
        sb = lambda n, s, d=F32: ctx.enter_context(nc.sbuf_tensor(f"o_{n}", s, d))
        sem = lambda n: ctx.enter_context(nc.semaphore(f"o_{n}"))
        lg = sb("lg", [P, 2 * RH])
        chunk_decay = sb("chunk_decay", [P, RH])
        gain = sb("gain", [P, HALF])
        out_gate = sb("out_gate", [P, 2, D])
        x = sb("x", [P, 2, D])
        part, qf, kv, gate, na_gate = (sb(n, [P, 2, HALF]) for n in ("part", "qf", "kv", "gate", "na_gate"))
        mix = sb("mix", [P, 2, D])
        state = sb("state_f", [P, 2, HALF])
        total = sb("total", [P, HALF])
        squares = sb("squares", [P, HALF])
        stat = sb("stat", [P, 3, RH])
        m_hi, m_lo = sb("m_hi", [P, 2, KB, P], F32R), sb("m_lo", [P, 2, KB, P], F32R)
        y = sb("y", [P, 2, D])
        cross_bank = ctx.enter_context(nc.psum_tensor("o_cross", [P, 512], F32))
        turn_banks = [ctx.enter_context(nc.psum_tensor(f"o_turn{j}", [P, 4, P], F32)) for j in range(2)]
        banks = [ctx.enter_context(nc.psum_tensor(f"o_proj{j}", [P, 512], F32)) for j in range(4)]
        wait_apart = apart(sem("passed"))
        const_in, lg_made, decay_made = sem("const_in"), sem("lg_made"), sem("decay_made")
        tile_in, x_in = [sem("tile_in0"), sem("tile_in1")], [sem("x_in0"), sem("x_in1")]
        state_made, crossed = sem("state_made"), sem("crossed")
        totalled, squared, summed, meaned, rstd_made = sem("totalled"), sem("squared"), sem("summed"), sem("meaned"), sem("rstd")
        gained, mixed, mix_turned = sem("gained"), sem("mixed"), sem("mix_turned")
        hi_made, lo_made, projected, scaled, added = sem("hi_made"), sem("lo_made"), sem("projected"), sem("scaled"), sem("added")
        y_stored = [sem("y_stored0"), sem("y_stored1")]
        block = ctx.enter_context(nc.Block())

        @block.sync
        def _(sp):
            def load_tile(t, par):
                wait_apart(sp, mixed, t - 1)
                wait_apart(sp, mix_turned, t - 1)
                for dst, src in ((kv, kv_d), (qf, qf_d), (part, part_d), (gate, gate_d)):
                    sp.dma_start(dst[:, par], src[t]).then_inc(tile_in[par], 16)
                sp.dma_start(mix[:, par, 0:HALF], na_d[t]).then_inc(tile_in[par], 16)
                sp.dma_start(na_gate[:, par], vg_d[t][:, HALF:D]).then_inc(tile_in[par], 16)

            def load_x(t, par):
                wait_apart(sp, added, t - 1)
                sp.dma_start(x[:, par], x_tiles[t]).then_inc(x_in[par], 16)

            def store_y(t, par):
                wait_apart(sp, added, t + 1)
                sp.dma_start(y_tiles[t], y[:, par]).then_inc(y_stored[par], 16)

            sp.dma_start(lg[:], decays.partition_broadcast(P)).then_inc(const_in, 16)
            sp.dma_start(gain[:], ret_gain.partition_broadcast(P)).then_inc(const_in, 16)
            for s in range(2):
                sp.dma_start(out_gate[:, s], gate_rows[s].partition_broadcast(P)).then_inc(const_in, 16)
            load_tile(0, 0)
            load_tile(1, 1)
            load_x(0, 0)
            load_x(1, 1)
            load_tile(2, 0)

            def body(i, tiles_left):
                for par in range(2):
                    t = 2 * i + par
                    if tiles_left > par + 3:
                        load_tile(t + 3, 1 - par)
                    store_y(t, par)
                    if tiles_left > par + 2:
                        load_x(t + 2, par)

            body(0, TILES)
            with sp.Fori(1, PAIRS - 2) as i:
                body(i, TILES)
            body(PAIRS - 2, 4)
            body(PAIRS - 1, 2)
            for par in range(2):
                wait_apart(sp, y_stored[par], 16 * PAIRS)

        @block.gpsimd
        def _(pool):
            def gate_and_rstd(t, par, i):
                wait_apart(pool, tile_in[par], 96 * (i + 1))
                nc.gpsimd.tensor_tensor(gate[:, par], gate[:, par], gain[:], ALU.mult)
                nc.gpsimd.tensor_tensor(mix[:, par, 0:HALF], mix[:, par, 0:HALF], na_gate[:, par],
                                        ALU.mult).then_inc(gained, 1)
                wait_apart(pool, meaned, t + 1)
                nc.gpsimd.tensor_tensor(stat[:, 2, :], stat[:, 1, :], exps[:, 0:RH], ALU.pow).then_inc(rstd_made, 1)

            wait_apart(pool, const_in, 64)

            def body(i, last):
                for par in range(2):
                    gate_and_rstd(2 * i + par, par, i)

            over_pairs(pool, body)

        @block.scalar
        def _(act):
            act.wait_ge(const_in, 64)
            nc.scalar.activation(lg[:], lg[:], ACT.Exp).then_inc(lg_made, 1)
            act.wait_ge(lg_made, 2)
            nc.scalar.activation(chunk_decay[:], lg[:, 0:RH], ACT.Exp, scale=float(C)).then_inc(decay_made, 1)
            def square(t):
                act.wait_ge(totalled, t + 1)
                at_least(act, summed, t)
                nc.scalar.activation(squares[:], total[:], ACT.Square).then_inc(squared, 1)

            def high(t, par):
                act.wait_ge(mix_turned, t + 1)
                at_least(act, projected, 2 * (t - 1))
                for j in range(2):
                    last = nc.scalar.activation(m_hi[:, par, 4 * j:4 * j + 4].rearrange("p k t -> p (k t)"),
                                                turn_banks[j][:].rearrange("p k t -> p (k t)"), ACT.Copy)
                last.then_inc(hi_made, 1)

            square(0)
            square(1)
            high(0, 0)

            def body(i, last):
                for par in range(2):
                    t = 2 * i + par
                    if not (last and par == 1):
                        high(t + 1, 1 - par)
                    if not last:
                        square(t + 2)

            over_pairs(act, body)

        @block.vector
        def _(dve):
            dve.wait_ge(lg_made, 1)
            nc.vector.tensor_scalar(lg[:], lg[:], -1.0, None, ALU.mult).then_inc(lg_made, 1)
            nc.vector.memset(state[:, 1], 0.0).then_inc(state_made, 1)

            def carry(t, par, i):
                dve.wait_ge(tile_in[par], 96 * (i + 1))
                dve.wait_ge(state_made, t + 1)
                at_least(dve, crossed, t)
                if isinstance(t, int) and t == T_SAMPLE // P - 1:
                    nc.vector.memset(state[:, par], 0.0).then_inc(state_made, 1)
                    return
                for h in range(RH):
                    cols = slice(h * RHD, (h + 1) * RHD)
                    last = nc.vector.scalar_tensor_tensor(out=state[:, par, cols], in0=state[:, 1 - par, cols],
                                                          scalar=chunk_decay[:, h:h + 1], in1=kv[:, par, cols],
                                                          op0=ALU.mult, op1=ALU.add)
                last.then_inc(state_made, 1)

            def total_up(t, par):
                dve.wait_ge(crossed, t + 1)
                at_least(dve, mixed, t)
                nc.vector.tensor_tensor(total[:], cross_bank[:], part[:, par], ALU.add).then_inc(totalled, 1)

            def norm(t, par):
                dve.wait_ge(squared, t + 1)
                nc.vector.tensor_reduce(stat[:, 0, :], squares[:].rearrange("p (h d) -> p h d", h=RH), AX.X,
                                        ALU.add).then_inc(summed, 1)
                dve.wait_ge(summed, t + 1)
                nc.vector.tensor_scalar(stat[:, 1, :], stat[:, 0, :], 1.0 / RHD, EPS, ALU.mult,
                                        ALU.add).then_inc(meaned, 1)

            def mix_up(t, par):
                dve.wait_ge(rstd_made, t + 1)
                at_least(dve, mix_turned, t - 1)
                dve.wait_ge(gained, t + 1)
                for h in range(RH):
                    cols = slice(h * RHD, (h + 1) * RHD)
                    last = nc.vector.scalar_tensor_tensor(out=mix[:, par, HALF + h * RHD:HALF + (h + 1) * RHD],
                                                          in0=total[:, cols], scalar=stat[:, 2, h:h + 1],
                                                          in1=gate[:, par, cols], op0=ALU.mult, op1=ALU.mult)
                last.then_inc(mixed, 1)

            def low(t, par):
                dve.wait_ge(hi_made, t + 1)
                for j in range(2):
                    hi = m_hi[:, par, 4 * j:4 * j + 4].bitcast(F32)
                    last = nc.vector.tensor_tensor(m_lo[:, par, 4 * j:4 * j + 4], turn_banks[j][:], hi, ALU.subtract)
                last.then_inc(lo_made, 1)

            def scale(t, par, n, seq, i):
                dve.wait_ge(projected, 2 * t + n + 1)
                if n == 0:
                    at_least(dve, y_stored[par], 16 * i)
                cols = slice(n * 512, (n + 1) * 512)
                nc.vector.tensor_tensor(y[:, par, cols], banks[2 * par + n][:], out_gate[:, seq, cols],
                                        ALU.mult).then_inc(scaled, 1)

            def add_x(t, par, i):
                dve.wait_ge(x_in[par], 16 * (i + 1))
                dve.wait_ge(scaled, 2 * t + 2)
                nc.vector.tensor_tensor(y[:, par], y[:, par], x[:, par], ALU.add).then_inc(added, 1)

            dve.wait_ge(decay_made, 1)
            dve.wait_ge(const_in, 64)
            carry(0, 0, 0)
            carry(1, 1, 0)
            for t in range(2):
                total_up(t, t)
                norm(t, t)
                mix_up(t, t)
            low(0, 0)

            def body(i, last, seq):
                for par in range(2):
                    t = 2 * i + par
                    if not last:
                        carry(t + 2, par, i + 1)
                    scale(t, par, 0, seq, i)
                    if not last:
                        total_up(t + 2, par)
                    if not (last and par == 1):
                        low(t + 1, 1 - par)
                    if not last:
                        norm(t + 2, par)
                        mix_up(t + 2, par)
                    scale(t, par, 1, seq, i)
                    add_x(t, par, i)

            seam = T_SAMPLE // P // 2
            body(0, False, 0)
            with dve.Fori(1, seam - 2) as i:
                body(i, False, 0)
            body(seam - 2, False, 0)
            body(seam - 1, False, 0)
            with dve.Fori(seam, PAIRS - 1) as i:
                body(i, False, 1)
            body(PAIRS - 1, True, 1)

        @block.tensor
        def _(pe):
            def cross(t, par, i):
                pe.wait_ge(state_made, t + 1)
                pe.wait_ge(tile_in[par], 96 * (i + 1))
                at_least(pe, totalled, t)
                for h in range(RH):
                    cols = slice(h * C, (h + 1) * C)
                    last = nc.tensor.matmul(cross_bank[:, cols], qf[:, par, cols], state[:, 1 - par, cols],
                                            start=True, stop=True)
                last.then_inc(crossed, 1)

            def turn(t, par):
                pe.wait_ge(mixed, t + 1)
                at_least(pe, lo_made, t)
                for k in range(KB):
                    last = nc.tensor.transpose(turn_banks[k // 4][:, k % 4, :], mix[:, par, k * P:(k + 1) * P],
                                               ident[:])
                last.then_inc(mix_turned, 1)

            def project(t, par, n):
                pe.wait_ge(lo_made, t + 1)
                at_least(pe, scaled, 2 * (t - 2) + n + 1)
                for k in range(KB):
                    for j, (m, w) in enumerate([(m_hi, w_out.hi), (m_hi, w_out.lo), (m_lo, w_out.hi)]):
                        last = nc.tensor.matmul(banks[2 * par + n][:], m[:, par, k, :], w[:, k, n * 512:(n + 1) * 512],
                                                start=(k == 0 and j == 0), stop=(k == KB - 1 and j == 2))
                last.then_inc(projected, 1)

            cross(0, 0, 0)
            cross(1, 1, 0)
            turn(0, 0)

            def body(i, last):
                for par in range(2):
                    t = 2 * i + par
                    project(t, par, 0)
                    if not (last and par == 1):
                        turn(t + 1, 1 - par)
                    if not last:
                        cross(t + 2, par, i + 1)
                    project(t, par, 1)

            over_pairs(pe, body)


def build(nc, a, y):
    dram = lambda n, s: nc.dram_tensor(n, s, F32, kind="Internal").ap()
    with ExitStack() as ctx:
        sb = lambda n, s: ctx.enter_context(nc.sbuf_tensor(n, s, F32))
        ident = sb("ident", [P, P])
        exps = sb("minus_half", [P, NH])
        gate_rows = dram("gate_rows", (2, D))
        bias_rows = dram("bias_rows", (QC, 3, NH * NDR, KC))
        qT_d = dram("qT_d", (NHD, NH, T))
        kT_d = dram("kT_d", (P, NH, T))
        vg_d = dram("vg_d", (TILES, P, D))
        na_d = dram("na_d", (TILES, P, HALF))
        masked_d = dram("masked_d", (P, 3, GH, KEYS))
        part_d, qf_d, kv_d, rg_d = (dram(n, (TILES, P, HALF)) for n in ("part_d", "qf_d", "kv_d", "rg_d"))
        x_tiles, y_tiles = a["x"], y
        with nc.sbuf_tensor("modx", [P, TILES, 16], F32) as modx:
            modulation_stage(nc, a["cT"], a["w_ada"], a["b_ada"], a["norm_gain"], a["rpb"], ident, modx, exps,
                             gate_rows, bias_rows)
            attention_in_stage(nc, x_tiles, a["w_in"][:, 0:4 * HALF], a["qk_gain"], modx, ident, exps, qT_d, kT_d, vg_d)
            retention_in_stage(nc, x_tiles, a["w_in"][:, 4 * HALF:8 * HALF], a["decays"], a["rope"], modx, ident, exps,
                               part_d, qf_d, kv_d, rg_d)
        w_out = Weights(nc, ctx, "w_out", a["w_out"], D)
        attention_stage(nc, qT_d, kT_d, vg_d, bias_rows, ident, masked_d, w_out, na_d)
        out_stage(nc, x_tiles, w_out, a["ret_gain"], gate_rows, a["decays"], na_d, vg_d, part_d, qf_d, kv_d, rg_d,
                  ident, exps, y_tiles)


def rope_table():
    half = RHD // 2
    inv = np.float32(10000.0) ** (-np.arange(half, dtype=np.float32) / np.float32(half))
    pos = np.concatenate([np.arange(T_SAMPLE), np.arange(T_PROMPT)]).astype(np.float32)
    angle = pos[:, None] * inv[None, :]
    return np.stack([np.cos(angle), np.sin(angle)], axis=1).astype(np.float32).reshape(TILES, P, 2, half)


def kernel(x_prompt, x_sample, c_prompt, c_sample, norm_gain, w_ada, b_ada, w_in, na_q_gain, na_k_gain, na_rpb,
           ret_decay_f, ret_decay_b, ret_out_gain, w_out):
    import concourse.bacc as bacc
    from concourse.bass_utils import run_bass_kernel_spmd

    c_both = np.concatenate([np.asarray(c_sample), np.asarray(c_prompt)])
    arrays = {
        "x": np.concatenate([np.asarray(x_sample)[0], np.asarray(x_prompt)[0]]).reshape(TILES, P, D),
        "cT": c_both.T.reshape(KB, P, 2).transpose(1, 0, 2),
        "norm_gain": np.asarray(norm_gain)[0].reshape(KB, P).T,
        "w_ada": np.asarray(w_ada)[0],
        "b_ada": np.asarray(b_ada),
        "w_in": np.asarray(w_in)[0],
        "qk_gain": np.stack([np.tile(np.asarray(g)[0], 2) for g in (na_q_gain, na_k_gain)], axis=1),
        "rpb": np.asarray(na_rpb)[0].reshape(NH * NDR, NDC),
        "decays": np.concatenate([np.asarray(ret_decay_f)[0], np.asarray(ret_decay_b)[0]]),
        "ret_gain": np.asarray(ret_out_gain)[0].reshape(HALF),
        "w_out": np.asarray(w_out)[0],
        "rope": rope_table(),
    }
    nc = bacc.Bacc("TRN2", target_bir_lowering=False, num_devices=1)
    arrays = {f"in_{n}": np.ascontiguousarray(v) for n, v in arrays.items()}
    aps = {n[3:]: nc.dram_tensor(n, v.shape, mybir.dt.from_np(v.dtype), kind="ExternalInput").ap()
           for n, v in arrays.items()}
    y = nc.dram_tensor("y", (TILES, P, D), F32, kind="ExternalOutput").ap()
    build(nc, aps, y)
    got = run_bass_kernel_spmd(nc, [arrays], core_ids=[0]).results[0]["y"].reshape(T, D)
    return got[T_SAMPLE:].reshape(1, T_PROMPT, D), got[:T_SAMPLE].reshape(1, T_SAMPLE, D)
```

```python
from contextlib import ExitStack

import concourse.bass as bass
import numpy as np
from concourse import mybir

F32 = mybir.dt.float32
F32R = mybir.dt.float32r
BF16 = mybir.dt.bfloat16
ALU = mybir.AluOpType
ACT = mybir.ActivationFunctionType
AX = mybir.AxisListType

P = 128
D = 1024
KB = D // P
T_SAMPLE, T_PROMPT = 4096, 1024
T = T_SAMPLE + T_PROMPT
TILES = T // P
PAIRS = TILES // 2
HALF = D // 2
NH, NHD = 8, 64
RH, RHD = 4, 128
C = 128
EPS = 1e-6
W = 64
QR, QC = 8, 16
KR, KC = 15, 32
KEYS = KR * KC
WIN_H, WIN_W = 8, 16
NDR, NDC = 2 * WIN_H - 1, 2 * WIN_W - 1
MASKED = 1.0e30
COLS = W // QC
K0 = [0, 8, 24, 32]
KIND = [0, 1, 1, 2]
S_ROWS, P_ROWS = T_SAMPLE // W, T_PROMPT // W
STRIPS = (
    [(0, 0), (S_ROWS, S_ROWS)]
    + [(QR * b, QR * b - 4) for b in range(1, S_ROWS // QR - 1)]
    + [(S_ROWS - QR, S_ROWS - KR), (S_ROWS + P_ROWS - QR, S_ROWS + P_ROWS - KR)]
)
GH = 4
GW = GH * NHD


def at_least(eng, sem, count):
    if isinstance(count, int) and count <= 0:
        return
    eng.wait_ge(sem, count)


def apart(passed):

    def wait_apart(eng, sem, count):
        at_least(eng, sem, count)
        if not isinstance(count, int):
            eng.sem_inc(passed, 1)

    return wait_apart


def over_pairs(eng, body):
    body(0, False)
    with eng.Fori(1, PAIRS - 1) as i:
        body(i, False)
    body(PAIRS - 1, True)


def modulation_stage(nc, cT, w_ada, b_ada, norm_gain, rpb, ident, modx, exps, gate_rows,
                     bias_rows, w):
    with ExitStack() as ctx:
        sb = lambda n, s, d=F32: ctx.enter_context(nc.sbuf_tensor(n, s, d))
        sem = lambda n: ctx.enter_context(nc.semaphore(n))
        ada = sb("ada", [P, 3, 3 * D])
        cond = sb("cond", [P, KB, 2])
        silu_c = sb("silu_c", [P, KB, 2])
        b_rows = sb("b_rows", [2, 3 * D])
        mod = sb("mod", [2, 3 * D])
        gain = sb("gain", [P, KB])
        mod_cols = sb("mod_cols", [P, 16, 2])
        one_seq = sb("one_seq", [P, 2, 16])
        rpb_rows = sb("rpb_rows", [NH * NDR, NDC])
        spread = sb("spread", [NH * NDR, 3, QC, KC])
        banks = [ctx.enter_context(nc.psum_tensor(f"mod_bank{j}", [P, 512], F32)) for j in range(6)]
        cols_bank = ctx.enter_context(nc.psum_tensor("cols_bank", [P, 16, 2], F32))
        wait_apart = apart(sem("m_passed"))
        small_in, ada_in, ada_used = sem("small_in"), [sem(f"ada_in{k}") for k in range(3)], sem("ada_used")
        ident_made, silu_made, mod_summed = sem("ident_made"), sem("silu_made"), sem("mod_summed")
        mod_made, cols_turned, modx_made = sem("mod_made"), sem("cols_turned"), sem("modx_made")
        spread_made, mod_stored = sem("spread_made"), sem("mod_stored")
        block = ctx.enter_context(nc.Block())

        @block.sync
        def _(sp):
            sp.dma_start(cond[:], cT).then_inc(small_in, 16)
            sp.dma_start(b_rows[0:1, :], b_ada).then_inc(small_in, 16)
            sp.dma_start(b_rows[1:2, :], b_ada).then_inc(small_in, 16)
            sp.dma_start(gain[:], norm_gain).then_inc(small_in, 16)
            sp.dma_start(rpb_rows[:], rpb).then_inc(small_in, 16)
            for k in range(KB):
                if k >= 3:
                    sp.wait_ge(ada_used, k - 2)
                sp.dma_start(ada[:, k % 3, :], w_ada[k * P:(k + 1) * P, :]).then_inc(ada_in[k % 3], 16)
                if k >= 4:
                    w.load(sp, k - 4)
            wait_apart(sp, spread_made, 6)
            for k in range(3):
                sp.dma_start(bias_rows[:, k].rearrange("c hd x -> hd c x"), spread[:, k]).then_inc(mod_stored, 16)
            for k in range(4, KB):
                w.load(sp, k)
            wait_apart(sp, mod_made, 6)
            sp.dma_start(gate_rows, mod[:, 2 * D:3 * D]).then_inc(mod_stored, 16)
            wait_apart(sp, mod_stored, 64)

        @block.gpsimd
        def _(pool):
            nc.gpsimd.memset(ident[:], 0.0).then_inc(ident_made, 1)
            wait_apart(pool, ident_made, 1)
            nc.gpsimd.affine_select(out=ident[:], in_=ident[:], compare_op=ALU.not_equal, fill=1.0, base=0,
                                    pattern=[[-1, P]], channel_multiplier=1).then_inc(ident_made, 1)
            nc.gpsimd.memset(exps[:], -0.5).then_inc(ident_made, 1)

        @block.scalar
        def _(act):
            act.wait_ge(small_in, 80)
            nc.scalar.activation(silu_c[:], cond[:], ACT.Silu).then_inc(silu_made, 1)
            for k in range(KB):
                w.make_hi(act, k)

        @block.vector
        def _(dve):
            nc.vector.memset(spread[:], MASKED).then_inc(spread_made, 1)
            dve.wait_ge(small_in, 80)
            dve.wait_ge(spread_made, 1)
            mid = NDC // 2

            def put(kind, c0, c1, key0, key_step, dc0, dc_step):
                flat = spread[:].rearrange("q k c x -> q (k c x)")
                src = rpb_rows[:]
                for c in range(c0, c1):
                    k_at = (kind * QC + c) * KC + key0 + key_step * (c - c0)
                    d_at = dc0 + dc_step * (c - c0)
                    last = nc.vector.tensor_scalar(flat[:, k_at:k_at + WIN_W], src[:, d_at:d_at + WIN_W], -1.0,
                                                   None, ALU.mult)
                last.then_inc(spread_made, 1)

            put(0, 0, 8, 0, 0, mid, -1)
            put(0, 8, QC, 0, 1, mid - 8, 0)
            put(1, 0, QC, 0, 1, mid - 8, 0)
            put(2, 0, 9, 8, 1, mid - 8, 0)
            put(2, 9, QC, 16, 0, mid - 9, -1)
            dve.wait_ge(mod_summed, 1)
            for n in range(6):
                nc.vector.tensor_tensor(mod[:, 512 * n:512 * (n + 1)], banks[n][0:2, :],
                                        b_rows[:, 512 * n:512 * (n + 1)], ALU.add).then_inc(mod_made, 1)
            dve.wait_ge(cols_turned, 1)
            nc.vector.tensor_copy(mod_cols[:], cols_bank[:]).then_inc(modx_made, 1)
            dve.wait_ge(modx_made, 1)
            for s in range(2):
                nc.vector.scalar_tensor_tensor(out=one_seq[:, s, 0:8], in0=mod_cols[:, 8:16, s], scalar=1.0,
                                               in1=gain[:], op0=ALU.add, op1=ALU.mult)
                nc.vector.tensor_copy(one_seq[:, s, 8:16], mod_cols[:, 0:8, s]).then_inc(modx_made, 1)
            dve.wait_ge(modx_made, 3)
            t_s = T_SAMPLE // P
            nc.vector.tensor_copy(modx[:, 0:t_s, :], one_seq[:, 0:1, :].to_broadcast([P, t_s, 16]))
            nc.vector.tensor_copy(modx[:, t_s:TILES, :],
                                  one_seq[:, 1:2, :].to_broadcast([P, TILES - t_s, 16])).then_inc(modx_made, 1)
            for k in range(4):
                w.make_lo(dve, k)

        @block.tensor
        def _(pe):
            pe.wait_ge(silu_made, 1)
            for k in range(KB):
                pe.wait_ge(ada_in[k % 3], 16 * (k // 3 + 1))
                for n in range(6):
                    last = nc.tensor.matmul(banks[n][0:2, :], silu_c[:, k, :], ada[:, k % 3, 512 * n:512 * (n + 1)],
                                            start=(k == 0), stop=(k == KB - 1))
                if k < KB - 1:
                    last.then_inc(ada_used, 1)
            last.then_inc(mod_summed, 1)
            pe.wait_ge(ident_made, 2)
            pe.wait_ge(mod_made, 6)
            for j in range(16):
                last = nc.tensor.transpose(cols_bank[:, j, :], mod[:, j * P:(j + 1) * P], ident[0:2, 0:2])
            last.then_inc(cols_turned, 1)


class Weights:

    def __init__(self, nc, ctx, tag, w, width):
        self.nc, self.w = nc, w
        with nc.sbuf_tensor(f"{tag}_raw", [P, KB, width], F32) as self.raw:
            pass
        self.lo, self.hi = (ctx.enter_context(nc.sbuf_tensor(f"{tag}_{n}", [P, KB, width], F32R)) for n in ("lo", "hi"))
        self.landed = [ctx.enter_context(nc.semaphore(f"{tag}_landed{j}")) for j in range(2)]
        self.hi_made, self.lo_made = (ctx.enter_context(nc.semaphore(f"{tag}_{n}")) for n in ("hi_made", "lo_made"))

    def load(self, eng, k):
        eng.dma_start(self.raw[:, k], self.w[k * P:(k + 1) * P, :]).then_inc(self.landed[k // 4], 16)

    def make_hi(self, act, k):
        act.wait_ge(self.landed[k // 4], 64)
        self.nc.scalar.activation(self.hi[:, k], self.raw[:, k], ACT.Copy).then_inc(self.hi_made, 1)

    def make_lo(self, dve, k):
        dve.wait_ge(self.hi_made, k + 1)
        self.nc.vector.tensor_tensor(self.lo[:, k], self.raw[:, k], self.hi[:, k].bitcast(F32),
                                     ALU.subtract).then_inc(self.lo_made, 1)


class NextWeights:

    def __init__(self, nc, ctx, tag, place, w):
        self.nc, self.w, self.raw, self.hi, self.lo = nc, w, place.raw, place.hi, place.lo
        self.landed = [ctx.enter_context(nc.semaphore(f"{tag}_landed{n}")) for n in range(4)]
        self.hi_made, self.lo_made = (ctx.enter_context(nc.semaphore(f"{tag}_{n}")) for n in ("hi_made", "lo_made"))

    def load(self, sp, n):
        cols = slice(n * HALF, (n + 1) * HALF)
        sp.dma_start(self.raw[:, :, cols], self.w[:, cols].rearrange("(k p) n -> p k n", p=P)
                     ).then_inc(self.landed[n], 16)

    def make_hi(self, act, n):
        cols = slice(n * HALF, (n + 1) * HALF)
        act.wait_ge(self.landed[n], 16)
        self.nc.scalar.activation(self.hi[:, :, cols], self.raw[:, :, cols], ACT.Copy).then_inc(self.hi_made, 1)

    def make_lo(self, dve, n):
        cols = slice(n * HALF, (n + 1) * HALF)
        dve.wait_ge(self.hi_made, n + 1)
        self.nc.vector.tensor_tensor(self.lo[:, :, cols], self.raw[:, :, cols], self.hi[:, :, cols].bitcast(F32),
                                     ALU.subtract).then_inc(self.lo_made, 1)


class Projection:

    def __init__(self, nc, ctx, tag, w, first=None):
        sb = lambda n, s, d=F32: ctx.enter_context(nc.sbuf_tensor(f"{tag}_{n}", s, d))
        self.nc, self.w = nc, w
        if first is None:
            self.h_hi, self.h_lo = sb("h_hi", [P, 2, KB, P], F32R), sb("h_lo", [P, 2, KB, P], F32R)
            self.banks = [ctx.enter_context(nc.psum_tensor(f"proj{n}", [P, 512], F32)) for n in range(4)]
        else:
            self.h_hi, self.h_lo, self.banks = first.h_hi, first.h_lo, first.banks
        self.projected = ctx.enter_context(nc.semaphore(f"{tag}_projected"))

    def project(self, par, n):
        bank = self.banks[n][:]
        cols = slice(n * HALF, (n + 1) * HALF)
        for k in range(KB):
            for j, (h, w) in enumerate([(self.h_hi, self.w.hi), (self.h_hi, self.w.lo), (self.h_lo, self.w.hi)]):
                last = self.nc.tensor.matmul(bank, h[:, par, k, :], w[:, k, cols], start=(k == 0 and j == 0),
                                             stop=(k == KB - 1 and j == 2))
        last.then_inc(self.projected, 1)


class Front:

    def __init__(self, nc, ctx, tag, x_tiles, xT_tiles, product, modx, ident, half_eps, h_d):
        self.nc, self.h_hi, self.h_lo, self.projected = nc, product.h_hi, product.h_lo, product.projected
        sb = lambda n, s, d=F32: ctx.enter_context(nc.sbuf_tensor(f"{tag}_{n}", s, d))
        sem = lambda n: ctx.enter_context(nc.semaphore(f"{tag}_{n}"))
        self.x_tiles, self.xT_tiles, self.modx, self.ident = x_tiles, xT_tiles, modx, ident
        self.half, self.h_d = half_eps, h_d
        self.x = sb("x", [P, 2, D])
        self.xT = sb("xT", [P, 2, KB, P])
        self.h_full = sb("h_full", [P, D])
        self.ones = sb("ones", [P, P])
        self.diagonal = sb("diagonal", [P, P])
        self.junk = sb("junk", [P, D], BF16)
        self.x_stat = sb("x_stat", [P, 4])
        self.mod_now = sb("mod_now", [P, 2, 16])
        self.rstd_bank = ctx.enter_context(nc.psum_tensor(f"{tag}_rstd", [P, P], F32))
        self.ones_made = sem("ones_made")
        self.wait_apart = apart(sem("passed"))
        self.x_in = [sem("x_in0"), sem("x_in1")]
        self.h_stored = [sem("h_stored0"), sem("h_stored1")]
        self.x_squared, self.x_mean, self.x_rstd = sem("x_squared"), sem("x_mean"), sem("x_rstd")
        self.diagonal_made, self.rstd_spread, self.x_normed = sem("diagonal_made"), sem("rstd_spread"), sem("x_normed")
        self.mod_placed = sem("mod_placed")
        self.h_modulated, self.h_hi_made, self.h_split = sem("h_modulated"), sem("h_hi_made"), sem("h_split")

    def load_x(self, sp, s, par):
        self.wait_apart(sp, self.x_normed, s - 1)
        sp.dma_start(self.x[:, par, :], self.x_tiles[s]).then_inc(self.x_in[par], 16)
        sp.dma_start(self.xT[:, par], self.xT_tiles[s]).then_inc(self.x_in[par], 16)

    def store_h(self, sp, s, par):
        self.wait_apart(sp, self.h_split, s + 1)
        for part, h in enumerate((self.h_hi, self.h_lo)):
            sp.dma_start(self.h_d[s, part], h[:, par].rearrange("p k t -> p (k t)").bitcast(F32)
                         ).then_inc(self.h_stored[par], 16)

    def square_x(self, act, s, par, i):
        act.wait_ge(self.x_in[par], 32 * (i + 1))
        at_least(act, self.x_mean, s)
        self.nc.scalar.activation(self.junk[:], self.x[:, par, :], ACT.Square,
                                  accum_out=self.x_stat[:, 0:1]).then_inc(self.x_squared, 1)

    def mean_x(self, dve, s):
        dve.wait_ge(self.x_squared, s + 1)
        self.nc.vector.tensor_scalar(self.x_stat[:, 1:2], self.x_stat[:, 0:1], 1.0 / D, EPS, ALU.mult,
                                     ALU.add).then_inc(self.x_mean, 1)

    def rstd_x(self, pool, s):
        self.wait_apart(pool, self.x_mean, s + 1)
        self.nc.gpsimd.tensor_tensor(self.x_stat[:, 2:3], self.x_stat[:, 1:2], self.half[:, 0:1],
                                     ALU.pow).then_inc(self.x_rstd, 1)

    def make_diagonal(self, dve, s):
        dve.wait_ge(self.x_rstd, s + 1)
        at_least(dve, self.rstd_spread, s)
        self.nc.vector.tensor_scalar(self.diagonal[:], self.ident[:], self.x_stat[:, 2:3], None,
                                     ALU.mult).then_inc(self.diagonal_made, 1)

    def norm_x(self, dve, s, par):
        dve.wait_ge(self.rstd_spread, s + 1)
        at_least(dve, self.h_split, s)
        self.nc.vector.tensor_tensor(self.h_full[:].rearrange("p (k t) -> p k t", k=KB), self.xT[:, par],
                                     self.rstd_bank[:].unsqueeze(1).to_broadcast([P, KB, P]),
                                     ALU.mult).then_inc(self.x_normed, 1)

    def place_mod(self, pool, s, par):
        self.wait_apart(pool, self.h_modulated, s - 1)
        self.nc.gpsimd.tensor_copy(self.mod_now[:, par, :], self.modx[:, bass.ds(s, 1), :]
                                   .rearrange("p a b -> p (a b)")).then_inc(self.mod_placed, 1)

    def spread_rstd(self, pe, s):
        pe.wait_ge(self.diagonal_made, s + 1)
        at_least(pe, self.x_normed, s)
        self.nc.tensor.matmul(self.rstd_bank[:], self.ones[:], self.diagonal[:], start=True,
                              stop=True).then_inc(self.rstd_spread, 1)

    def modulate(self, act, s, par):
        act.wait_ge(self.x_normed, s + 1)
        act.wait_ge(self.mod_placed, s + 1)
        for k in range(KB):
            last = self.nc.scalar.activation(self.h_full[:, k * P:(k + 1) * P], self.h_full[:, k * P:(k + 1) * P],
                                             ACT.Identity, scale=self.mod_now[:, par, k:k + 1],
                                             bias=self.mod_now[:, par, KB + k:KB + k + 1])
        last.then_inc(self.h_modulated, 1)

    def split_h(self, dve, s, par, i):
        dve.wait_ge(self.h_modulated, s + 1)
        at_least(dve, self.h_stored[par], 32 * i)
        at_least(dve, self.projected, 4 * (s - 1))
        hi = self.h_hi[:, par].rearrange("p k t -> p (k t)")
        lo = self.h_lo[:, par].rearrange("p k t -> p (k t)")
        self.nc.vector.tensor_copy(hi, self.h_full[:]).then_inc(self.h_hi_made, 1)
        dve.wait_ge(self.h_hi_made, s + 1)
        self.nc.vector.tensor_tensor(lo, self.h_full[:], hi.bitcast(F32), ALU.subtract).then_inc(self.h_split, 1)


def attention_in_stage(nc, x_tiles, xT_tiles, product, next_product, gains, modx, ident, exps, h_d, qT_d, kT_d, vg_d):
    with ExitStack() as ctx:
        w, next_w = product.w, next_product.w
        f = Front(nc, ctx, "a", x_tiles, xT_tiles, product, modx, ident, exps, h_d)
        sb = lambda n, s, d=F32: ctx.enter_context(nc.sbuf_tensor(n, s, d))
        sem = lambda n: ctx.enter_context(nc.semaphore(n))
        gain = sb("qk_gain", [P, 2])
        normed, squares = sb("normed", [P, 2, HALF]), sb("qk_squares", [P, 2, HALF])
        vg = sb("vg", [P, 2, D])
        turned = sb("qkT", [P, 2, 4, 2 * P])
        k_parts = sb("k_parts", [P, 2, 4, 2 * P], F32R)
        stat = sb("qk_stat", [P, 3, 2, NH])
        banks = product.banks
        qk_banks = [ctx.enter_context(nc.psum_tensor(f"a_qkT{j}", [P, 4, P], F32)) for j in range(2)]
        wait_apart = f.wait_apart
        gain_in, gain_made = sem("gain_in"), sem("gain_made")
        squared, summed, meaned, rstd_made = sem("qk_squared"), sem("qk_summed"), sem("qk_meaned"), sem("qk_rstd")
        qk_normed, qk_turned, qk_out = sem("qk_normed"), sem("qk_turned"), sem("qk_out")
        vg_made, k_split = sem("vg_made"), sem("k_split")
        vg_stored, qk_stored = [sem("vg_stored0"), sem("vg_stored1")], sem("qk_stored")
        block = ctx.enter_context(nc.Block())

        @block.sync
        def _(sp):
            for par in range(2):
                f.load_x(sp, par, par)
            sp.dma_start(gain[:], gains).then_inc(gain_in, 16)
            f.store_h(sp, 0, 0)

            def store_vg(t, par):
                wait_apart(sp, vg_made, 2 * t + 2)
                sp.dma_start(vg_d[t], vg[:, par, :]).then_inc(vg_stored[par], 16)

            def store_qk(i):
                tokens = bass.ds(i * 2 * P, 2 * P)
                wait_apart(sp, k_split, 4 * i + 4)
                for odd in range(2):
                    rows = slice(odd * NHD, (odd + 1) * NHD)
                    sp.dma_start(qT_d.rearrange("d (j x) t -> d j x t", x=2)[:, :, odd, tokens],
                                 turned[rows, 0]).then_inc(qk_stored, 16)
                    for part in range(2):
                        sp.dma_start(kT_d.rearrange("d (j x) t -> d j x t", x=2)
                                     [part * NHD:(part + 1) * NHD, :, odd, tokens],
                                     k_parts[rows, part].bitcast(F32)).then_inc(qk_stored, 16)

            def body(i, last):
                for par in range(2):
                    t = 2 * i + par
                    if not last:
                        f.load_x(sp, t + 2, par)
                    if not (last and par == 1):
                        f.store_h(sp, t + 1, 1 - par)
                    else:
                        for n in range(3):
                            sp.wait_ge(f.projected, 4 * t + n + 1)
                            next_w.load(sp, n)
                    store_vg(t, par)
                store_qk(i)
                if last:
                    next_w.load(sp, 3)

            over_pairs(sp, body)
            for par in range(2):
                wait_apart(sp, f.h_stored[par], 32 * PAIRS)
                wait_apart(sp, vg_stored[par], 16 * PAIRS)
            wait_apart(sp, qk_stored, 96 * PAIRS)

        @block.gpsimd
        def _(pool):
            nc.gpsimd.memset(f.ones[:], 1.0).then_inc(f.ones_made, 1)
            f.rstd_x(pool, 0)
            f.place_mod(pool, 0, 0)
            f.rstd_x(pool, 1)

            def body(i, last):
                for par in range(2):
                    t = 2 * i + par
                    for a in range(2):
                        wait_apart(pool, meaned, 2 * t + a + 1)
                        nc.gpsimd.tensor_tensor(stat[:, 2, a, :], stat[:, 1, a, :], exps[:, 0:NH],
                                                ALU.pow).then_inc(rstd_made, 1)
                    if not (last and par == 1):
                        f.place_mod(pool, t + 1, 1 - par)
                    if not last:
                        f.rstd_x(pool, t + 2)

            over_pairs(pool, body)

        @block.scalar
        def _(act):
            f.square_x(act, 0, 0, 0)
            f.modulate(act, 0, 0)
            f.square_x(act, 1, 1, 0)

            def body(i, last):
                for par in range(2):
                    t = 2 * i + par
                    for a in range(2):
                        act.wait_ge(f.projected, 4 * t + a + 1)
                        at_least(act, summed, 2 * t + a - 1)
                        nc.scalar.activation(squares[:, a, :], banks[a][:], ACT.Square).then_inc(squared, 1)
                    if not (last and par == 1):
                        f.modulate(act, t + 1, 1 - par)
                    else:
                        next_w.make_hi(act, 0)
                    act.wait_ge(f.projected, 4 * t + 3)
                    at_least(act, vg_stored[par], 16 * i)
                    nc.scalar.activation(vg[:, par, 0:HALF], banks[2][:], ACT.Copy).then_inc(vg_made, 1)
                    if not last:
                        f.square_x(act, t + 2, par, i + 1)
                    act.wait_ge(f.projected, 4 * t + 4)
                    nc.scalar.activation(vg[:, par, HALF:D], banks[3][:], ACT.Silu).then_inc(vg_made, 1)

            over_pairs(act, body)
            next_w.make_hi(act, 1)
            next_w.make_hi(act, 2)

        @block.vector
        def _(dve):
            w.make_lo(dve, 4)
            w.make_lo(dve, 5)
            f.mean_x(dve, 0)
            f.make_diagonal(dve, 0)
            f.norm_x(dve, 0, 0)
            w.make_lo(dve, 6)
            w.make_lo(dve, 7)
            f.split_h(dve, 0, 0, 0)
            f.mean_x(dve, 1)
            f.make_diagonal(dve, 1)
            dve.wait_ge(gain_in, 16)
            nc.vector.tensor_scalar(gain[:, 0:1], gain[:, 0:1], -(NHD ** -0.5), None, ALU.mult).then_inc(gain_made, 1)
            dve.wait_ge(gain_made, 1)

            def norm_heads(t, a):
                n = 2 * t + a
                dve.wait_ge(squared, n + 1)
                nc.vector.tensor_reduce(stat[:, 0, a, :], squares[:, a, :].rearrange("p (h d) -> p h d", h=NH),
                                        AX.X, ALU.add).then_inc(summed, 1)
                dve.wait_ge(summed, n + 1)
                nc.vector.tensor_scalar(stat[:, 1, a, :], stat[:, 0, a, :], 1.0 / NHD, EPS, ALU.mult,
                                        ALU.add).then_inc(meaned, 1)
                dve.wait_ge(rstd_made, n + 1)
                at_least(dve, qk_turned, n - 1)
                nc.vector.tensor_tensor(normed[:, a, :].rearrange("p (h d) -> p h d", h=NH),
                                        banks[a][:].rearrange("p (h d) -> p h d", h=NH),
                                        stat[:, 2, a, :].unsqueeze(2).to_broadcast([P, NH, NHD]),
                                        ALU.mult).then_inc(qk_normed, 1)

            def heads_out(i, t, par, a):
                dve.wait_ge(qk_turned, 2 * t + a + 1)
                if par == 0:
                    at_least(dve, qk_stored, 96 * i)
                nc.vector.tensor_scalar(turned[:, a, :, par * P:(par + 1) * P], qk_banks[a][:], gain[:, a:a + 1],
                                        None, ALU.mult).then_inc(qk_out, 1)

            def split_k(t, par):
                tokens = slice(par * P, (par + 1) * P)
                dve.wait_ge(qk_out, 2 * t + 2)
                nc.vector.tensor_copy(k_parts[:, 0, :, tokens], turned[:, 1, :, tokens]).then_inc(k_split, 1)
                dve.wait_ge(k_split, 2 * t + 1)
                nc.vector.tensor_tensor(k_parts[:, 1, :, tokens], turned[:, 1, :, tokens],
                                        k_parts[:, 0, :, tokens].bitcast(F32), ALU.subtract).then_inc(k_split, 1)

            def body(i, last):
                for par in range(2):
                    t = 2 * i + par
                    norm_heads(t, 0)
                    if not (last and par == 1):
                        f.norm_x(dve, t + 1, 1 - par)
                    norm_heads(t, 1)
                    if not (last and par == 1):
                        f.split_h(dve, t + 1, 1 - par, i + par)
                    else:
                        next_w.make_lo(dve, 0)
                    if not last:
                        f.mean_x(dve, t + 2)
                        f.make_diagonal(dve, t + 2)
                    heads_out(i, t, par, 0)
                    heads_out(i, t, par, 1)
                    split_k(t, par)

            over_pairs(dve, body)
            next_w.make_lo(dve, 1)

        @block.tensor
        def _(pe):
            pe.wait_ge(f.ones_made, 1)
            f.spread_rstd(pe, 0)

            def turn_heads(t, a):
                pe.wait_ge(qk_normed, 2 * t + a + 1)
                at_least(pe, qk_out, 2 * t + a - 1)
                for j in range(4):
                    last = nc.tensor.transpose(qk_banks[a][:, j, :], normed[:, a, j * P:(j + 1) * P], ident[:])
                last.then_inc(qk_turned, 1)

            pe.wait_ge(w.lo_made, KB)

            def body(i, last):
                for par in range(2):
                    t = 2 * i + par
                    pe.wait_ge(f.h_split, t + 1)
                    for n in range(4):
                        if n < 2:
                            at_least(pe, qk_normed, 2 * t + n - 1)
                        else:
                            at_least(pe, vg_made, 2 * t + n - 3)
                        product.project(par, n)
                        if n == 1 and not (last and par == 1):
                            f.spread_rstd(pe, t + 1)
                        if n == 2:
                            turn_heads(t, 0)
                    turn_heads(t, 1)

            over_pairs(pe, body)
            for n in range(2):
                pe.wait_ge(next_w.lo_made, n + 1)
                pe.wait_ge(qk_normed, 2 * TILES - 1 + n)
                next_product.project(1, n)


def retention_in_stage(nc, f, h_d, decays, rope, ident, part_d, qf_d, kv_d, gate_d):
    with ExitStack() as ctx:
        w, proj = f.w, f.banks
        sb = lambda n, s, d=F32: ctx.enter_context(nc.sbuf_tensor(n, s, d))
        sem = lambda n: ctx.enter_context(nc.semaphore(n))
        raw, rot = sb("raw", [P, 2, HALF]), sb("rot", [P, 2, HALF])
        v, gate = sb("v", [P, HALF])[:], sb("gate", [P, HALF])[:]
        turned = sb("rqkT", [P, 2, HALF])
        cs = sb("cos_sin", [P, 2, 2, 64])
        product = sb("rot_product", [P, 2, 256])
        q_dec = sb("q_dec", [P, 2, HALF])
        k_dec = sb("k_dec", [P, 2, HALF])
        weighted = sb("weighted", [P, HALF])
        state = sb("state_b", [P, 2, HALF])
        kv_out = sb("kv_out", [P, HALF])
        part = sb("part", [P, HALF])
        within = sb("within", [P, RH, C])
        q_scale = sb("q_scale", [P, 2, RH, C])
        lg = sb("lg", [P, 2 * RH])
        k_scale = sb("k_scale", [P, 2 * RH])
        chunk_decay = sb("chunk_decay", [P, 2 * RH])
        pos = sb("pos", [P, 2])
        qk_banks = [ctx.enter_context(nc.psum_tensor(f"r_qkT{j}", [P, 4, P], F32)) for j in range(2)]
        so_bank = ctx.enter_context(nc.psum_tensor("r_so", [P, 512], F32))
        kv_bank = ctx.enter_context(nc.psum_tensor("r_kv", [P, 512], F32))
        wait_apart = apart(sem("r_passed"))
        decay_in, lg_made, pos_made = sem("decay_in"), sem("lg_made"), sem("pos_made")
        const_made, expo_made = sem("const_made"), sem("expo_made")
        cs_in, h_in = [sem("cs_in0"), sem("cs_in1")], [sem("h_in0"), sem("h_in1")]
        raw_made, multiplied, rotated = sem("raw_made"), sem("multiplied"), sem("rotated")
        v_made, gate_made = sem("v_made"), sem("gate_made")
        qk_turned, turned_out = sem("rqk_turned"), sem("turned_out")
        q_decayed, k_decayed = sem("q_decayed"), sem("k_decayed")
        scored, kv_b_done, kv_f_done, part_done = sem("scored"), sem("kv_b_done"), sem("kv_f_done"), sem("part_done")
        weighted_made, state_decayed, state_made = sem("weighted_made"), sem("state_decayed"), sem("state_made")
        kv_out_made, part_made = sem("kv_out_made"), sem("part_made")
        kv_stored, part_stored = sem("kv_stored"), sem("part_stored")
        qf_stored, gate_stored = sem("qf_stored"), sem("gate_stored")
        block = ctx.enter_context(nc.Block())

        def tile(s):
            return TILES - 1 - s

        def heads(ap):
            return ap.rearrange("p (h n) -> p h n", h=RH)

        @block.sync
        def _(sp):
            sp.dma_start(lg[:], decays.partition_broadcast(P)).then_inc(decay_in, 16)

            def load_cs(s, par):
                wait_apart(sp, rotated, 4 * (s - 1))
                sp.dma_start(cs[:, par], rope[tile(s)]).then_inc(cs_in[par], 16)

            def load_h(s, par):
                wait_apart(sp, f.projected, 4 * (s - 1))
                for part, h in enumerate((f.h_hi, f.h_lo)):
                    sp.dma_start(h[:, 1 - par].rearrange("p k t -> p (k t)").bitcast(F32),
                                 h_d[tile(s), part]).then_inc(h_in[par], 16)

            load_h(1, 1)
            for par in range(2):
                load_cs(par, par)

            def store_late(s):
                wait_apart(sp, kv_out_made, s + 1)
                sp.dma_start(kv_d[tile(s)], kv_out[:]).then_inc(kv_stored, 16)
                wait_apart(sp, part_made, s + 1)
                sp.dma_start(part_d[tile(s)], part[:]).then_inc(part_stored, 16)

            def body(i, last):
                for par in range(2):
                    s = 2 * i + par
                    if not (isinstance(i, int) and s == 0):
                        store_late(s - 1)
                    wait_apart(sp, q_decayed, 2 * s + 1)
                    sp.dma_start(qf_d[tile(s)], q_dec[:, 0]).then_inc(qf_stored, 16)
                    wait_apart(sp, gate_made, s + 1)
                    sp.dma_start(gate_d[tile(s)], gate).then_inc(gate_stored, 16)
                    if not last:
                        load_cs(s + 2, par)
                        load_h(s + 2, par)

            over_pairs(sp, body)
            store_late(TILES - 1)
            for q in (kv_stored, part_stored, qf_stored, gate_stored):
                wait_apart(sp, q, 16 * TILES)

        @block.gpsimd
        def _(pool):
            nc.gpsimd.iota(within[:], pattern=[[0, RH], [1, C]], base=0, channel_multiplier=-1,
                           allow_small_or_imprecise_dtypes=True).then_inc(pos_made, 1)
            nc.gpsimd.iota(q_scale[:, 0], pattern=[[0, RH], [1, C]], base=1, channel_multiplier=0,
                           allow_small_or_imprecise_dtypes=True).then_inc(pos_made, 1)
            nc.gpsimd.iota(q_scale[:, 1], pattern=[[0, RH], [-1, C]], base=C, channel_multiplier=0,
                           allow_small_or_imprecise_dtypes=True).then_inc(pos_made, 1)
            nc.gpsimd.iota(pos[:, 0:1], pattern=[[0, 1]], base=C - 1, channel_multiplier=-1,
                           allow_small_or_imprecise_dtypes=True).then_inc(pos_made, 1)
            nc.gpsimd.iota(pos[:, 1:2], pattern=[[0, 1]], base=0, channel_multiplier=1,
                           allow_small_or_imprecise_dtypes=True).then_inc(pos_made, 1)

        @block.scalar
        def _(act):
            act.wait_ge(decay_in, 16)
            nc.scalar.activation(lg[:], lg[:], ACT.Exp).then_inc(lg_made, 1)
            w.make_hi(act, 3)
            act.wait_ge(expo_made, 12)
            nc.scalar.activation(within[:], within[:], ACT.Exp).then_inc(const_made, 1)
            nc.scalar.activation(q_scale[:], q_scale[:], ACT.Exp).then_inc(const_made, 1)
            nc.scalar.activation(k_scale[:], k_scale[:], ACT.Exp).then_inc(const_made, 1)
            nc.scalar.activation(chunk_decay[:], lg[:], ACT.Exp, scale=float(C)).then_inc(const_made, 1)

            def late(s):
                act.wait_ge(kv_f_done, s + 1)
                at_least(act, kv_stored, 16 * s)
                nc.scalar.activation(kv_out[:], kv_bank[:], ACT.Copy).then_inc(kv_out_made, 1)
                act.wait_ge(part_done, s + 1)
                at_least(act, part_stored, 16 * s)
                nc.scalar.activation(part[:], so_bank[:], ACT.Copy).then_inc(part_made, 1)

            def body(i, last):
                for par in range(2):
                    s = 2 * i + par
                    for a in range(2):
                        act.wait_ge(f.projected, 4 * s + a + 1)
                        at_least(act, rotated, 4 * s + 2 * a - 2)
                        nc.scalar.activation(raw[:, a], proj[a][:], ACT.Copy,
                                             scale=(1.0 if a == 0 else RHD ** -0.5)).then_inc(raw_made, 1)
                    if not (isinstance(i, int) and s == 0):
                        late(s - 1)
                    act.wait_ge(f.projected, 4 * s + 3)
                    nc.scalar.activation(v, proj[2][:], ACT.Copy).then_inc(v_made, 1)
                    act.wait_ge(qk_turned, 2 * s + 1)
                    at_least(act, q_decayed, 2 * s)
                    nc.scalar.activation(turned[:, 0], qk_banks[0][:].rearrange("p h n -> p (h n)"),
                                         ACT.Copy).then_inc(turned_out, 1)
                    act.wait_ge(f.projected, 4 * s + 4)
                    at_least(act, gate_stored, 16 * s)
                    nc.scalar.activation(gate, proj[3][:], ACT.Silu).then_inc(gate_made, 1)
                    act.wait_ge(qk_turned, 2 * s + 2)
                    nc.scalar.activation(turned[:, 1], qk_banks[1][:].rearrange("p h n -> p (h n)"),
                                         ACT.Copy).then_inc(turned_out, 1)

            over_pairs(act, body)
            late(TILES - 1)

        @block.vector
        def _(dve):
            w.make_lo(dve, 2)
            w.make_lo(dve, 3)
            dve.wait_ge(lg_made, 1)
            nc.vector.tensor_scalar(lg[:], lg[:], -1.0, None, ALU.mult).then_inc(expo_made, 1)
            dve.wait_ge(pos_made, 5)
            dve.wait_ge(expo_made, 1)
            for h in range(RH):
                nc.vector.tensor_scalar(weighted[:, h * C:(h + 1) * C], within[:, h, :], 0.0, lg[:, h:h + 1],
                                        ALU.max, ALU.mult)
                last = nc.vector.tensor_scalar(part[:, h * C:(h + 1) * C], within[:, h, :], 0.0,
                                               lg[:, RH + h:RH + h + 1], ALU.min, ALU.mult)
            last.then_inc(expo_made, 1)
            dve.wait_ge(expo_made, 2)
            nc.vector.tensor_tensor(within[:].rearrange("p h n -> p (h n)"), weighted[:], part[:],
                                    ALU.subtract).then_inc(expo_made, 1)
            for a in range(2):
                for h in range(RH):
                    nc.vector.tensor_scalar(q_scale[:, a, h, :], q_scale[:, a, h, :], lg[:, a * RH + h:a * RH + h + 1],
                                            None, ALU.mult).then_inc(expo_made, 1)
                last = nc.vector.tensor_scalar(k_scale[:, a * RH:(a + 1) * RH], lg[:, a * RH:(a + 1) * RH],
                                               pos[:, a:a + 1], None, ALU.mult)
            last.then_inc(expo_made, 1)
            nc.vector.memset(state[:, 1], 0.0).then_inc(state_made, 1)

            dve.wait_ge(const_made, 4)

            def late(s, par):
                dve.wait_ge(scored, s + 1)
                at_least(dve, part_done, s)
                nc.vector.tensor_tensor(weighted[:], so_bank[:], within[:].rearrange("p h n -> p (h n)"),
                                        ALU.mult).then_inc(weighted_made, 1)
                dve.wait_ge(state_made, s + 1)
                at_least(dve, part_done, s)
                if isinstance(s, int) and s == T_PROMPT // P - 1:
                    nc.vector.memset(state[:, par, 0:HALF // 2], 0.0).then_inc(state_decayed, 1)
                    dve.wait_ge(state_decayed, s + 1)
                    dve.wait_ge(kv_b_done, s + 1)
                    nc.vector.memset(state[:, par, HALF // 2:], 0.0).then_inc(state_made, 1)
                    return
                for h in range(RH):
                    last = nc.vector.tensor_scalar(state[:, par, h * RHD:(h + 1) * RHD],
                                                   state[:, 1 - par, h * RHD:(h + 1) * RHD],
                                                   chunk_decay[:, RH + h:RH + h + 1], None, ALU.mult)
                last.then_inc(state_decayed, 1)
                dve.wait_ge(state_decayed, s + 1)
                dve.wait_ge(kv_b_done, s + 1)
                nc.vector.tensor_tensor(state[:, par], state[:, par], kv_bank[:], ALU.add).then_inc(state_made, 1)

            def rotate(s, par, a, i):
                n = 2 * s + a
                dve.wait_ge(raw_made, n + 1)
                dve.wait_ge(cs_in[par], 16 * (i + 1))
                at_least(dve, qk_turned, n - 1)
                src = raw[:, a].rearrange("p (h x n) -> p x h n", h=RH, x=2)
                dst = rot[:, a].rearrange("p (h x n) -> p x h n", h=RH, x=2)
                prod = [product[:, j].rearrange("p (h n) -> p h n", h=RH) for j in range(2)]
                trig = [cs[:, par, j:j + 1, :].to_broadcast([P, RH, 64]) for j in range(2)]
                for x, (first, second, op) in enumerate([(0, 1, ALU.subtract), (1, 0, ALU.add)]):
                    at_least(dve, rotated, 2 * n + x)
                    nc.vector.tensor_tensor(prod[0], src[:, 0], trig[first], ALU.mult)
                    nc.vector.tensor_tensor(prod[1], src[:, 1], trig[second], ALU.mult).then_inc(multiplied, 1)
                    dve.wait_ge(multiplied, 2 * n + x + 1)
                    nc.vector.tensor_tensor(dst[:, x], prod[0], prod[1], op).then_inc(rotated, 1)

            def body(i, last):
                for par in range(2):
                    s = 2 * i + par
                    if not (isinstance(i, int) and s == 0):
                        late(s - 1, 1 - par)
                    rotate(s, par, 0, i)
                    rotate(s, par, 1, i)
                    dve.wait_ge(rotated, 4 * s + 4)
                    for a, done in enumerate((kv_f_done, kv_b_done)):
                        at_least(dve, done, s)
                        k = nc.vector.tensor_tensor(heads(k_dec[:, a]), heads(rot[:, 1]),
                                                    k_scale[:, a * RH:(a + 1) * RH].unsqueeze(2)
                                                    .to_broadcast([P, RH, RHD]), ALU.mult)
                    k.then_inc(k_decayed, 1)
                    dve.wait_ge(turned_out, 2 * s + 1)
                    at_least(dve, qf_stored, 16 * s)
                    at_least(dve, part_done, s)
                    for a in range(2):
                        nc.vector.tensor_tensor(q_dec[:, a], turned[:, 0], q_scale[:, a].rearrange("p h n -> p (h n)"),
                                                ALU.mult).then_inc(q_decayed, 1)

            seam = T_PROMPT // P
            body(0, False)
            with dve.Fori(1, seam // 2) as i:
                body(i, False)
            body(seam // 2, False)
            with dve.Fori(seam // 2 + 1, PAIRS - 1) as i:
                body(i, False)
            body(PAIRS - 1, True)
            late(TILES - 1, 1)

        @block.tensor
        def _(pe):

            def turn_heads(s, a):
                pe.wait_ge(rotated, 4 * s + 2 * a + 2)
                at_least(pe, turned_out, 2 * s + a - 1)
                for h in range(RH):
                    last = nc.tensor.transpose(qk_banks[a][:, h, :], rot[:, a, h * RHD:(h + 1) * RHD], ident[:])
                last.then_inc(qk_turned, 1)

            def scores(s):
                pe.wait_ge(turned_out, 2 * s + 2)
                at_least(pe, part_made, s)
                for h in range(RH):
                    cols = slice(h * C, (h + 1) * C)
                    last = nc.tensor.matmul(so_bank[:, cols], turned[:, 1, cols], turned[:, 0, cols],
                                            start=True, stop=True)
                last.then_inc(scored, 1)

            def key_values(s, a, done):
                pe.wait_ge(k_decayed, s + 1)
                if a == 1:
                    pe.wait_ge(v_made, s + 1)
                    at_least(pe, kv_out_made, s)
                else:
                    pe.wait_ge(state_made, s + 2)
                for h in range(RH):
                    cols = slice(h * RHD, (h + 1) * RHD)
                    last = nc.tensor.matmul(kv_bank[:, cols], k_dec[:, a, cols], v[:, cols], start=True, stop=True)
                last.then_inc(done, 1)

            def outputs(s, par):
                pe.wait_ge(weighted_made, s + 1)
                pe.wait_ge(q_decayed, 2 * s + 2)
                pe.wait_ge(state_made, s + 1)
                for h in range(RH):
                    cols = slice(h * C, (h + 1) * C)
                    nc.tensor.matmul(so_bank[:, cols], weighted[:, cols], v[:, cols], start=True, stop=False)
                    last = nc.tensor.matmul(so_bank[:, cols], q_dec[:, 1, cols], state[:, 1 - par, cols],
                                            start=False, stop=True)
                last.then_inc(part_done, 1)

            def body(i, last):
                for par in range(2):
                    s = 2 * i + par
                    late = not (isinstance(i, int) and s == 0)

                    def project(n, out, count):
                        if not late and n < 2:
                            return
                        if not late:
                            pe.wait_ge(w.lo_made, n + 1)
                        at_least(pe, out, count)
                        f.project(1 - par, n)

                    at_least(pe, h_in[par], 32 * (i + par))
                    project(0, raw_made, 2 * s - 1)
                    if late:
                        scores(s - 1)
                        key_values(s - 1, 1, kv_b_done)
                    project(1, raw_made, 2 * s)
                    if late:
                        key_values(s - 1, 0, kv_f_done)
                        outputs(s - 1, 1 - par)
                    project(2, v_made, s)
                    if late:
                        turn_heads(s, 0)
                    project(3, gate_made, s)
                    if not late:
                        turn_heads(s, 0)
                    turn_heads(s, 1)

            over_pairs(pe, body)
            s = TILES - 1
            scores(s)
            key_values(s, 1, kv_b_done)
            key_values(s, 0, kv_f_done)
            outputs(s, 1)


def attention_stage(nc, qT_d, kT_d, vg_d, bias_rows, ident, masked_d, w_out, na_d):
    with ExitStack() as ctx:
        sb = lambda n, s, d=F32: ctx.enter_context(nc.sbuf_tensor(n, s, d))
        sem = lambda n: ctx.enter_context(nc.semaphore(n))
        tables = sb("bias_tables", [P, 2, 3, GH, KEYS])
        k_strip = sb("k_strip", [P, 2, GH, KR * W], F32R)
        q_strip = sb("q_strip", [P, 2, GH, QR * W])
        q_block = sb("q_block", [P, 2, 2, GH, P], F32R)
        v_strip = sb("v_strip", [P, 2, W // 8, GW])
        out = sb("na_out", [P, 2, COLS, GW])
        biased = sb("biased", [P, 4, KEYS])
        probs = sb("probs", [P, 4, KEYS])
        probs_T = sb("probs_T", [P, 2, 4, P])
        neg_max = sb("neg_max", [P, 4])
        sums = sb("sums", [P, 4, GH])
        inverse = sb("inverse", [P, 2, GH])
        s_banks = [ctx.enter_context(nc.psum_tensor(f"s_bank{j}", [P, 512], F32)) for j in range(4)]
        t_banks = [ctx.enter_context(nc.psum_tensor(f"t_bank{j}", [P, 4, P], F32)) for j in range(2)]
        o_banks = [ctx.enter_context(nc.psum_tensor(f"o_bank{j}", [P, 512], F32)) for j in range(2)]
        wait_apart = apart(sem("n_passed"))
        cleared, masked_placed = [sem("cleared0"), sem("cleared1")], sem("masked_placed")
        tables_in, first_in = [sem(f"tables_in{n}") for n in range(6)], sem("first_in")
        q_in, k_in, v_in = ([sem(f"{n}_in{half}") for half in range(2)] for n in ("q", "k", "v"))
        q_placed, scored, biased_made, exped = sem("q_placed"), sem("na_scored"), sem("biased_made"), sem("exped")
        probs_turned, turned_act, turned_dve = sem("probs_turned"), sem("turned_act"), sem("turned_dve")
        valued, inverted, scaled = sem("valued"), sem("inverted"), sem("scaled")
        out_stored = [sem("out_stored0"), sem("out_stored1")]
        block = ctx.enter_context(nc.Block())

        G_BODIES = len(STRIPS) // 2
        BODIES = NH // GH * G_BODIES
        UNITS = 2 * COLS
        STEPS = UNITS * GH
        HALF_STEPS = STEPS // 2
        GROUP_KEYS = KR * 8
        FILLS = [(g, edge) for g in range(NH // GH) for edge in ("top", "inner", "bottom")]

        @block.sync
        def _(sp):
            def rows_of(b, half):
                g = b // G_BODIES if isinstance(b, int) else b_group
                strip = 2 * (b - g * G_BODIES) + half
                if isinstance(b, int) and b % G_BODIES in (0, G_BODIES - 1):
                    return g, *STRIPS[strip]
                q0, k0 = STRIPS[2]
                return g, q0 + QR * (strip - 2), k0 + QR * (strip - 2)

            def load_qk(b, half):
                g, q0, k0 = rows_of(b, half)
                heads = slice(g * GH, (g + 1) * GH)
                wait_apart(sp, scored, STEPS * b + HALF_STEPS * (half - 1))
                for rows in (slice(0, NHD), slice(NHD, P)):
                    sp.dma_start(q_strip[rows, half],
                                 qT_d[:, heads, bass.ds(q0 * W, QR * W)]).then_inc(q_in[half], 16)
                sp.dma_start(k_strip[:, half].bitcast(F32),
                             kT_d[:, heads, bass.ds(k0 * W, KR * W)]).then_inc(k_in[half], 16)

            def load_v(b, half):
                g, q0, k0 = rows_of(b, half)
                wait_apart(sp, valued, STEPS * b + HALF_STEPS * (half - 1))
                for r in range(KR):
                    sp.dma_start(v_strip[r * 8:(r + 1) * 8, half],
                                 vg_rows[k0 + r, :, g * GW:(g + 1) * GW].rearrange("(c w) n -> w c n", w=8)
                                 ).then_inc(v_in[half], 16)

            def store_pass(b, half):
                g, q0, _ = rows_of(b, half)
                wait_apart(sp, scaled, UNITS * b + COLS * (half + 1))
                for r in range(QR):
                    sp.dma_start(na_rows[q0 + r, :, g * GW:(g + 1) * GW].rearrange("(c w) n -> w c n", w=QC),
                                 out[r * QC:(r + 1) * QC, half]).then_inc(out_stored[half], 16)

            def fill(n, kinds=range(3)):
                g, edge = FILLS[n]
                landed = first_in if n == 0 and kinds[0] == 0 else tables_in[n]
                for r in range(QR):
                    if edge == "top":
                        key0, dr0 = max(r - 4, 0), max(r - 4, 0) - r + WIN_H - 1
                    elif edge == "inner":
                        key0, dr0 = r, 3
                    else:
                        key0, dr0 = min(r - 4, 0) + KR - QR, min(r - 4, 0) - r + WIN_H - 1
                    for k in kinds:
                        rows = bias_rows[:, k].rearrange("c (h r) x -> c h (r x)", h=NH)
                        sp.dma_start(tables[r * QC:(r + 1) * QC, n % 2, k, :, key0 * KC:(key0 + WIN_H) * KC],
                                     rows[:, g * GH:(g + 1) * GH, dr0 * KC:(dr0 + WIN_H) * KC]
                                     ).then_inc(landed, 16)

            def refill(n, b):
                wait_apart(sp, biased_made, STEPS * (b + 1))
                sp.dma_start(tables[:, n % 2], masked_d).then_inc(masked_placed, 16)
                wait_apart(sp, masked_placed, 16 * n)
                fill(n)

            def body(b):
                for half in range(2):
                    load_qk(b, half)
                    load_v(b, half)
                    store_pass(b - 1, half)

            vg_rows = vg_d.rearrange("t (r w) n -> (t r) w n", w=W)
            na_rows = na_d.rearrange("t (r w) n -> (t r) w n", w=W)
            load_qk(0, 0)
            load_v(0, 0)
            wait_apart(sp, cleared[0], 1)
            fill(0, [0])
            wait_apart(sp, cleared[0], 3)
            fill(0, [1, 2])
            load_qk(0, 1)
            load_v(0, 1)
            wait_apart(sp, cleared[1], 1)
            sp.dma_start(masked_d, tables[:, 1]).then_inc(masked_placed, 16)
            wait_apart(sp, masked_placed, 16)
            fill(1)
            for g in range(NH // GH):
                b0, b_group = g * G_BODIES, g
                if g > 0:
                    body(b0)
                    refill(3 * g + 1, b0 - 1)
                body(b0 + 1)
                refill(3 * g + 2, b0)
                with sp.Fori(b0 + 2, b0 + G_BODIES - 1) as b:
                    body(b)
                body(b0 + G_BODIES - 1)
                if g == 0:
                    refill(3, b0 + G_BODIES - 2)
            for half in range(2):
                store_pass(BODIES - 1, half)
            for half in range(2):
                wait_apart(sp, out_stored[half], 16 * QR * BODIES)

        @block.gpsimd
        def _(pool):
            def place_q(b, u):
                half, n = u // COLS, u % COLS
                if n == 0:
                    wait_apart(pool, q_in[half], 32 * (b + 1))
                wait_apart(pool, scored, STEPS * b + GH * (u - 1))
                src = q_strip[:, half].rearrange("p h (r w) -> p h r w", r=QR)[:, :, :, QC * n:QC * (n + 1)]
                hi, lo = (q_block[:, u % 2, j].rearrange("p h (r w) -> p h r w", r=QR) for j in range(2))
                nc.gpsimd.tensor_copy(hi, src).then_inc(q_placed, 1)
                wait_apart(pool, q_placed, 2 * (UNITS * b + u) + 1)
                nc.gpsimd.tensor_tensor(lo, src, hi.bitcast(F32), ALU.subtract).then_inc(q_placed, 1)

            def body(b):
                for u in range(UNITS):
                    place_q(b, u)

            place_q(0, 0)
            place_q(0, 1)
            nc.gpsimd.memset(tables[:, 1], MASKED).then_inc(cleared[1], 1)
            for u in range(2, UNITS):
                place_q(0, u)
            with pool.Fori(1, BODIES - 4) as b:
                body(b)
            for k in range(KB // 2):
                w_out.load(pool, k)
            body(BODIES - 4)
            for k in range(KB // 2, KB):
                w_out.load(pool, k)
            with pool.Fori(BODIES - 3, BODIES) as b:
                body(b)

        @block.scalar
        def _(act):
            def exponentiate(b, j):
                act.wait_ge(biased_made, STEPS * b + j + 1)
                at_least(act, probs_turned, STEPS * b + j - 3)
                if j % GH == 0:
                    at_least(act, inverted, UNITS * b + j // GH - 3)
                nc.scalar.activation(probs[:, j % 4].rearrange("p (c r w) -> p c r w", r=KR, w=8),
                                     biased[:, j % 4].rearrange("p (r c w) -> p c r w", r=KR, w=8), ACT.Exp, scale=-1.0,
                                     bias=neg_max[:, j % 4:j % 4 + 1],
                                     accum_out=sums[:, j // GH % 4, j % GH:j % GH + 1]).then_inc(exped, 1)

            def take_out(b, j):
                act.wait_ge(probs_turned, STEPS * b + j + 1)
                at_least(act, valued, STEPS * b + j - 1)
                nc.scalar.activation(probs_T[0:GROUP_KEYS, 0].rearrange("p c q -> p (c q)"),
                                     t_banks[0][0:GROUP_KEYS].rearrange("p c q -> p (c q)"),
                                     ACT.Copy).then_inc(turned_act, 1)

            def body(b, first=False, last=False):
                for k in range(STEPS):
                    if k % 2 == 0 and not (first and k < 2):
                        take_out(b, k - 2)
                    exponentiate(b, k)
                    if last and k % (STEPS // KB) == 1:
                        w_out.make_hi(act, k // (STEPS // KB))

            body(0, first=True)
            with act.Fori(1, BODIES - 1) as b:
                body(b)
            body(BODIES - 1, last=True)
            take_out(BODIES, -2)

        @block.vector
        def _(dve):
            def add_bias(b, slot, j):
                at_least(dve, exped, STEPS * b + j - 3)
                wait_apart(dve, scored, STEPS * b + j + 1)
                nc.vector.tensor_tensor_reduce(out=biased[:, j % 4, :], in0=s_banks[j % 4][:, 0:KEYS],
                                               in1=tables[:, slot, KIND[j // GH % COLS], j % GH, :], scale=1.0,
                                               scalar=3.0e38, op0=ALU.add, op1=ALU.min,
                                               accum_out=neg_max[:, j % 4:j % 4 + 1]).then_inc(biased_made, 1)

            def take_out(b, j):
                dve.wait_ge(probs_turned, STEPS * b + j + 1)
                at_least(dve, valued, STEPS * b + j - 1)
                nc.vector.tensor_copy(probs_T[0:GROUP_KEYS, 1], t_banks[1][0:GROUP_KEYS]).then_inc(turned_dve, 1)

            def scale_unit(b, u):
                n = UNITS * b + u + 1
                dve.wait_ge(valued, GH * n)
                nc.vector.reciprocal(inverse[:, u % 2, :], sums[:, u % 4, :]).then_inc(inverted, 1)
                dve.wait_ge(inverted, n)
                if u % COLS == 0:
                    at_least(dve, out_stored[u // COLS], 16 * QR * b)
                nc.vector.tensor_tensor(out[:, u // COLS % 2, u % COLS].rearrange("p (h d) -> p h d", h=GH),
                                        o_banks[u % 2][:, 0:GW].rearrange("p (h d) -> p h d", h=GH),
                                        inverse[:, u % 2, :].unsqueeze(2).to_broadcast([P, GH, NHD]),
                                        ALU.mult).then_inc(scaled, 1)

            def body(b, slot, first=False, last=False):
                for k in range(STEPS):
                    if first and k == GH:
                        dve.wait_ge(tables_in[0], 32 * QR)
                    if k % 2 == 1 and not (first and k < 2):
                        take_out(b, k - 2)
                    add_bias(b, slot, k)
                    if k % GH == 0 and not (first and k < 2 * GH):
                        scale_unit(b, k // GH - 2)
                    if last and k % (STEPS // KB) == 2:
                        w_out.make_lo(dve, k // (STEPS // KB))

            for k in range(3):
                nc.vector.memset(tables[:, 0, k], MASKED).then_inc(cleared[0], 1)
            for g in range(NH // GH):
                b0, n0 = g * G_BODIES, 3 * g
                if g == 0:
                    dve.wait_ge(first_in, 16 * QR)
                else:
                    dve.wait_ge(tables_in[n0], 48 * QR)
                body(b0, n0 % 2, g == 0)
                dve.wait_ge(tables_in[n0 + 1], 48 * QR)
                with dve.Fori(b0 + 1, b0 + G_BODIES - 1) as b:
                    body(b, (n0 + 1) % 2)
                dve.wait_ge(tables_in[n0 + 2], 48 * QR)
                body(b0 + G_BODIES - 1, n0 % 2, last=g > 0)
            take_out(BODIES, -1)
            scale_unit(BODIES, -2)
            scale_unit(BODIES, -1)

        @block.tensor
        def _(pe):
            def score(b, j):
                u, h = j // GH, j % GH
                if h == 0:
                    pe.wait_ge(q_placed, 2 * (UNITS * b + u + 1))
                    if u % COLS == 0:
                        pe.wait_ge(k_in[u // COLS], 16 * (b + 1))
                at_least(pe, biased_made, STEPS * b + j - 3)
                keys = k_strip[:, u // COLS, h, :].rearrange("p (r w) -> p r w", w=W)
                k0 = K0[u % COLS]
                for part in range(2):
                    last = nc.tensor.matmul(s_banks[j % 4][:, 0:KEYS], q_block[:, u % 2, part, h, :],
                                            keys[:, :, k0:k0 + KC], start=(part == 0), stop=(part == 1))
                last.then_inc(scored, 1)

            def turn(b, j):
                pe.wait_ge(exped, STEPS * b + j + 1)
                at_least(pe, turned_act if j % 2 == 0 else turned_dve, STEPS // 2 * b + j // 2)
                for c in range(4):
                    last = nc.tensor.transpose(t_banks[j % 2][0:GROUP_KEYS, c, :],
                                               probs[:, j % 4, c * GROUP_KEYS:(c + 1) * GROUP_KEYS], ident[:])
                last.then_inc(probs_turned, 1)

            def value(b, j):
                u, h = j // GH, j % GH
                pe.wait_ge(turned_act if j % 2 == 0 else turned_dve, STEPS // 2 * b + j // 2 + 1)
                if h == 0:
                    if u % COLS == 0:
                        pe.wait_ge(v_in[u // COLS], 16 * KR * (b + 1))
                    at_least(pe, scaled, UNITS * b + u - 1)
                cols = slice(h * NHD, (h + 1) * NHD)
                for c in range(4):
                    last = nc.tensor.matmul(o_banks[u % 2][:, cols], probs_T[0:GROUP_KEYS, j % 2, c, :],
                                            v_strip[0:GROUP_KEYS, u // COLS, K0[u % COLS] // 8 + c, cols],
                                            start=(c == 0), stop=(c == 3))
                last.then_inc(valued, 1)

            pe.wait_ge(first_in, 16 * QR)
            for j in range(4):
                score(0, j)
            turn(0, 0)

            def body(b, last):
                for k in range(STEPS):
                    if k + 4 < STEPS:
                        score(b, k + 4)
                    elif not last:
                        score(b + 1, k + 4 - STEPS)
                    if k + 1 < STEPS:
                        turn(b, k + 1)
                    elif not last:
                        turn(b + 1, 0)
                    value(b, k)

            body(0, False)
            with pe.Fori(1, BODIES - 1) as b:
                body(b, False)
            body(BODIES - 1, True)


def out_stage(nc, x_tiles, w_out, ret_gain, gate_rows, decays, na_d, vg_d, part_d, qf_d, kv_d, gate_d, ident, exps,
              y_tiles):
    with ExitStack() as ctx:
        sb = lambda n, s, d=F32: ctx.enter_context(nc.sbuf_tensor(f"o_{n}", s, d))
        sem = lambda n: ctx.enter_context(nc.semaphore(f"o_{n}"))
        lg = sb("lg", [P, 2 * RH])
        chunk_decay = sb("chunk_decay", [P, RH])
        gain = sb("gain", [P, HALF])
        out_gate = sb("out_gate", [P, 2, D])
        x = sb("x", [P, 2, D])
        part, qf, kv, gate, na_gate = (sb(n, [P, 2, HALF]) for n in ("part", "qf", "kv", "gate", "na_gate"))
        mix = sb("mix", [P, 2, D])
        state = sb("state_f", [P, 2, HALF])
        total = sb("total", [P, HALF])
        squares = sb("squares", [P, HALF])
        stat = sb("stat", [P, 3, RH])
        m_hi, m_lo = sb("m_hi", [P, 2, KB, P], F32R), sb("m_lo", [P, 2, KB, P], F32R)
        y = sb("y", [P, 2, D])
        cross_bank = ctx.enter_context(nc.psum_tensor("o_cross", [P, 512], F32))
        turn_banks = [ctx.enter_context(nc.psum_tensor(f"o_turn{j}", [P, 4, P], F32)) for j in range(2)]
        banks = [ctx.enter_context(nc.psum_tensor(f"o_proj{j}", [P, 512], F32)) for j in range(4)]
        wait_apart = apart(sem("passed"))
        lg_in, gain_in, gate_in = sem("lg_in"), sem("gain_in"), sem("gate_in")
        lg_made, decay_made = sem("lg_made"), sem("decay_made")
        scan_in, tile_in, x_in = ([sem(f"{n}_in{par}") for par in range(2)] for n in ("scan", "tile", "x"))
        state_made, crossed = sem("state_made"), sem("crossed")
        totalled, squared, summed = sem("totalled"), sem("squared"), sem("summed")
        meaned, rstd_made = sem("meaned"), sem("rstd")
        gained, mixed, mix_turned = sem("gained"), sem("mixed"), sem("mix_turned")
        hi_made, lo_made, projected = sem("hi_made"), sem("lo_made"), sem("projected")
        scaled, added = sem("scaled"), sem("added")
        y_stored = [sem("y_stored0"), sem("y_stored1")]
        block = ctx.enter_context(nc.Block())

        @block.sync
        def _(sp):
            def load_tile(t, par):
                wait_apart(sp, mixed, t - 1)
                wait_apart(sp, mix_turned, t - 1)
                for dst, src in ((kv, kv_d), (qf, qf_d)):
                    sp.dma_start(dst[:, par], src[t]).then_inc(scan_in[par], 16)
                for dst, src in ((part, part_d), (gate, gate_d)):
                    sp.dma_start(dst[:, par], src[t]).then_inc(tile_in[par], 16)
                sp.dma_start(mix[:, par, 0:HALF], na_d[t]).then_inc(tile_in[par], 16)
                sp.dma_start(na_gate[:, par], vg_d[t][:, HALF:D]).then_inc(tile_in[par], 16)

            def load_x(t, par):
                wait_apart(sp, added, t - 1)
                sp.dma_start(x[:, par], x_tiles[t]).then_inc(x_in[par], 16)

            def store_y(t, par):
                wait_apart(sp, added, t + 1)
                sp.dma_start(y_tiles[t], y[:, par]).then_inc(y_stored[par], 16)

            sp.dma_start(lg[:], decays.partition_broadcast(P)).then_inc(lg_in, 16)
            load_tile(0, 0)
            sp.dma_start(gain[:], ret_gain.partition_broadcast(P)).then_inc(gain_in, 16)
            load_tile(1, 1)
            for s in range(2):
                sp.dma_start(out_gate[:, s], gate_rows[s].partition_broadcast(P)).then_inc(gate_in, 16)
            load_x(0, 0)
            load_x(1, 1)
            load_tile(2, 0)

            def body(i, tiles_left):
                for par in range(2):
                    t = 2 * i + par
                    if tiles_left > par + 3:
                        load_tile(t + 3, 1 - par)
                    store_y(t, par)
                    if tiles_left > par + 2:
                        load_x(t + 2, par)

            body(0, TILES)
            with sp.Fori(1, PAIRS - 2) as i:
                body(i, TILES)
            body(PAIRS - 2, 4)
            body(PAIRS - 1, 2)
            for par in range(2):
                wait_apart(sp, y_stored[par], 16 * PAIRS)

        @block.gpsimd
        def _(pool):
            def gate_and_rstd(t, par, i):
                wait_apart(pool, tile_in[par], 64 * (i + 1))
                nc.gpsimd.tensor_tensor(gate[:, par], gate[:, par], gain[:], ALU.mult)
                nc.gpsimd.tensor_tensor(mix[:, par, 0:HALF], mix[:, par, 0:HALF], na_gate[:, par],
                                        ALU.mult).then_inc(gained, 1)
                wait_apart(pool, meaned, t + 1)
                nc.gpsimd.tensor_tensor(stat[:, 2, :], stat[:, 1, :], exps[:, 0:RH], ALU.pow).then_inc(rstd_made, 1)

            wait_apart(pool, gain_in, 16)

            def body(i, last):
                for par in range(2):
                    gate_and_rstd(2 * i + par, par, i)

            over_pairs(pool, body)

        @block.scalar
        def _(act):
            act.wait_ge(lg_in, 16)
            nc.scalar.activation(lg[:], lg[:], ACT.Exp).then_inc(lg_made, 1)
            act.wait_ge(lg_made, 2)
            nc.scalar.activation(chunk_decay[:], lg[:, 0:RH], ACT.Exp, scale=float(C)).then_inc(decay_made, 1)
            def square(t):
                act.wait_ge(totalled, t + 1)
                at_least(act, summed, t)
                nc.scalar.activation(squares[:], total[:], ACT.Square).then_inc(squared, 1)

            def high(t, par):
                act.wait_ge(mix_turned, t + 1)
                at_least(act, projected, 2 * (t - 1))
                for j in range(2):
                    last = nc.scalar.activation(m_hi[:, par, 4 * j:4 * j + 4].rearrange("p k t -> p (k t)"),
                                                turn_banks[j][:].rearrange("p k t -> p (k t)"), ACT.Copy)
                last.then_inc(hi_made, 1)

            square(0)
            high(0, 0)
            square(1)

            def body(i, last):
                for par in range(2):
                    t = 2 * i + par
                    if not (last and par == 1):
                        high(t + 1, 1 - par)
                    if not last:
                        square(t + 2)

            over_pairs(act, body)

        @block.vector
        def _(dve):
            dve.wait_ge(lg_made, 1)
            nc.vector.tensor_scalar(lg[:], lg[:], -1.0, None, ALU.mult).then_inc(lg_made, 1)
            nc.vector.memset(state[:, 1], 0.0).then_inc(state_made, 1)

            def carry(t, par, i):
                dve.wait_ge(scan_in[par], 32 * (i + 1))
                dve.wait_ge(state_made, t + 1)
                at_least(dve, crossed, t)
                if isinstance(t, int) and t == T_SAMPLE // P - 1:
                    nc.vector.memset(state[:, par], 0.0).then_inc(state_made, 1)
                    return
                for h in range(RH):
                    cols = slice(h * RHD, (h + 1) * RHD)
                    last = nc.vector.scalar_tensor_tensor(out=state[:, par, cols], in0=state[:, 1 - par, cols],
                                                          scalar=chunk_decay[:, h:h + 1], in1=kv[:, par, cols],
                                                          op0=ALU.mult, op1=ALU.add)
                last.then_inc(state_made, 1)

            def total_up(t, par, i):
                dve.wait_ge(crossed, t + 1)
                dve.wait_ge(tile_in[par], 64 * (i + 1))
                at_least(dve, mixed, t)
                nc.vector.tensor_tensor(total[:], cross_bank[:], part[:, par], ALU.add).then_inc(totalled, 1)

            def norm(t, par):
                dve.wait_ge(squared, t + 1)
                nc.vector.tensor_reduce(stat[:, 0, :], squares[:].rearrange("p (h d) -> p h d", h=RH), AX.X,
                                        ALU.add).then_inc(summed, 1)
                dve.wait_ge(summed, t + 1)
                nc.vector.tensor_scalar(stat[:, 1, :], stat[:, 0, :], 1.0 / RHD, EPS, ALU.mult,
                                        ALU.add).then_inc(meaned, 1)

            def mix_up(t, par):
                dve.wait_ge(rstd_made, t + 1)
                at_least(dve, mix_turned, t - 1)
                dve.wait_ge(gained, t + 1)
                for h in range(RH):
                    cols = slice(h * RHD, (h + 1) * RHD)
                    last = nc.vector.scalar_tensor_tensor(out=mix[:, par, HALF + h * RHD:HALF + (h + 1) * RHD],
                                                          in0=total[:, cols], scalar=stat[:, 2, h:h + 1],
                                                          in1=gate[:, par, cols], op0=ALU.mult, op1=ALU.mult)
                last.then_inc(mixed, 1)

            def low(t, par):
                dve.wait_ge(hi_made, t + 1)
                for j in range(2):
                    hi = m_hi[:, par, 4 * j:4 * j + 4].bitcast(F32)
                    last = nc.vector.tensor_tensor(m_lo[:, par, 4 * j:4 * j + 4], turn_banks[j][:], hi, ALU.subtract)
                last.then_inc(lo_made, 1)

            def scale(t, par, n, seq, i):
                dve.wait_ge(projected, 2 * t + n + 1)
                if n == 0:
                    at_least(dve, y_stored[par], 16 * i)
                cols = slice(n * 512, (n + 1) * 512)
                nc.vector.tensor_tensor(y[:, par, cols], banks[2 * par + n][:], out_gate[:, seq, cols],
                                        ALU.mult).then_inc(scaled, 1)

            def add_x(t, par, i):
                dve.wait_ge(x_in[par], 16 * (i + 1))
                dve.wait_ge(scaled, 2 * t + 2)
                nc.vector.tensor_tensor(y[:, par], y[:, par], x[:, par], ALU.add).then_inc(added, 1)

            dve.wait_ge(decay_made, 1)
            carry(0, 0, 0)
            total_up(0, 0, 0)
            carry(1, 1, 0)
            norm(0, 0)
            mix_up(0, 0)
            total_up(1, 1, 0)
            low(0, 0)
            norm(1, 1)
            mix_up(1, 1)
            dve.wait_ge(gate_in, 32)

            def body(i, last, seq):
                for par in range(2):
                    t = 2 * i + par
                    if not last:
                        carry(t + 2, par, i + 1)
                    scale(t, par, 0, seq, i)
                    if not last:
                        total_up(t + 2, par, i + 1)
                    if not (last and par == 1):
                        low(t + 1, 1 - par)
                    if not last:
                        norm(t + 2, par)
                        mix_up(t + 2, par)
                    scale(t, par, 1, seq, i)
                    add_x(t, par, i)

            seam = T_SAMPLE // P // 2
            body(0, False, 0)
            with dve.Fori(1, seam - 2) as i:
                body(i, False, 0)
            body(seam - 2, False, 0)
            body(seam - 1, False, 0)
            with dve.Fori(seam, PAIRS - 1) as i:
                body(i, False, 1)
            body(PAIRS - 1, True, 1)

        @block.tensor
        def _(pe):
            def cross(t, par, i):
                pe.wait_ge(state_made, t + 1)
                pe.wait_ge(scan_in[par], 32 * (i + 1))
                at_least(pe, totalled, t)
                for h in range(RH):
                    cols = slice(h * C, (h + 1) * C)
                    last = nc.tensor.matmul(cross_bank[:, cols], qf[:, par, cols], state[:, 1 - par, cols],
                                            start=True, stop=True)
                last.then_inc(crossed, 1)

            def turn(t, par):
                pe.wait_ge(mixed, t + 1)
                at_least(pe, lo_made, t)
                for k in range(KB):
                    last = nc.tensor.transpose(turn_banks[k // 4][:, k % 4, :], mix[:, par, k * P:(k + 1) * P],
                                               ident[:])
                last.then_inc(mix_turned, 1)

            def project(t, par, n):
                pe.wait_ge(lo_made, t + 1)
                at_least(pe, scaled, 2 * (t - 2) + n + 1)
                for k in range(KB):
                    for j, (m, w) in enumerate([(m_hi, w_out.hi), (m_hi, w_out.lo), (m_lo, w_out.hi)]):
                        last = nc.tensor.matmul(banks[2 * par + n][:], m[:, par, k, :], w[:, k, n * 512:(n + 1) * 512],
                                                start=(k == 0 and j == 0), stop=(k == KB - 1 and j == 2))
                last.then_inc(projected, 1)

            cross(0, 0, 0)
            cross(1, 1, 0)
            turn(0, 0)

            def body(i, last):
                for par in range(2):
                    t = 2 * i + par
                    project(t, par, 0)
                    if not (last and par == 1):
                        turn(t + 1, 1 - par)
                    if not last:
                        cross(t + 2, par, i + 1)
                    project(t, par, 1)

            over_pairs(pe, body)


def build(nc, a, y):
    dram = lambda n, s: nc.dram_tensor(n, s, F32, kind="Internal").ap()
    with ExitStack() as ctx:
        sb = lambda n, s: ctx.enter_context(nc.sbuf_tensor(n, s, F32))
        ident = sb("ident", [P, P])
        exps = sb("minus_half", [P, NH])
        gate_rows = dram("gate_rows", (2, D))
        bias_rows = dram("bias_rows", (QC, 3, NH * NDR, KC))
        qT_d = dram("qT_d", (NHD, NH, T))
        kT_d = dram("kT_d", (P, NH, T))
        vg_d = dram("vg_d", (TILES, P, D))
        na_d = dram("na_d", (TILES, P, HALF))
        h_d = dram("h_d", (TILES, 2, P, D))
        masked_d = dram("masked_d", (P, 3, GH, KEYS))
        part_d, qf_d, kv_d, rg_d = (dram(n, (TILES, P, HALF)) for n in ("part_d", "qf_d", "kv_d", "rg_d"))
        x_tiles, y_tiles = a["x"], y
        with ExitStack() as w_ctx, ExitStack() as in_ctx:
            modx = w_ctx.enter_context(nc.sbuf_tensor("modx", [P, TILES, 16], F32))
            w_att = Weights(nc, w_ctx, "w_att", a["w_in"][:, 0:4 * HALF], 4 * HALF)
            w_ret = NextWeights(nc, w_ctx, "w_ret", w_att, a["w_in"][:, 4 * HALF:8 * HALF])
            modulation_stage(nc, a["cT"], a["w_ada"], a["b_ada"], a["norm_gain"], a["rpb"], ident, modx, exps,
                             gate_rows, bias_rows, w_att)
            attention_product = Projection(nc, in_ctx, "a", w_att)
            retention_product = Projection(nc, in_ctx, "r", w_ret, attention_product)
            attention_in_stage(nc, x_tiles, a["xT"], attention_product, retention_product, a["qk_gain"], modx, ident,
                               exps, h_d, qT_d, kT_d, vg_d)
            retention_in_stage(nc, retention_product, h_d, a["decays"], a["rope"], ident, part_d, qf_d, kv_d, rg_d)
        w_out = Weights(nc, ctx, "w_out", a["w_out"], D)
        attention_stage(nc, qT_d, kT_d, vg_d, bias_rows, ident, masked_d, w_out, na_d)
        out_stage(nc, x_tiles, w_out, a["ret_gain"], gate_rows, a["decays"], na_d, vg_d, part_d, qf_d, kv_d, rg_d,
                  ident, exps, y_tiles)


def rope_table():
    half = RHD // 2
    inv = np.float32(10000.0) ** (-np.arange(half, dtype=np.float32) / np.float32(half))
    pos = np.concatenate([np.arange(T_SAMPLE), np.arange(T_PROMPT)]).astype(np.float32)
    angle = pos[:, None] * inv[None, :]
    return np.stack([np.cos(angle), np.sin(angle)], axis=1).astype(np.float32).reshape(TILES, P, 2, half)


def kernel(x_prompt, x_sample, c_prompt, c_sample, norm_gain, w_ada, b_ada, w_in, na_q_gain, na_k_gain, na_rpb,
           ret_decay_f, ret_decay_b, ret_out_gain, w_out):
    import concourse.bacc as bacc
    from concourse.bass_utils import run_bass_kernel_spmd

    c_both = np.concatenate([np.asarray(c_sample), np.asarray(c_prompt)])
    x = np.concatenate([np.asarray(x_sample)[0], np.asarray(x_prompt)[0]])
    arrays = {
        "x": x.reshape(TILES, P, D),
        "xT": x.reshape(TILES, P, KB, P).transpose(0, 3, 2, 1),
        "cT": c_both.T.reshape(KB, P, 2).transpose(1, 0, 2),
        "norm_gain": np.asarray(norm_gain)[0].reshape(KB, P).T,
        "w_ada": np.asarray(w_ada)[0],
        "b_ada": np.asarray(b_ada),
        "w_in": np.asarray(w_in)[0],
        "qk_gain": np.stack([np.tile(np.asarray(g)[0], 2) for g in (na_q_gain, na_k_gain)], axis=1),
        "rpb": np.asarray(na_rpb)[0].reshape(NH * NDR, NDC),
        "decays": np.concatenate([np.asarray(ret_decay_f)[0], np.asarray(ret_decay_b)[0]]),
        "ret_gain": np.asarray(ret_out_gain)[0].reshape(HALF),
        "w_out": np.asarray(w_out)[0],
        "rope": rope_table(),
    }
    nc = bacc.Bacc("TRN2", target_bir_lowering=False, num_devices=1)
    arrays = {f"in_{n}": np.ascontiguousarray(v) for n, v in arrays.items()}
    aps = {n[3:]: nc.dram_tensor(n, v.shape, mybir.dt.from_np(v.dtype), kind="ExternalInput").ap()
           for n, v in arrays.items()}
    y = nc.dram_tensor("y", (TILES, P, D), F32, kind="ExternalOutput").ap()
    build(nc, aps, y)
    got = run_bass_kernel_spmd(nc, [arrays], core_ids=[0]).results[0]["y"].reshape(T, D)
    return got[T_SAMPLE:].reshape(1, T_PROMPT, D), got[:T_SAMPLE].reshape(1, T_SAMPLE, D)
```
